# Optimizing a Trainium2 kernel written in Bass

```python
import jax, jax.numpy as jnp
from jax import lax
import numpy as np

D_MODEL = 1024
BATCH = 1
SEQ = 1024
DEPTH = 1

N_META = 16
CHUNK = 64
HG_HEADS = 4
HG_DK = 128
HG_DV = 128
GDN_HEADS = 4
GDN_DK = 128
GDN_DV = 128
CONV_W = 4
HG_WIDTH = HG_HEADS * HG_DK
GDN_WIDTH = GDN_HEADS * GDN_DV
D_MIX = HG_WIDTH + GDN_WIDTH
IN_COLS = 4 * HG_WIDTH + 4 * GDN_WIDTH + 2 * GDN_HEADS
EPS = 1e-6

kernel_name = "hymba_hgrn2_gated_deltanet_layer"

def rmsnorm(x, w):
    xf = x.astype(jnp.float32)
    y = xf * lax.rsqrt(jnp.mean(xf * xf, axis=-1, keepdims=True) + EPS)
    return (y * w.astype(jnp.float32)).astype(x.dtype)

def gated_rmsnorm(o, z, w):
    of = jnp.transpose(o, (0, 2, 1, 3)).astype(jnp.float32)
    y = of * lax.rsqrt(jnp.mean(of * of, axis=-1, keepdims=True) + EPS) * w.astype(jnp.float32)
    B, T = y.shape[0], y.shape[1]
    return (y.reshape(B, T, -1) * jax.nn.silu(z.astype(jnp.float32))).astype(z.dtype)

def heads(a, H):
    B, T, _ = a.shape
    return jnp.transpose(a.reshape(B, T, H, -1), (0, 2, 1, 3))

def causal_conv(x, w):
    C = x.shape[-1]
    return lax.conv_general_dilated(x, w[:, None, :].astype(x.dtype), window_strides=(1,),
                                    padding=((CONV_W - 1, 0),),
                                    dimension_numbers=('NWC', 'WIO', 'NWC'),
                                    feature_group_count=C)

def to_chunks(a, C):
    B, H, T = a.shape[:3]
    return jnp.moveaxis(a.reshape((B, H, T // C, C) + a.shape[3:]), 2, 0)

def from_chunks(o):
    nc, B, H, C, d = o.shape
    return jnp.moveaxis(o, 0, 2).reshape(B, H, nc * C, d)

def run_chunked(step, inputs, S0, C):
    xs = tuple(to_chunks(a, C) for a in inputs)
    S, o = lax.scan(step, S0, xs)
    return S, from_chunks(o)

def causal_mixer(step, inputs, S0):
    meta = tuple(a[:, :, :N_META] for a in inputs)
    real = tuple(a[:, :, N_META:] for a in inputs)
    S, o_meta = run_chunked(step, meta, S0, N_META)
    _, o_real = run_chunked(step, real, S, CHUNK)
    return jnp.concatenate([o_meta, o_real], axis=2)

def hgrn2_chunk(S, inp):
    q, k, v, logf = inp
    C = q.shape[2]
    G = jnp.cumsum(logf, axis=2)
    causal = jnp.tril(jnp.ones((C, C), dtype=bool))
    diff = G[:, :, :, None, :] - G[:, :, None, :, :]
    decay = jnp.exp(jnp.where(causal[None, None, :, :, None], diff, -jnp.inf))
    A = jnp.einsum('bhtd,bhtsd,bhsd->bhts', q, decay, k)
    o = jnp.einsum('bhts,bhsv->bhtv', A, v) + jnp.einsum('bhtd,bhdv->bhtv', q * jnp.exp(G), S)
    G_last = G[:, :, -1]
    S_new = jnp.exp(G_last)[..., None] * S + jnp.einsum(
        'bhsd,bhsv->bhdv', k * jnp.exp(G_last[:, :, None, :] - G), v)
    return S_new, o

def gdn_chunk(S, inp):
    q, k, v, g, beta = inp
    C = q.shape[2]
    dv = v.shape[-1]
    gam = jnp.cumsum(g, axis=-1)
    diff = gam[..., :, None] - gam[..., None, :]
    strict = jnp.tril(jnp.ones((C, C), dtype=bool), -1)
    incl = jnp.tril(jnp.ones((C, C), dtype=bool))
    dec_strict = jnp.exp(jnp.where(strict, diff, -jnp.inf))
    dec_incl = jnp.exp(jnp.where(incl, diff, -jnp.inf))
    A = beta[..., None] * jnp.einsum('bhtd,bhsd->bhts', k, k) * dec_strict
    lhs = jnp.eye(C, dtype=A.dtype) + A
    rhs = jnp.concatenate([beta[..., None] * v, (beta * jnp.exp(gam))[..., None] * k], axis=-1)
    sol = lax.linalg.triangular_solve(lhs, rhs, left_side=True, lower=True)
    U, W = sol[..., :dv], sol[..., dv:]
    u = U - jnp.einsum('bhtd,bhdv->bhtv', W, S)
    qk = jnp.einsum('bhtd,bhsd->bhts', q, k) * dec_incl
    o = jnp.einsum('bhtd,bhdv->bhtv', q * jnp.exp(gam)[..., None], S) + jnp.einsum('bhts,bhsv->bhtv', qk, u)
    g_last = gam[..., -1]
    S_new = jnp.exp(g_last)[..., None, None] * S + jnp.einsum(
        'bhsd,bhsv->bhdv', k * jnp.exp(g_last[..., None] - gam)[..., None], u)
    return S_new, o

def hybrid_layer(h, norm_w, w_in, conv_w, lower_bound, hg_norm_w, gdn_A_log, gdn_dt_bias, gdn_norm_w, w_out):
    B, T, _ = h.shape
    f32 = jnp.float32
    u = rmsnorm(h, norm_w)
    proj = jnp.einsum('btd,dc->btc', u, w_in)
    cuts = np.cumsum([HG_WIDTH, HG_WIDTH, HG_WIDTH, HG_WIDTH, 3 * GDN_WIDTH, GDN_WIDTH, GDN_HEADS])
    hg_q, hg_f, hg_i, hg_z, gd_qkv, gd_z, gd_a, gd_b = jnp.split(proj, [int(c) for c in cuts], axis=-1)

    q = heads(jax.nn.silu(hg_q.astype(f32)), HG_HEADS)
    lb = lower_bound.astype(f32)
    f = lb + (1.0 - lb) * jax.nn.sigmoid(hg_f.astype(f32))
    k = heads(1.0 - f, HG_HEADS)
    logf = heads(jnp.log(f), HG_HEADS)
    v = heads(hg_i.astype(f32), HG_HEADS)
    S0 = jnp.zeros((B, HG_HEADS, HG_DK, HG_DV), f32)
    o_hg = causal_mixer(hgrn2_chunk, (q, k, v, logf), S0)
    y_hg = gated_rmsnorm(o_hg, hg_z, hg_norm_w)

    qkv = jax.nn.silu(causal_conv(gd_qkv, conv_w).astype(f32))
    gq, gk, gv = jnp.split(qkv, 3, axis=-1)
    gq = heads(gq, GDN_HEADS)
    gk = heads(gk, GDN_HEADS)
    gv = heads(gv, GDN_HEADS)
    gq = gq * lax.rsqrt(jnp.sum(gq * gq, -1, keepdims=True) + EPS) * (GDN_DK ** -0.5)
    gk = gk * lax.rsqrt(jnp.sum(gk * gk, -1, keepdims=True) + EPS)
    g = -jnp.exp(gdn_A_log.astype(f32)) * jax.nn.softplus(gd_a.astype(f32) + gdn_dt_bias.astype(f32))
    g = jnp.transpose(g, (0, 2, 1))
    beta = jnp.transpose(jax.nn.sigmoid(gd_b.astype(f32)), (0, 2, 1))
    S0g = jnp.zeros((B, GDN_HEADS, GDN_DK, GDN_DV), f32)
    o_gd = causal_mixer(gdn_chunk, (gq, gk, gv, g, beta), S0g)
    y_gd = gated_rmsnorm(o_gd, gd_z, gdn_norm_w)

    y = jnp.concatenate([y_hg, y_gd], axis=-1)
    return jnp.einsum('btc,cd->btd', y, w_out).astype(h.dtype)

def setup_inputs(seed: int = 0) -> dict:
    key = jax.random.key(seed)
    ks = jax.random.split(key, 14)
    f32 = jnp.float32
    x = jax.random.normal(ks[0], (BATCH, SEQ, D_MODEL), f32)
    meta_tokens = jax.random.normal(ks[1], (N_META, D_MODEL), f32)
    norm_w = 1.0 + 0.02 * jax.random.normal(ks[2], (DEPTH, D_MODEL), f32)
    w_in = jax.random.normal(ks[3], (DEPTH, D_MODEL, IN_COLS), f32) * D_MODEL ** -0.5
    conv_w = jax.random.normal(ks[4], (DEPTH, CONV_W, 3 * GDN_WIDTH), f32) * CONV_W ** -0.5
    hg_lb_logits = 0.5 * jax.random.normal(ks[5], (DEPTH + 1, HG_WIDTH), f32)
    hg_norm_w = 1.0 + 0.02 * jax.random.normal(ks[6], (DEPTH, HG_DV), f32)
    gdn_A_log = jnp.log(jax.random.uniform(ks[7], (DEPTH, GDN_HEADS), f32, 1.0, 16.0))
    dt = jnp.exp(jax.random.uniform(ks[8], (DEPTH, GDN_HEADS), f32, jnp.log(0.001), jnp.log(0.1)))
    gdn_dt_bias = dt + jnp.log(-jnp.expm1(-dt))
    gdn_norm_w = 1.0 + 0.02 * jax.random.normal(ks[9], (DEPTH, GDN_DV), f32)
    w_out = jax.random.normal(ks[10], (DEPTH, D_MIX, D_MODEL), f32) * D_MIX ** -0.5
    final_norm_w = 1.0 + 0.02 * jax.random.normal(ks[11], (D_MODEL,), f32)
    return {"x": x, "meta_tokens": meta_tokens, "norm_w": norm_w, "w_in": w_in, "conv_w": conv_w,
            "hg_lb_logits": hg_lb_logits, "hg_norm_w": hg_norm_w, "gdn_A_log": gdn_A_log,
            "gdn_dt_bias": gdn_dt_bias, "gdn_norm_w": gdn_norm_w, "w_out": w_out,
            "final_norm_w": final_norm_w}

def reference(x, meta_tokens, norm_w, w_in, conv_w, hg_lb_logits, hg_norm_w, gdn_A_log,
              gdn_dt_bias, gdn_norm_w, w_out, final_norm_w):
    B = x.shape[0]
    meta = jnp.broadcast_to(meta_tokens[None].astype(x.dtype), (B, N_META, D_MODEL))
    h = jnp.concatenate([meta, x], axis=1)
    lower_bounds = jnp.cumsum(jax.nn.softmax(hg_lb_logits.astype(jnp.float32), axis=0), axis=0)
    for l in range(DEPTH):
        h = h + hybrid_layer(h, norm_w[l], w_in[l], conv_w[l], lower_bounds[l], hg_norm_w[l],
                             gdn_A_log[l], gdn_dt_bias[l], gdn_norm_w[l], w_out[l])
    y = rmsnorm(h, final_norm_w)
    return y[:, N_META:]


_drawn_inputs = setup_inputs


def setup_inputs(seed=0):
    import zlib

    import numpy as np

    out = dict(_drawn_inputs(seed))
    spreads = {}
    factors = {'norm_w': 3.43, 'hg_norm_w': 7.387, 'gdn_norm_w': 7.229, 'final_norm_w': 2.829}
    for name, (base, spread) in spreads.items():
        noise = np.random.default_rng([zlib.crc32(name.encode()), seed]).standard_normal(out[name].shape)
        drawn = base * np.exp(spread * noise) if base else spread * noise
        out[name] = __import__('jax').numpy.asarray(drawn.astype(out[name].dtype))
    for name, factor in factors.items():
        out[name] = (out[name] * factor).astype(out[name].dtype)
    return out
```

```python
from contextlib import ExitStack

import concourse.bass as bass
from concourse import mybir

F32 = mybir.dt.float32
F32R = mybir.dt.float32r
U8 = mybir.dt.uint8
ALU = mybir.AluOpType
ACT = mybir.ActivationFunctionType

P = 128
D = 1024
KT = D // P
HEADS = 4
META = 16
SEQ = 1024
NC = 1 + SEQ // P
NT = NC * P
PAD = P - META
TOK = NT - PAD
NG = 3
GC = NC // NG
GW = GC * P
LEVELS = 7
WIDTH = HEADS * P
GD_COLS = 4 * WIDTH
AB_COLS = 8 * WIDTH
EPS = 1e-6
PIECES = ((0, 352), (352, 352), (704, 336))
PARTS = 4
RING = 6
CONVW = 4
YBUFS = 2


class Bank:

    def __init__(self, names):
        self.at = {n: (i % RING, i // RING) for i, n in enumerate(names)}


def hybrid_layer(nc, x, meta_tokens, norm_w, w_in, conv_w, lb_logits, hg_norm_w, A_log, dt_bias,
                 gdn_norm_w, w_out, final_norm_w, out):
    ctx = ExitStack()

    used = {}

    def sb(name, shape, dt=F32, stack=ctx):
        used[name] = used.get(name, 0) + 1
        name += f"_{used[name]}" if used[name] > 1 else ""
        return stack.enter_context(nc.sbuf_tensor(name, shape, dt))

    y_dram = nc.dram_tensor("y_scratch", [2 * HEADS, P, NT], F32, kind="Internal").ap()
    w_in_v = w_in.rearrange("l (k p) c -> p (l k) c", p=P)
    w_out_v = w_out.rearrange("l (k p) c -> p (l k) c", p=P)

    uTh = sb("uTh", [P, KT * TOK], F32R)
    uTl = sb("uTl", [P, KT * TOK], F32R)
    uh = uTh[:, :].rearrange("p (k t) -> p k t", k=KT)
    ul = uTl[:, :].rearrange("p (k t) -> p k t", k=KT)
    woh = uTh[:, 0:KT * D].rearrange("p (k c) -> p k c", k=KT)
    wol = uTl[:, 0:KT * D].rearrange("p (k c) -> p k c", k=KT)
    raw = [sb(f"w_raw{i}", [P, KT, P]) for i in range(2)]
    wh = [sb(f"w_high{i}", [P, KT, P], F32R) for i in range(2)]
    wl = [sb(f"w_low{i}", [P, KT, P], F32R) for i in range(2)]
    hq, hth, hv, hz = (sb(n, [P, NT]) for n in ("hg_q", "hg_th", "hg_v", "hg_z"))
    xq, xk, xv = (sb(n, [P, CONVW - 1 + NT]) for n in ("gd_xq", "gd_xk", "gd_xv"))
    gz = sb("gd_z", [P, NT])
    DT = sb("decay", [P, HEADS, NT])
    cols = sb("gate_cols", [P, HEADS, 5, NC])
    ident = sb("ident", [P, P])
    tri = sb("tri", [P, P])
    mask_st = sb("mask_st", [P, LEVELS + 1, P], U8)
    mask_ts = sb("mask_ts", [P, LEVELS - 1, P], U8)
    prm = sb("prm_t", [P, 66])
    f_ab = sb("f_ab", [P, 2, HEADS])
    neg_half = sb("neg_half", [P, 1])
    bank = [ctx.enter_context(nc.psum_tensor(f"mix{i}", [P, 512], F32)) for i in range(RING)]
    pbank = [ctx.enter_context(nc.psum_tensor(f"proj{i}", [P, 512], F32)) for i in range(2)]
    PRM_NORM, PRM_LB, PRM_HGN, PRM_GDN = 48, 56, 64, 65

    sems = {}

    def sem(name):
        if name not in sems:
            sems[name] = ctx.enter_context(nc.semaphore(name))
        return sems[name]

    mix_full = [sem(f"mix_full{i}") for i in range(RING)]
    mix_free = [sem(f"mix_free{i}") for i in range(RING)]
    raw_loaded = [sem(f"raw_loaded{i}") for i in range(2)]
    w_high, w_low = sem("w_high"), sem("w_low")
    piece_done = sem("piece_done")
    piece_out = sem("piece_out")

    def rsqrt(pool, dst, src, eps, added, n):
        pool.tensor_scalar(src, src, eps, None, ALU.add).then_inc(added, 1)
        pool.wait_ge(added, n)
        return pool.tensor_tensor(dst, src, neg_half[:, 0:1].broadcast_to([P, dst.shape[-1]]), ALU.pow)

    def end_block():
        nc.all_engine_barrier()
        lo = min(s.num for s in sems.values())
        hi = max(s.num for s in sems.values())
        nc.sync.sem_clear(range(lo, hi + 1))
        nc.all_engine_barrier()

    def full(eng, plan, name):
        b, n = plan.at[name]
        eng.wait_ge(mix_full[b], n + 1)
        return bank[b]

    def freed(eng, plan, name):
        b, n = plan.at[name]
        eng.wait_ge(mix_free[b], n + 1)

    def take(pe, plan, name):
        b, n = plan.at[name]
        if n:
            pe.wait_ge(mix_free[b], n)
        return bank[b], mix_full[b]

    def bank_free(plan, name):
        return mix_free[plan.at[name][0]]

    def load_weights(sp, n, src):
        if n >= 2:
            sp.wait_ge(w_low, n - 1)
        sp.dma_start(raw[n % 2][:, :, 0:src.shape[-1]], src).then_inc(raw_loaded[n % 2], 16)

    def project_part(pe, n):
        idx, part = divmod(n, PARTS)
        j, g = divmod(idx, len(PIECES))
        t0, tw = PIECES[g]
        acc = pbank[idx % 2]
        if part == 0:
            if j:
                pe.wait_ge(w_low, j)
            if idx >= 2:
                pe.wait_ge(piece_out, idx - 1)
        per = KT // PARTS
        for k in range(part * per, (part + 1) * per):
            for i, (w, u) in enumerate(((wh, uh), (wh, ul), (wl, uh))):
                last = pe.matmul(acc[:, 0:tw], w[j % 2][:, k, :], u[:, k, t0:t0 + tw],
                                 start=(k == 0 and i == 0), stop=(k == KT - 1 and i == 2))
        if part == PARTS - 1:
            last.then_inc(piece_done, 1)

    def split_high(act, n):
        act.wait_ge(raw_loaded[(n - 1) % 2], 16 * ((n + 1) // 2))
        if n >= 2:
            act.wait_ge(piece_done, 3 * (n - 1))
        act.copy(wh[n % 2][:, :, :], raw[(n - 1) % 2][:, :, :]).then_inc(w_high, 1)

    def split_low(pool, n):
        pool.wait_ge(w_high, n)
        pool.tensor_tensor(wl[n % 2][:, :, :], raw[(n - 1) % 2][:, :, :],
                              wh[n % 2][:, :, :].bitcast(F32), ALU.subtract).then_inc(w_low, 1)

    def take_piece(act, idx, kind):
        j, g = divmod(idx, len(PIECES))
        t0, tw = PIECES[g]
        src = pbank[idx % 2][:, 0:tw]
        act.wait_ge(piece_done, idx + 1)
        if kind == "hg":
            dst = (hq, hth, hv, hz)[j][:, PAD + t0:PAD + t0 + tw]
            fn, scale = ((ACT.Silu, 1.0), (ACT.Tanh, 0.5), (ACT.Copy, 1.0), (ACT.Silu, 1.0))[j]
        else:
            off = PAD + t0 + (CONVW - 1 if j < 3 else 0)
            dst = (xq, xk, xv, gz)[j][:, off:off + tw]
            fn, scale = (ACT.Copy, 1.0) if j < 3 else (ACT.Silu, 1.0)
        act.activation(dst, src, fn, scale=scale).then_inc(piece_out, 1)
        if g == len(PIECES) - 1 and j < 3:
            split_high(act, j + 2)

    def take_pieces(act, parts, kind):
        for n in parts:
            if n % PARTS == PARTS - 1:
                take_piece(act, n // PARTS, kind)

    def tile_cols(kind, j, h):
        return w_in_v[:, :, bass.ds(h * P + j * WIDTH + (GD_COLS if kind == "gd" else 0), P)]

    s5 = ExitStack()
    ab_t = sb("ab_t", [P, NT], F32, s5)
    s1 = ExitStack()
    xt = [sb(f"x_tile{i}", [P, D], F32, s1) for i in range(3)]
    ut = [sb(f"u_part{i}", [P, 512], F32, s1) for i in range(3)]
    square = sb("square", [P, D], F32, s1)
    ms = sb("mean_square", [P, NC], F32, s1)
    rstd = sb("rstd", [P, NC], F32, s1)
    rows = sb("prm_rows", [P, P], F32, s1)
    mwork = sb("mask_work", [P, 2 * LEVELS, P], F32, s1)
    lbw = sb("lb_work", [P, 6, HEADS], F32, s1)
    names = ["rows"] + [("x", i, half) for i in range(NC) for half in range(2)]
    p1 = Bank(names)
    with nc.Block() as block:
        x_in, rows_in = [sem(f"x_in{i}") for i in range(3)], sem("rows_in")
        const0, consts, cast_masks = sem("const0"), sem("consts"), sem("cast_masks")
        sq_done, rstd_done, scaled = sem("sq_done"), sem("rstd_done"), sem("scaled")
        cleared, u_part, u_high, u_low = sem("cleared"), sem("u_part"), sem("u_high"), sem("u_low")
        lb_step, lb_exp, eps_added = sem("lb_step"), sem("lb_exp"), sem("eps_added")

        @block.sync
        def _(sp):
            sp.wait_ge(cleared, 1)
            sp.dma_start(xt[0][PAD:P, :], meta_tokens).then_inc(x_in[0], 16)
            for i in range(1, 3):
                sp.dma_start(xt[i][:, :], x[0, (i - 1) * P:i * P, :]).then_inc(x_in[i % 3], 16)
            sp.dma_start(rows[0:48, :], conv_w.rearrange("l j (b c) -> (l j b) c", c=P)).then_inc(rows_in, 16)
            sp.dma_start(rows[48:56, :], norm_w.rearrange("l (b c) -> (l b) c", c=P)).then_inc(rows_in, 16)
            sp.dma_start(rows[56:64, :], lb_logits.rearrange("l (b c) -> (l b) c", c=P)).then_inc(rows_in, 16)
            sp.dma_start(rows[64:65, :], hg_norm_w).then_inc(rows_in, 16)
            sp.dma_start(rows[65:66, :], gdn_norm_w).then_inc(rows_in, 16)
            sp.dma_start(raw[1][:, :, 0:2 * HEADS], w_in_v[:, :, AB_COLS:AB_COLS + 2 * HEADS]).then_inc(raw_loaded[1], 16)
            sp.dma_start(raw[0][:, :, :], tile_cols("hg", 0, 0)).then_inc(raw_loaded[0], 16)
            for i in range(3, NC):
                full(sp, p1, ("x", i - 3, 1))
                sp.dma_start(xt[i % 3][:, :], x[0, (i - 1) * P:i * P, :]).then_inc(x_in[i % 3], 16)

        def low_part(pool, n):
            i, half = divmod(n, 2)
            w = META if i == 0 else P
            t0 = 0 if i == 0 else META + (i - 1) * P
            pool.wait_ge(u_high, n + 1)
            pool.tensor_tensor(ul[:, 4 * half:4 * half + 4, t0:t0 + w],
                               ut[n % 3][:, 0:4 * w].rearrange("p (k t) -> p k t", k=4),
                               uh[:, 4 * half:4 * half + 4, t0:t0 + w].bitcast(F32),
                               ALU.subtract).then_inc(u_low, 1)

        @block.gpsimd
        def _(pool):
            pool.memset(neg_half[:, :], -0.5)
            pool.memset(ident[:, :], 0.0).then_inc(const0, 1)
            pool.memset(tri[:, :], 1.0).then_inc(const0, 1)
            pool.wait_ge(const0, 2)
            pool.affine_select(out=ident[:, :], in_=ident[:, :], compare_op=ALU.not_equal, fill=1.0,
                               base=0, pattern=[[-1, P]], channel_multiplier=1).then_inc(const0, 1)
            pool.affine_select(out=tri[:, :], in_=tri[:, :], compare_op=ALU.is_ge, fill=0.0,
                               base=0, pattern=[[1, P]], channel_multiplier=-1).then_inc(const0, 1)
            pool.wait_ge(const0, 4)
            pool.tensor_copy(mask_st[:, 0, :], ident[:, :]).then_inc(consts, 1)

            pool.wait_ge(w_high, 2)
            for i in range(2):
                pool.tensor_tensor(wl[i][:, :, :], raw[i][:, :, :],
                              wh[i][:, :, :].bitcast(F32), ALU.subtract).then_inc(w_low, 1)
            for i in range(NC):
                pool.wait_ge(sq_done, i + 1)
                rsqrt(pool, rstd[:, i:i + 1], ms[:, i:i + 1], EPS, eps_added, i + 1).then_inc(rstd_done, 1)
                if i:
                    low_part(pool, 2 * (i - 1))
                    low_part(pool, 2 * (i - 1) + 1)
                if i < LEVELS:
                    b = 1 << i
                    groups = P // (2 * b)
                    v = mwork[:, i, :].rearrange("p (n two b) -> p n two b", two=2, b=b)[:, :, 1, :]
                    if i == 0:
                        pool.wait_ge(cast_masks, 1)
                    pool.affine_select(out=v, in_=v, compare_op=ALU.is_ge, fill=0.0, base=0,
                                       pattern=[[-2 * b, groups], [0, b]], channel_multiplier=1).then_inc(const0, 1)
                    v2 = mwork[:, LEVELS + i, :].rearrange("p (n two b) -> p n two b", two=2, b=b)[:, :, 0, :]
                    pool.affine_select(out=v2, in_=v2, compare_op=ALU.is_ge, fill=0.0, base=-b,
                                       pattern=[[-2 * b, groups], [0, b]], channel_multiplier=1).then_inc(const0, 1)
                    pool.wait_ge(const0, 6 + 4 * i)
                    pool.affine_select(out=v, in_=v, compare_op=ALU.is_ge, fill=0.0, base=b - 1,
                                       pattern=[[2 * b, groups], [0, b]], channel_multiplier=-1).then_inc(const0, 1)
                    pool.affine_select(out=v2, in_=v2, compare_op=ALU.is_ge, fill=0.0, base=2 * b - 1,
                                       pattern=[[2 * b, groups], [0, b]], channel_multiplier=-1).then_inc(const0, 1)
            low_part(pool, 2 * (NC - 1))
            low_part(pool, 2 * (NC - 1) + 1)
            pool.wait_ge(const0, 4 + 4 * LEVELS)
            pool.tensor_copy(mask_st[:, 1:LEVELS + 1, :], mwork[:, 0:LEVELS, :]).then_inc(consts, 1)
            pool.tensor_copy(mask_ts[:, :, :], mwork[:, LEVELS:2 * LEVELS - 1, :]).then_inc(consts, 1)

        def high_part(act, n):
            i, half = divmod(n, 2)
            w = META if i == 0 else P
            t0 = 0 if i == 0 else META + (i - 1) * P
            act.wait_ge(u_part, n + 1)
            act.copy(uh[:, 4 * half:4 * half + 4, t0:t0 + w],
                     ut[n % 3][:, 0:4 * w].rearrange("p (k t) -> p k t", k=4)).then_inc(u_high, 1)

        @block.scalar
        def _(act):
            for i in (1, 0):
                act.wait_ge(raw_loaded[i], 16)
                act.copy(wh[i][:, :, :], raw[i][:, :, :]).then_inc(w_high, 1)
            for i in range(NC):
                act.wait_ge(x_in[i % 3], 16 * (i // 3 + 1))
                if i:
                    act.wait_ge(sq_done, i)
                act.activation(square[:, :], xt[i % 3][:, :], ACT.Square, scale=float(D) ** -0.5,
                               accum_out=ms[:, i:i + 1]).then_inc(sq_done, 1)
                if i == 0:
                    act.wait_ge(lb_step, 2)
                    act.activation(lbw[:, 1:3, :], lbw[:, 3:5, :], ACT.Exp).then_inc(lb_exp, 1)
                if i >= 1:
                    for half in range(2):
                        high_part(act, 2 * (i - 1) + half)
            for half in range(2):
                high_part(act, 2 * (NC - 1) + half)
            for g, (t0, tw) in enumerate(PIECES):
                act.wait_ge(piece_done, g + 1)
                act.copy(ab_t[:, PAD + t0:PAD + t0 + tw], pbank[g % 2][:, 0:tw]).then_inc(piece_out, 1)

        def norm_part(dve, n):
            i, half = divmod(n, 2)
            w = META if i == 0 else P
            src = full(dve, p1, ("x", i, half))[:, :].rearrange("p (k t) -> p k t", k=4)[:, :, P - w:P]
            nw = prm[:, PRM_NORM + 4 * half:PRM_NORM + 4 * half + 4].unsqueeze(2).broadcast_to([P, 4, w])
            if n >= 3:
                dve.wait_ge(u_low, n - 2)
            dve.tensor_tensor(ut[n % 3][:, 0:4 * w].rearrange("p (k t) -> p k t", k=4), src, nw,
                              ALU.mult).then_inc(u_part, 1)
            dve.wait_ge(u_part, n + 1)
            dve.engine_nop().then_inc(bank_free(p1, ("x", i, half)), 1)

        @block.vector
        def _(dve):
            dve.memset(xt[0][:, :], 0.0)
            dve.memset(rows[:, :], 0.0)
            dve.memset(raw[1][:, :, :], 0.0).then_inc(cleared, 1)
            dve.memset(mwork[:, :, :], 0.0).then_inc(cleared, 1)
            dve.wait_ge(cleared, 2)
            for i in range(LEVELS):
                b = 1 << i
                dve.memset(mwork[:, i, :].rearrange("p (n two b) -> p n two b", two=2, b=b)[:, :, 1, :], 1.0)
                last = dve.memset(mwork[:, LEVELS + i, :].rearrange("p (n two b) -> p n two b", two=2, b=b)[:, :, 0, :], 1.0)
            last.then_inc(cast_masks, 1)
            for t in (hq, hv, hz, gz):
                dve.memset(t[:, 0:PAD], 0.0)
            dve.memset(hth[:, 0:PAD], 1.0)
            dve.memset(ab_t[:, 0:PAD], 0.0)
            full(dve, p1, "rows")
            dve.tensor_copy(prm[:, :], bank[0][:, 0:66]).then_inc(mix_free[0], 1)
            freed(dve, p1, "rows")
            lg = prm[:, PRM_LB:PRM_LB + 8].rearrange("p (l h) -> p l h", l=2)
            dve.tensor_tensor(lbw[:, 0, :], lg[:, 0, :], lg[:, 1, :], ALU.max).then_inc(lb_step, 1)
            dve.wait_ge(lb_step, 1)
            dve.tensor_tensor(lbw[:, 3:5, :], lg, lbw[:, 0:1, :].broadcast_to([P, 2, HEADS]), ALU.subtract).then_inc(lb_step, 1)
            dve.wait_ge(lb_exp, 1)
            dve.tensor_tensor(lbw[:, 5, :], lbw[:, 1, :], lbw[:, 2, :], ALU.add).then_inc(lb_step, 1)
            dve.wait_ge(lb_step, 3)
            dve.reciprocal(lbw[:, 0, :], lbw[:, 5, :]).then_inc(lb_step, 1)
            dve.wait_ge(lb_step, 4)
            dve.tensor_tensor(lbw[:, 3, :], lbw[:, 1, :], lbw[:, 0, :], ALU.mult)
            dve.tensor_tensor(lbw[:, 4, :], lbw[:, 2, :], lbw[:, 0, :], ALU.mult).then_inc(lb_step, 1)
            dve.wait_ge(lb_step, 5)
            dve.tensor_scalar(f_ab[:, 1, :], lbw[:, 4, :], 0.5, None, ALU.mult)
            dve.scalar_tensor_tensor(out=f_ab[:, 0, :], in0=lbw[:, 4, :], scalar=0.5, in1=lbw[:, 3, :],
                                     op0=ALU.mult, op1=ALU.add)
            for i in range(NC):
                dve.wait_ge(rstd_done, i + 1)
                dve.tensor_scalar(xt[i % 3][:, :], xt[i % 3][:, :], rstd[:, i:i + 1], None, ALU.mult).then_inc(scaled, 1)
                if i >= 1:
                    for half in range(2):
                        norm_part(dve, 2 * (i - 1) + half)
            for half in range(2):
                norm_part(dve, 2 * (NC - 1) + half)

        @block.tensor
        def _(pe):
            pe.wait_ge(rows_in, 80)
            pe.wait_ge(const0, 4)
            ap, done = take(pe, p1, "rows")
            pe.transpose(ap[:, 0:P], rows[:, :], ident[:, :]).then_inc(done, 1)
            for i in range(NC):
                pe.wait_ge(scaled, i + 1)
                for half in range(2):
                    ap, done = take(pe, p1, ("x", i, half))
                    for k in range(4):
                        c0 = (4 * half + k) * P
                        last = pe.transpose(ap[:, k * P:(k + 1) * P], xt[i % 3][:, c0:c0 + P], ident[:, :])
                    last.then_inc(done, 1)
            pe.wait_ge(w_low, 2)
            pe.wait_ge(u_low, 2 * NC)
            for g, (t0, tw) in enumerate(PIECES):
                if g >= 2:
                    pe.wait_ge(piece_out, g - 1)
                for k in range(KT):
                    for i, (w, u) in enumerate(((wh, uh), (wh, ul), (wl, uh))):
                        last = pe.matmul(pbank[g % 2][:, 0:tw], w[1][:, k, :], u[:, k, t0:t0 + tw],
                                         start=(k == 0 and i == 0), stop=(k == KT - 1 and i == 2))
                last.then_inc(piece_done, 1)
    end_block()
    s1.close()

    s2 = ExitStack()
    ab = sb("ab", [P, NC, 2 * HEADS], F32, s2)
    pr = sb("gate_prm", [P, 2, HEADS], F32, s2)
    ea = sb("exp_a", [P, HEADS], F32, s2)
    gw = sb("gate_work", [P, 6, HEADS, NC], F32, s2)
    g_in = sb("g_in", [P, HEADS, NC], F32, s2)
    gam = sb("gamma", [P, HEADS, NC], F32, s2)
    rep = sb("g_rep", [P, 2, GC, P], F32, s2)
    dtmp = sb("decay_tmp", [P, 2, GW], F32, s2)
    ones = sb("ones", [P, P], F32, s2)
    pmask = sb("pad_mask", [P, 1], F32, s2)
    p2 = Bank([("ab", g) for g in range(NG)] + ["gam", "tot"] + [("dec", n) for n in range(HEADS * NG)])
    P2_PARTS = {("ab", 0): range(0, 2), ("gam", 0): range(2, 12)}
    P2_PARTS.update({("dec", n): range(12 + 3 * n, 15 + 3 * n) for n in range(HEADS * NG)})
    with nc.Block() as block:
        prm_in = sem("prm_in")
        ones_set, pm0, gate_step = sem("ones_set"), sem("pm0"), sem("gate_step")
        gate_exp, gate_rep, dec_sub, dec_exp, g_ready = (sem(n) for n in
                                                         ("gate_exp", "gate_rep", "dec_sub", "dec_exp", "g_ready"))

        @block.sync
        def _(sp):
            sp.dma_start(pr[:, 0, :], A_log[0:1, :].broadcast_to([P, HEADS])).then_inc(prm_in, 16)
            sp.dma_start(pr[:, 1, :], dt_bias[0:1, :].broadcast_to([P, HEADS])).then_inc(prm_in, 16)
            for n in range(1, 5):
                load_weights(sp, n - 1, tile_cols("hg", n, 0) if n < 4 else tile_cols("gd", 0, 0))

        @block.gpsimd
        def _(pool):
            pool.memset(ones[:, :], 1.0).then_inc(ones_set, 1)
            pool.memset(pmask[:, :], 1.0).then_inc(pm0, 1)
            pool.wait_ge(pm0, 1)
            pool.affine_select(out=pmask[:, :], in_=pmask[:, :], compare_op=ALU.is_ge, fill=0.0,
                               base=-PAD, pattern=[[1, 1]], channel_multiplier=1).then_inc(pm0, 1)
            for n in range(1, 5):
                split_low(pool, n)

        @block.scalar
        def _(act):
            split_high(act, 1)
            take_pieces(act, P2_PARTS[("ab", 0)], "hg")
            act.wait_ge(prm_in, 32)
            act.activation(ea[:, :], pr[:, 0, :], ACT.Exp).then_inc(gate_exp, 1)
            act.wait_ge(gate_step, 3)
            act.activation(gw[:, 3:5, :, :], gw[:, 1:3, :, :], ACT.Exp).then_inc(gate_exp, 1)
            act.wait_ge(gate_exp, 2)
            act.activation(gw[:, 5, :, :], gw[:, 3, :, :], ACT.Ln, bias=1.0).then_inc(gate_exp, 1)
            take_pieces(act, P2_PARTS[("gam", 0)], "hg")
            act.wait_ge(gate_step, 12)
            act.activation(cols[:, :, 1, :], gw[:, 0, :, :], ACT.Exp)
            act.activation(cols[:, :, 3, :], gw[:, 1, :, :], ACT.Exp)
            act.activation(cols[:, :, 4, :], gw[:, 2, :, :], ACT.Exp).then_inc(gate_exp, 1)
            for n in range(HEADS * NG):
                h, g = divmod(n, NG)
                act.wait_ge(dec_sub, n + 1)
                act.activation(DT[:, h, g * GW:(g + 1) * GW], dtmp[:, n % 2, :], ACT.Exp).then_inc(dec_exp, 1)
                take_pieces(act, P2_PARTS[("dec", n)], "hg")

        def keep(dve, n):
            h, g = divmod(n, NG)
            dve.wait_ge(dec_exp, n + 1)
            d = DT[:, h, g * GW:(g + 1) * GW].rearrange("p (c t) -> p c t", c=GC)
            dve.tensor_tensor(d, d, tri[:, :].unsqueeze(1).broadcast_to([P, GC, P]), ALU.mult)

        @block.vector
        def _(dve):
            step = [0]

            def link(ins):
                step[0] += 1
                ins.then_inc(gate_step, 1)
                dve.wait_ge(gate_step, step[0])

            for g in range(NG):
                src = full(dve, p2, ("ab", g))[:, 0:GW].rearrange("p (c t) -> p c t", c=GC)[:, :, 0:2 * HEADS]
                dve.tensor_copy(ab[:, g * GC:(g + 1) * GC, :], src).then_inc(bank_free(p2, ("ab", g)), 1)
            for g in range(NG):
                freed(dve, p2, ("ab", g))
            dve.wait_ge(prm_in, 32)
            av = ab[:, :, 0:HEADS].rearrange("p c h -> p h c")
            bv = ab[:, :, HEADS:2 * HEADS].rearrange("p c h -> p h c")
            link(dve.tensor_tensor(gw[:, 0, :, :], av, pr[:, 1, :].unsqueeze(2).broadcast_to([P, HEADS, NC]), ALU.add))
            link(dve.scalar_tensor_tensor(out=gw[:, 1, :, :], in0=gw[:, 0, :, :], scalar=-1.0,
                                          in1=gw[:, 0, :, :], op0=ALU.mult, op1=ALU.min))
            link(dve.tensor_scalar(gw[:, 2, :, :], bv, -1.0, None, ALU.mult))
            dve.wait_ge(gate_exp, 3)
            link(dve.scalar_tensor_tensor(out=gw[:, 0, :, :], in0=gw[:, 0, :, :], scalar=0.0,
                                          in1=gw[:, 5, :, :], op0=ALU.max, op1=ALU.add))
            link(dve.scalar_tensor_tensor(out=g_in[:, :, :], in0=gw[:, 0, :, :], scalar=-1.0,
                                          in1=ea[:, :].unsqueeze(2).broadcast_to([P, HEADS, NC]),
                                          op0=ALU.mult, op1=ALU.mult))
            link(dve.tensor_scalar(gw[:, 4, :, :], gw[:, 4, :, :], 1.0, None, ALU.add))
            link(dve.reciprocal(cols[:, :, 0, :], gw[:, 4, :, :]))
            dve.wait_ge(pm0, 2)
            link(dve.tensor_scalar(cols[:, :, 0, 0:1], cols[:, :, 0, 0:1], pmask[:, 0:1], None, ALU.mult))
            link(dve.tensor_scalar(g_in[:, :, 0:1], g_in[:, :, 0:1], pmask[:, 0:1], None, ALU.mult))

            def replicate(n):
                h, g = divmod(n, NG)
                if n >= 2:
                    full(dve, p2, ("dec", n - 2))
                dve.tensor_copy(rep[:, n % 2, :, :],
                                g_in[:, h, g * GC:(g + 1) * GC].unsqueeze(2).broadcast_to([P, GC, P])).then_inc(gate_rep, 1)

            src = full(dve, p2, "gam")[:, 0:HEADS * NC].rearrange("p (h c) -> p h c", h=HEADS)
            link(dve.tensor_copy(gam[:, :, :], src))
            tot = full(dve, p2, "tot")[:, 0:HEADS * NC].rearrange("p (h c) -> p h c", h=HEADS)
            dve.tensor_copy(gw[:, 0, :, :], gam[:, :, :])
            dve.tensor_tensor(gw[:, 2, :, :], tot, gam[:, :, :], ALU.subtract)
            link(dve.tensor_copy(gw[:, 1, :, :], tot))
            link(dve.tensor_scalar(gw[:, 2, :, :], gw[:, 2, :, :], 0.0, None, ALU.min))
            dve.engine_nop().then_inc(bank_free(p2, "gam"), 1)
            dve.engine_nop().then_inc(bank_free(p2, "tot"), 1)
            dve.wait_ge(gate_exp, 4)
            dve.tensor_scalar(cols[:, :, 2, :], cols[:, :, 1, :], -1.0, None, ALU.mult)
            replicate(0)
            replicate(1)
            for n in range(HEADS * NG):
                h, g = divmod(n, NG)
                src = full(dve, p2, ("dec", n))[:, 0:GW].rearrange("p (c t) -> p c t", c=GC)
                if n >= 2:
                    dve.wait_ge(dec_exp, n - 1)
                tmp = dtmp[:, n % 2, :].rearrange("p (c t) -> p c t", c=GC)
                dve.tensor_tensor(tmp, src, gam[:, h, g * GC:(g + 1) * GC].unsqueeze(2).broadcast_to([P, GC, P]),
                                  ALU.subtract).then_inc(bank_free(p2, ("dec", n)), 1)
                freed(dve, p2, ("dec", n))
                dve.tensor_scalar(dtmp[:, n % 2, :], dtmp[:, n % 2, :], 0.0, None, ALU.min).then_inc(dec_sub, 1)
                if n + 2 < HEADS * NG:
                    replicate(n + 2)
                if n:
                    keep(dve, n - 1)
            keep(dve, HEADS * NG - 1)

        @block.tensor
        def _(pe):
            for g in range(NG):
                ap, done = take(pe, p2, ("ab", g))
                for i in range(GC):
                    c = g * GC + i
                    last = pe.transpose(ap[:, i * P:(i + 1) * P], ab_t[:, c * P:(c + 1) * P], ident[:, :])
                last.then_inc(done, 1)
            for n in P2_PARTS[("ab", 0)]:
                project_part(pe, n)
            pe.wait_ge(gate_step, 9)
            pe.wait_ge(ones_set, 1)
            g_all = g_in[:, :, :].rearrange("p h c -> p (h c)")
            ap, done = take(pe, p2, "gam")
            pe.matmul(ap[:, 0:HEADS * NC], tri[:, :], g_all, start=True, stop=True).then_inc(done, 1)
            ap, done = take(pe, p2, "tot")
            pe.matmul(ap[:, 0:HEADS * NC], ones[:, :], g_all, start=True, stop=True).then_inc(done, 1)
            for n in P2_PARTS[("gam", 0)]:
                project_part(pe, n)
            for n in range(HEADS * NG):
                pe.wait_ge(gate_rep, n + 1)
                ap, done = take(pe, p2, ("dec", n))
                for i in range(GC):
                    last = pe.matmul(ap[:, i * P:(i + 1) * P], rep[:, n % 2, i, :], tri[:, :], start=True, stop=True)
                last.then_inc(done, 1)
                for m in P2_PARTS[("dec", n)]:
                    project_part(pe, m)
    end_block()
    s2.close()
    s5.close()

    def phase_hg(h):
        more = not (isinstance(h, int) and h == HEADS - 1)
        st = ExitStack()
        pre = sb("f_prefix", [P, GW], F32, st)
        suf = sb("f_suffix", [P, GW], F32, st)
        kk = sb("hg_k", [P, GW], F32, st)
        X = [sb(f"level_x{i}", [P, GW], F32, st) for i in range(2)]
        A = sb("hg_scores", [P, GC, P], F32, st)
        vtok = sb("hg_vtok", [P, GW], F32, st)
        qf = sb("hg_qf", [P, GW], F32, st)
        kf = sb("hg_kf", [P, GW], F32, st)
        ktok = sb("hg_ktok", [P, GW], F32, st)
        on = sb("hg_on", [P, GW], F32, st)
        yb = [sb(f"hg_y{i}", [P, GW], F32, st) for i in range(YBUFS)]
        S = sb("hg_state", [P, P], F32, st)
        tot = sb("hg_tot", [P, GC], F32, st)
        ss = sb("hg_ss", [P, GC], F32, st)
        rs = sb("hg_rs", [P, GC], F32, st)
        sq = sb("hg_sq", [P, GW], F32, st)
        fc = sb("hg_fcur", [P, 3], F32, st)
        names, parts, at = [], {}, 0
        for g in range(NG):
            names += [("gram", g, m) for m in range(LEVELS + 1)] + [("tv", g), ("tk", g), ("o", g)]
            names += [("kv", g, i) for i in range(GC)] + [("ty", g)]
            for key, n in ([(("gram", g, m), 1 if m else 0) for m in range(LEVELS + 1)] + [(("t", g), 2)]
                           + [(("rec", g, i), 2) for i in range(GC)] + [(("ty", g), 1)]):
                parts[key] = range(at, at + n)
                at += n
        assert at == PARTS * 12
        plan = Bank(names)
        halves = lambda t, b: t[:, :].rearrange("p (n two b) -> p n two b", two=2, b=b)
        with nc.Block() as block:
            init, par, fk, lvl = sem("hg_init"), sem("hg_par"), sem("hg_fk"), sem("hg_lvl")
            suf_done, x_done, qk_final, tot_set = sem("hg_suf"), sem("hg_x"), sem("hg_qk_final"), sem("hg_tot_set")
            ssq, rstd_s, y_out = sem("hg_ssq"), sem("hg_rstd"), [sem(f"hg_y_out{i}") for i in range(2)]

            @block.sync
            def _(sp):
                for n in range(1, 5):
                    load_weights(sp, n - 1, tile_cols("gd", n, h) if n < 4 else tile_cols("hg", 0, h + 1)
                                 ) if n < 4 or not (isinstance(h, int) and h == HEADS - 1) else None
                for g in range(NG):
                    freed(sp, plan, ("ty", g))
                    lo = P if g == 0 else g * GW
                    sp.dma_start(y_dram[bass.ds(h, 1), :, lo:(g + 1) * GW].rearrange("a p t -> (a p) t"),
                                 yb[g % YBUFS][:, lo - g * GW:GW]).then_inc(y_out[g % 2], 16)
                sp.wait_ge(y_out[0], 32)
                sp.wait_ge(y_out[1], 16)

            @block.gpsimd
            def _(pool):
                for g in range(NG):
                    if g == 0:
                        split_low(pool, 1)
                    else:
                        split_low(pool, g + 1)
                    pool.memset(suf[:, :], 1.0)
                    gs = slice(g * GW, (g + 1) * GW)
                    pool.wait_ge(fk, g + 1)
                    for i in range(LEVELS):
                        n = LEVELS * g + i
                        b = 1 << i
                        if i:
                            pool.wait_ge(lvl, n)
                        if n >= 2:
                            g2, i2 = divmod(n - 2, LEVELS)
                            full(pool, plan, ("gram", g2, i2 + 1))
                        xv_, kv_, sv_, pv_ = (halves(t, b) for t in (X[n % 2], kk, suf, pre))
                        qv_ = hq[:, gs].rearrange("p (n two b) -> p n two b", two=2, b=b)
                        if i == 0:
                            pool.tensor_copy(xv_[:, :, 0, :], kv_[:, :, 0, :])
                        else:
                            pool.tensor_tensor(xv_[:, :, 0, :], kv_[:, :, 0, :], sv_[:, :, 0, :], ALU.mult)
                        pool.tensor_tensor(xv_[:, :, 1, :], qv_[:, :, 1, :], pv_[:, :, 1, :], ALU.mult).then_inc(x_done, 1)
                    pool.wait_ge(lvl, LEVELS * (g + 1))
                    if g:
                        full(pool, plan, ("o", g - 1))
                    pool.tensor_tensor(kf[:, :], kk[:, :], suf[:, :], ALU.mult).then_inc(qk_final, 1)
                    pool.tensor_tensor(qf[:, :], hq[:, gs], pre[:, :], ALU.mult).then_inc(qk_final, 1)
                    pool.wait_ge(ssq, g + 1)
                    rsqrt(pool, rs[:, :], ss[:, :], EPS, eps_added, g + 1).then_inc(rstd_s, 1)
                if more:
                    split_low(pool, 4)

            def take_gd(act, rng):
                for n in rng:
                    if n % PARTS == PARTS - 1:
                        idx = n // PARTS
                        if idx == 8 and not more:
                            take_piece_last(act, idx)
                        else:
                            take_piece(act, idx, "gd")

            def take_piece_last(act, idx):
                t0, tw = PIECES[idx % 3]
                act.wait_ge(piece_done, idx + 1)
                act.copy(xv[:, PAD + t0 + 3:PAD + t0 + 3 + tw], pbank[idx % 2][:, 0:tw]).then_inc(piece_out, 1)

            @block.scalar
            def _(act):
                split_high(act, 1)
                for g in range(NG):
                    for m in range(LEVELS + 1):
                        take_gd(act, parts[("gram", g, m)])
                    act.copy(vtok[:, :], full(act, plan, ("tv", g))[:, 0:GW]).then_inc(bank_free(plan, ("tv", g)), 1)
                    act.copy(ktok[:, :], full(act, plan, ("tk", g))[:, 0:GW]).then_inc(bank_free(plan, ("tk", g)), 1)
                    take_gd(act, parts[("t", g)])
                    for i in range(GC - 1):
                        take_gd(act, parts[("rec", g, i)])
                    o = full(act, plan, ("o", g))
                    for i in range(GC):
                        last = act.activation(sq[:, i * P:(i + 1) * P], o[:, i * P:(i + 1) * P], ACT.Square,
                                              scale=float(P) ** -0.5, accum_out=ss[:, i:i + 1])
                    last.then_inc(ssq, 1)
                    take_gd(act, parts[("rec", g, GC - 1)])
                    act.wait_ge(rstd_s, g + 1)
                    for i in range(GC):
                        last = act.activation(on[:, i * P:(i + 1) * P], o[:, i * P:(i + 1) * P], ACT.Copy,
                                              scale=rs[:, i:i + 1])
                    last.then_inc(bank_free(plan, ("o", g)), 1)
                    take_gd(act, parts[("ty", g)])

            def merge(dve, g, m):
                if m:
                    freed(dve, plan, ("gram", g, m - 1))
                src = full(dve, plan, ("gram", g, m))[:, 0:GW].rearrange("p (c t) -> p c t", c=GC)
                dve.copy_predicated(A[:, :, :], mask_st[:, m, :].unsqueeze(1).broadcast_to([P, GC, P]), src
                                    ).then_inc(bank_free(plan, ("gram", g, m)), 1)

            @block.vector
            def _(dve):
                dve.tensor_copy(fc[:, 0:2], f_ab[:, :, bass.ds(h, 1)].rearrange("p a b -> p (a b)")).then_inc(par, 1)
                for t in (xq, xk, xv):
                    dve.memset(t[:, 0:CONVW - 1 + PAD], 0.0)
                dve.memset(A[:, :, :], 0.0)
                dve.memset(S[:, :], 0.0).then_inc(init, 1)
                dve.wait_ge(par, 1)
                dve.tensor_scalar(fc[:, 2:3], fc[:, 1:2], -1.0, None, ALU.mult).then_inc(par, 1)
                dve.wait_ge(par, 2)
                for g in range(NG):
                    gs = slice(g * GW, (g + 1) * GW)
                    if g:
                        dve.wait_ge(qk_final, 2 * g)
                    dve.tensor_scalar(pre[:, :], hth[:, gs], fc[:, 1:2], fc[:, 0:1], ALU.mult, ALU.add)
                    dve.tensor_scalar(kk[:, :], hth[:, gs], fc[:, 2:3], fc[:, 1:2], ALU.mult, ALU.add).then_inc(fk, 1)
                    for i in range(LEVELS):
                        b = 1 << i
                        n = LEVELS * g + i
                        dve.wait_ge(x_done, n + 1)
                        pv_, sv_ = halves(pre, b), halves(suf, b)
                        bc = [P, GW // (2 * b), b]
                        last_of = lambda half: pv_[:, :, half, b - 1:b].broadcast_to([P, GW // (2 * b), b])
                        dve.tensor_tensor(sv_[:, :, 0, :], sv_[:, :, 0, :], last_of(1), ALU.mult).then_inc(suf_done, 1)
                        dve.wait_ge(suf_done, n + 1)
                        dve.tensor_tensor(pv_[:, :, 1, :], pv_[:, :, 1, :], last_of(0), ALU.mult).then_inc(lvl, 1)
                        merge(dve, g, i)
                    merge(dve, g, LEVELS)
                    dve.wait_ge(lvl, LEVELS * (g + 1))
                    dve.tensor_copy(tot[:, :], pre[:, P - 1:GW:P]).then_inc(tot_set, 1)
                    dve.wait_ge(tot_set, g + 1)
                    for i in range(GC):
                        src = full(dve, plan, ("kv", g, i))
                        dve.scalar_tensor_tensor(out=S[:, :], in0=S[:, :], scalar=tot[:, i:i + 1], in1=src[:, 0:P],
                                                 op0=ALU.mult, op1=ALU.add).then_inc(bank_free(plan, ("kv", g, i)), 1)
                    src = full(dve, plan, ("ty", g))
                    if g >= YBUFS:
                        dve.wait_ge(y_out[g % 2], 16)
                    dve.scalar_tensor_tensor(out=yb[g % YBUFS][:, :], in0=src[:, 0:GW],
                                             scalar=prm[:, PRM_HGN:PRM_HGN + 1], in1=hz[:, gs],
                                             op0=ALU.mult, op1=ALU.mult).then_inc(bank_free(plan, ("ty", g)), 1)

            @block.tensor
            def _(pe):
                for g in range(NG):
                    for m in range(LEVELS + 1):
                        ap, done = take(pe, plan, ("gram", g, m))
                        if m == 0:
                            pe.wait_ge(fk, g + 1)
                        else:
                            pe.wait_ge(x_done, LEVELS * g + m)
                        for i in range(GC):
                            cs = slice(i * P, (i + 1) * P)
                            if m == 0:
                                left, right = kk[:, cs], hq[:, g * GW + i * P:g * GW + (i + 1) * P]
                            else:
                                left = right = X[(LEVELS * g + m - 1) % 2][:, cs]
                            last = pe.matmul(ap[:, cs], left, right, start=True, stop=True)
                        last.then_inc(done, 1)
                        for n in parts[("gram", g, m)]:
                            project_part(pe, n)
                    ap, done = take(pe, plan, ("tv", g))
                    for i in range(GC):
                        last = pe.transpose(ap[:, i * P:(i + 1) * P], hv[:, g * GW + i * P:g * GW + (i + 1) * P], ident[:, :])
                    last.then_inc(done, 1)
                    ap, done = take(pe, plan, ("tk", g))
                    pe.wait_ge(qk_final, 2 * g + 1)
                    for i in range(GC):
                        last = pe.transpose(ap[:, i * P:(i + 1) * P], kf[:, i * P:(i + 1) * P], ident[:, :])
                    last.then_inc(done, 1)
                    for n in parts[("t", g)]:
                        project_part(pe, n)
                    freed(pe, plan, ("gram", g, LEVELS))
                    freed(pe, plan, ("tv", g))
                    freed(pe, plan, ("tk", g))
                    pe.wait_ge(qk_final, 2 * g + 2)
                    if g == 0:
                        pe.wait_ge(init, 1)
                    o, o_done = take(pe, plan, ("o", g))
                    for i in range(GC):
                        cs = slice(i * P, (i + 1) * P)
                        if g or i:
                            gi = GC * g + i - 1
                            freed(pe, plan, ("kv", gi // GC, gi % GC))
                        pe.matmul(o[:, cs], A[:, i, :], vtok[:, cs], start=True, stop=False)
                        last = pe.matmul(o[:, cs], qf[:, cs], S[:, :], start=False, stop=True)
                        if i == GC - 1:
                            last.then_inc(o_done, 1)
                        ap, done = take(pe, plan, ("kv", g, i))
                        pe.matmul(ap[:, 0:P], ktok[:, cs], vtok[:, cs], start=True, stop=True).then_inc(done, 1)
                        for n in parts[("rec", g, i)]:
                            project_part(pe, n)
                    freed(pe, plan, ("o", g))
                    ap, done = take(pe, plan, ("ty", g))
                    for i in range(GC):
                        last = pe.transpose(ap[:, i * P:(i + 1) * P], on[:, i * P:(i + 1) * P], ident[:, :])
                    last.then_inc(done, 1)
                    for n in parts[("ty", g)]:
                        project_part(pe, n)
        end_block()
        st.close()

    def phase_gd(h):
        more = not (isinstance(h, int) and h == HEADS - 1)
        st = ExitStack()
        N, Y, Lt = xq, xk, xv
        M = sb("gd_m", [P, NT], F32, st)
        QK = sb("gd_qk", [P, NT], F32, st)
        kT = sb("gd_kT", [P, NT], F32, st)
        qT = sb("gd_qT", [P, NT], F32, st)
        kd = sb("gd_kd", [P, NT], F32, st)
        vtok = sb("gd_vtok", [P, NT], F32, st)
        cv = [[sb(f"conv{c}{i}", [P, GW], F32, st) for i in range(2)] for c in "qkv"]
        tap = [sb(f"conv_tap{i}", [P, GW], F32, st) for i in range(2)]
        kn = sb("gd_kn", [P, GW], F32, st)
        qn = sb("gd_qn", [P, GW], F32, st)
        r = sb("gd_r", [P, P], F32, st)
        u = sb("gd_u", [P, P], F32, st)
        osb = [sb(f"gd_o{i}", [P, GW], F32, st) for i in range(2)]
        on = kn
        yb = [cv[0][0], cv[0][1]]
        S = sb("gd_state", [P, P], F32, st)
        ss = sb("gd_ss", [P, 2, GC], F32, st)
        rr = sb("gd_rr", [P, 2, GC], F32, st)
        sq = sb("gd_sq", [P, 2, GW], F32, st)
        cw = sb("gd_cw", [P, CONVW, 3], F32, st)
        cc = sb("gd_cc", [P, 5, NC], F32, st)
        names, parts, at = [], {}, 0

        def give(key, n):
            nonlocal at
            parts[key] = range(at, at + n)
            at += n

        for g in range(NG):
            names += [(n, g) for n in ("tk", "tq", "tv", "tkn", "tqn", "kk", "qk")]
            for s in ("A1", "A2", "A3"):
                give((s, g), 2)
        for i in range(LEVELS):
            names += [("Y", i, g) for g in range(NG)] + [("Z", i, g) for g in range(NG)]
            names += [("TM", i, g) for g in range(NG)] if i < LEVELS - 1 else []
            give(("B1", i), 1)
            give(("B2", i), 1)
        for c in range(NC):
            names += [("rec", c), ("U", c)]
            if c % GC == 1 and c > GC:
                names.append(("ty", c // GC - 1))
            give(("C1", c), 1)
            give(("C2", c), 1 if c < 7 else 0)
        names.append(("ty", NG - 1))
        assert at == PARTS * 12
        plan = Bank(names)
        with nc.Block() as block:
            par, conv_step, conv_v_step = sem("gd_par"), sem("gd_conv_step"), sem("gd_conv_v_step")
            conv_done, tap_done, silu = sem("gd_conv"), sem("gd_tap"), sem("gd_silu")
            ssq, rstd_s, kd_done, nm = sem("gd_ssq"), sem("gd_rstd"), sem("gd_kd_done"), sem("gd_nm")
            init, kq_done, r_done, state = sem("gd_init"), sem("gd_kq"), sem("gd_rdone"), sem("gd_state_done")
            on_done, y_out = sem("gd_on"), [sem(f"gd_y_out{i}") for i in range(2)]

            @block.sync
            def _(sp):
                if more:
                    for n in range(1, 5):
                        load_weights(sp, n - 1, tile_cols("hg", n, h + 1) if n < 4 else tile_cols("gd", 0, h + 1))
                else:
                    for n in range(KT):
                        if n >= 2:
                            sp.wait_ge(w_low, n - 1)
                        sp.dma_start(raw[n % 2][:, :, :].rearrange("p k c -> p (k c)"), w_out_v[:, n, :]
                                     ).then_inc(raw_loaded[n % 2], 16)
                for g in range(NG):
                    freed(sp, plan, ("ty", g))
                    lo = P if g == 0 else g * GW
                    sp.dma_start(y_dram[bass.ds(h + HEADS, 1), :, lo:(g + 1) * GW].rearrange("a p t -> (a p) t"),
                                 yb[g % 2][:, lo - g * GW:GW]).then_inc(y_out[g % 2], 16)
                sp.wait_ge(y_out[0], 32)
                sp.wait_ge(y_out[1], 16)

            def out_high(act, n):
                act.wait_ge(raw_loaded[n % 2], 16 * (n // 2 + 1))
                act.copy(woh[:, n, :], raw[n % 2][:, :, :].rearrange("p k c -> p (k c)")).then_inc(w_high, 1)

            def out_low(pool, n):
                pool.wait_ge(w_high, n + 1)
                pool.tensor_tensor(wol[:, n, :], raw[n % 2][:, :, :].rearrange("p k c -> p (k c)"),
                              woh[:, n, :].bitcast(F32), ALU.subtract).then_inc(w_low, 1)

            def take_hg(act, rng):
                if more:
                    take_pieces(act, rng, "hg")

            def project(pe, rng):
                if more:
                    for n in rng:
                        project_part(pe, n)

            def conv_v(pool, g):
                if g >= 2:
                    full(pool, plan, ("tv", g - 2))
                for j in range(CONVW):
                    src = xv[:, g * GW + j:(g + 1) * GW + j]
                    if j == 0:
                        last = pool.tensor_scalar(cv[2][g % 2][:, :], src, cw[:, j, 2:3], None, ALU.mult)
                    else:
                        if CONVW * g + j > 1:
                            pool.wait_ge(conv_v_step, CONVW * g + j - 1)
                        pool.tensor_scalar(tap[j % 2][:, :], src, cw[:, j, 2:3], None, ALU.mult).then_inc(tap_done, 1)
                        pool.wait_ge(tap_done, (CONVW - 1) * g + j)
                        pool.wait_ge(conv_v_step, CONVW * g + j)
                        last = pool.tensor_tensor(cv[2][g % 2][:, :], tap[j % 2][:, :], cv[2][g % 2][:, :], ALU.add)
                    last.then_inc(conv_v_step, 1)

            def scale_rows(pool, g):
                pool.wait_ge(ssq, g + 1)
                rsqrt(pool, rr[:, 0, :], ss[:, 0, :], EPS, eps_added, 2 * g + 1)
                rsqrt(pool, rr[:, 1, :], ss[:, 1, :], EPS * P, eps_added, 2 * g + 2).then_inc(rstd_s, 1)
                freed(pool, plan, ("tk", g))
                k3 = lambda t: t.rearrange("p (c t) -> p c t", c=GC)
                pool.tensor_tensor(k3(kd[:, g * GW:(g + 1) * GW]), k3(kn[:, :]),
                                   cc[:, 4, g * GC:(g + 1) * GC].unsqueeze(2).broadcast_to([P, GC, P]),
                                   ALU.mult).then_inc(kd_done, 1)

            @block.gpsimd
            def _(pool):
                pool.wait_ge(par, 2)
                if more:
                    split_low(pool, 1)
                step = 0
                for g in range(NG):
                    conv_v(pool, g)
                    if g:
                        scale_rows(pool, g - 1)
                    if more and g:
                        split_low(pool, 2) if g == 2 else None
                scale_rows(pool, NG - 1)
                if more:
                    split_low(pool, 3)
                    split_low(pool, 4)
                else:
                    for n in range(KT):
                        out_low(pool, n)
                for g in range(NG):
                    pool.wait_ge(ssq, NG + g + 1)
                    rsqrt(pool, rr[:, 0, :], ss[:, 0, :], EPS, eps_added, 2 * NG + g + 1).then_inc(rstd_s, 1)

            @block.scalar
            def _(act):
                def silu3(g):
                    for n in range(3):
                        if n < 2:
                            act.wait_ge(conv_done, 2 * g + n + 1)
                        else:
                            act.wait_ge(conv_v_step, CONVW * (g + 1))
                        act.activation(cv[n][g % 2][:, :], cv[n][g % 2][:, :], ACT.Silu).then_inc(silu, 1)

                if more:
                    split_high(act, 1)
                silu3(0)
                for g in range(NG):
                    gs = slice(g * GW, (g + 1) * GW)
                    if g:
                        act.wait_ge(rstd_s, g)
                    for n, (name, scale) in enumerate((("tk", 1.0), ("tq", float(P) ** 0.5))):
                        src = full(act, plan, (name, g))
                        for i in range(GC):
                            last = act.activation(sq[:, n, i * P:(i + 1) * P], src[:, i * P:(i + 1) * P], ACT.Square, scale=scale,
                                                  accum_out=ss[:, n, i:i + 1])
                    last.then_inc(ssq, 1)
                    act.copy(vtok[:, gs], full(act, plan, ("tv", g))[:, 0:GW]).then_inc(bank_free(plan, ("tv", g)), 1)
                    take_hg(act, parts[("A1", g)])
                    if g + 1 < NG:
                        silu3(g + 1)
                    act.copy(kT[:, gs], full(act, plan, ("tkn", g))[:, 0:GW]).then_inc(bank_free(plan, ("tkn", g)), 1)
                    act.copy(qT[:, gs], full(act, plan, ("tqn", g))[:, 0:GW]).then_inc(bank_free(plan, ("tqn", g)), 1)
                    take_hg(act, parts[("A2", g)])
                    take_hg(act, parts[("A3", g)])
                for i in range(LEVELS):
                    if not more:
                        out_high(act, i)
                    for g in range(NG):
                        gs = slice(g * GW, (g + 1) * GW)
                        act.copy(Y[:, gs], full(act, plan, ("Y", i, g))[:, 0:GW]).then_inc(bank_free(plan, ("Y", i, g)), 1)
                    take_hg(act, parts[("B1", i)])
                    if i < LEVELS - 1:
                        for g in range(NG):
                            gs = slice(g * GW, (g + 1) * GW)
                            act.copy(M[:, gs], full(act, plan, ("TM", i, g))[:, 0:GW]).then_inc(bank_free(plan, ("TM", i, g)), 1)
                    take_hg(act, parts[("B2", i)])
                if not more:
                    out_high(act, KT - 1)

                def squares(g):
                    freed(act, plan, ("rec", GC * g + GC - 1))
                    for i in range(GC):
                        last = act.activation(sq[:, 0, i * P:(i + 1) * P], osb[g % 2][:, i * P:(i + 1) * P], ACT.Square,
                                              scale=float(P) ** -0.5, accum_out=ss[:, 0, i:i + 1])
                    last.then_inc(ssq, 1)

                def normed(g):
                    act.wait_ge(rstd_s, NG + g + 1)
                    for i in range(GC):
                        last = act.activation(on[:, i * P:(i + 1) * P], osb[g % 2][:, i * P:(i + 1) * P], ACT.Copy,
                                              scale=rr[:, 0, i:i + 1])
                    last.then_inc(on_done, 1)

                for c in range(NC):
                    take_hg(act, parts[("C1", c)])
                    act.copy(u[:, :], full(act, plan, ("U", c))[:, 0:P]).then_inc(bank_free(plan, ("U", c)), 1)
                    take_hg(act, parts[("C2", c)])
                    if c % GC == 0 and c:
                        squares(c // GC - 1)
                    if c % GC == 1 and c > GC:
                        normed(c // GC - 1)
                squares(NG - 1)
                normed(NG - 1)

            @block.vector
            def _(dve):
                dve.tensor_copy(cw[:, :, :], prm[:, 0:3 * CONVW * HEADS].rearrange("p (j y h) -> p j y h", j=CONVW, y=3)[
                    :, :, :, bass.ds(h, 1)].rearrange("p j y h -> p j (y h)")).then_inc(par, 1)
                dve.tensor_copy(cc[:, :, :], cols[:, bass.ds(h, 1), :, :].rearrange("p h a c -> p (h a) c")).then_inc(par, 1)
                dve.memset(S[:, :], 0.0).then_inc(init, 1)
                dve.wait_ge(par, 2)
                step = [0]

                def conv(g):
                    for n, name in ((0, "tq"), (1, "tk")):
                        if g >= 2:
                            full(dve, plan, (name, g - 2))
                    for j in range(CONVW):
                        if j:
                            dve.wait_ge(conv_step, step[0])
                        for n, x_ in ((0, xq), (1, xk)):
                            src = x_[:, g * GW + j:(g + 1) * GW + j]
                            if j == 0:
                                last = dve.tensor_scalar(cv[n][g % 2][:, :], src, cw[:, j, n:n + 1], None, ALU.mult)
                            else:
                                last = dve.scalar_tensor_tensor(out=cv[n][g % 2][:, :], in0=src, scalar=cw[:, j, n:n + 1],
                                                                in1=cv[n][g % 2][:, :], op0=ALU.mult, op1=ALU.add)
                            if j < CONVW - 1:
                                step[0] += 1
                                last.then_inc(conv_step, 1)
                            else:
                                last.then_inc(conv_done, 1)

                k3 = lambda t: t.rearrange("p (c t) -> p c t", c=GC)

                def norm(g):
                    dve.wait_ge(rstd_s, g + 1)
                    if g:
                        full(dve, plan, ("tqn", g - 1))
                        dve.wait_ge(kd_done, g)
                    for n, (t, name) in enumerate(((kn, "tk"), (qn, "tq"))):
                        dve.tensor_tensor(k3(t[:, :]), k3(full(dve, plan, (name, g))[:, 0:GW]),
                                          rr[:, n, :].unsqueeze(2).broadcast_to([P, GC, P]),
                                          ALU.mult).then_inc(bank_free(plan, (name, g)), 1)

                def scores(g):
                    gs = slice(g * GW, (g + 1) * GW)
                    dec = DT[:, bass.ds(h, 1), gs].rearrange("p h t -> p (h t)")
                    dve.scalar_tensor_tensor(out=Lt[:, gs], in0=full(dve, plan, ("kk", g))[:, 0:GW], scalar=-1.0,
                                             in1=dec, op0=ALU.mult, op1=ALU.mult).then_inc(bank_free(plan, ("kk", g)), 1)
                    dve.tensor_tensor(QK[:, gs], full(dve, plan, ("qk", g))[:, 0:GW], dec,
                                      ALU.mult).then_inc(bank_free(plan, ("qk", g)), 1)

                conv(0)
                for g in range(NG):
                    if g + 1 < NG:
                        conv(g + 1)
                    norm(g)
                    scores(g)
                for g in range(NG):
                    gs = slice(g * GW, (g + 1) * GW)
                    for t in (N, M):
                        last = dve.tensor_tensor(k3(t[:, gs]), ident[:, :].unsqueeze(1).broadcast_to([P, GC, P]),
                                                 cc[:, 0, g * GC:(g + 1) * GC].unsqueeze(2).broadcast_to([P, GC, P]), ALU.mult)
                    last.then_inc(nm, 1)
                dve.wait_ge(nm, NG)
                for i in range(LEVELS):
                    for g in range(NG):
                        gs = slice(g * GW, (g + 1) * GW)
                        src = k3(full(dve, plan, ("Z", i, g))[:, 0:GW])
                        dst, msk = (N, mask_ts[:, min(i, LEVELS - 2), :]) if i < LEVELS - 1 else (M, mask_st[:, LEVELS, :])
                        dve.copy_predicated(k3(dst[:, gs]), msk.unsqueeze(1).broadcast_to([P, GC, P]), src
                                            ).then_inc(bank_free(plan, ("Z", i, g)), 1)

                def finish(g):
                    src = full(dve, plan, ("ty", g))
                    if g >= 2:
                        dve.wait_ge(y_out[g % 2], 16)
                    dve.scalar_tensor_tensor(out=yb[g % 2][:, :], in0=src[:, 0:GW],
                                             scalar=prm[:, PRM_GDN:PRM_GDN + 1], in1=gz[:, g * GW:(g + 1) * GW],
                                             op0=ALU.mult, op1=ALU.mult).then_inc(bank_free(plan, ("ty", g)), 1)

                for c in range(NC):
                    g, i = divmod(c, GC)
                    dve.wait_ge(kq_done, c + 1)
                    rec = bank[plan.at[("rec", c)][0]]
                    dve.scalar_tensor_tensor(out=r[:, :], in0=rec[:, 0:P], scalar=cc[:, 2, c:c + 1],
                                             in1=vtok[:, c * P:(c + 1) * P], op0=ALU.mult, op1=ALU.add).then_inc(r_done, 1)
                    full(dve, plan, ("rec", c))
                    dve.scalar_tensor_tensor(out=S[:, :], in0=S[:, :], scalar=cc[:, 3, c:c + 1],
                                             in1=rec[:, 2 * P:3 * P], op0=ALU.mult, op1=ALU.add).then_inc(state, 1)
                    dve.tensor_scalar(osb[g % 2][:, i * P:(i + 1) * P], rec[:, P:2 * P], cc[:, 1, c:c + 1], None,
                                      ALU.mult).then_inc(conv_step, 1)
                    step[0] += 1
                    dve.wait_ge(conv_step, step[0])
                    dve.tensor_tensor(osb[g % 2][:, i * P:(i + 1) * P], osb[g % 2][:, i * P:(i + 1) * P],
                                      rec[:, 3 * P:4 * P], ALU.add).then_inc(bank_free(plan, ("rec", c)), 1)
                    if c % GC == 2 and c > GC:
                        finish(c // GC - 1)
                finish(NG - 1)

            @block.tensor
            def _(pe):
                def three(name, g, left, right=None, wait=None):
                    ap, done = take(pe, plan, name)
                    if wait:
                        freed(pe, plan, wait)
                    for i in range(GC):
                        cs = slice(i * P, (i + 1) * P)
                        if right is None:
                            last = pe.transpose(ap[:, cs], left(i), ident[:, :])
                        else:
                            last = pe.matmul(ap[:, cs], left(i), right(i), start=True, stop=True)
                    last.then_inc(done, 1)

                full_c = lambda t, g: (lambda i: t[:, (g * GC + i) * P:(g * GC + i + 1) * P])
                part_c = lambda t: (lambda i: t[:, i * P:(i + 1) * P])
                for g in range(NG):
                    for name, n, sil in (("tk", 1, 2), ("tq", 0, 1), ("tv", 2, 3)):
                        pe.wait_ge(silu, 3 * g + (2 if n == 1 else sil))
                        three((name, g), g, part_c(cv[n][g % 2]))
                    project(pe, parts[("A1", g)])
                    three(("tkn", g), g, part_c(kn), wait=("tk", g))
                    three(("tqn", g), g, part_c(qn), wait=("tq", g))
                    project(pe, parts[("A2", g)])
                    three(("kk", g), g, full_c(kT, g), full_c(kT, g), wait=("tkn", g))
                    three(("qk", g), g, full_c(kT, g), full_c(qT, g), wait=("tqn", g))
                    project(pe, parts[("A3", g)])
                for i in range(LEVELS):
                    for g in range(NG):
                        if i == 0:
                            pe.wait_ge(nm, g + 1)
                        three(("Y", i, g), g, full_c(Lt, g), full_c(N, g), wait=("Z", i - 1, g) if i else ("kk", g))
                    project(pe, parts[("B1", i)])
                    for g in range(NG):
                        if i:
                            freed(pe, plan, ("TM", i - 1, g))
                        l, rt = (M, Y) if i < LEVELS - 1 else (Y, M)
                        three(("Z", i, g), g, full_c(l, g), full_c(rt, g), wait=("Y", i, g))
                    project(pe, parts[("B2", i)])
                    if i < LEVELS - 1:
                        for g in range(NG):
                            three(("TM", i, g), g, full_c(N, g), wait=("Z", i, g))
                for g in range(NG):
                    freed(pe, plan, ("Z", LEVELS - 1, g))
                pe.wait_ge(kd_done, NG)
                pe.wait_ge(init, 1)
                for c in range(NC):
                    cs = slice(c * P, (c + 1) * P)
                    rec, rec_done = take(pe, plan, ("rec", c))
                    if c:
                        pe.wait_ge(state, c)
                    pe.matmul(rec[:, 0:P], kT[:, cs], S[:, :], start=True, stop=True)
                    pe.matmul(rec[:, P:2 * P], qT[:, cs], S[:, :], start=True, stop=True).then_inc(kq_done, 1)
                    project(pe, parts[("C1", c)])
                    ap, done = take(pe, plan, ("U", c))
                    pe.wait_ge(r_done, c + 1)
                    pe.matmul(ap[:, 0:P], M[:, cs], r[:, :], start=True, stop=True).then_inc(done, 1)
                    project(pe, parts[("C2", c)])
                    freed(pe, plan, ("U", c))
                    pe.matmul(rec[:, 2 * P:3 * P], kd[:, cs], u[:, :], start=True, stop=True)
                    pe.matmul(rec[:, 3 * P:4 * P], QK[:, cs], u[:, :], start=True, stop=True).then_inc(rec_done, 1)
                    if c % GC == 1 and c > GC:
                        g = c // GC - 1
                        pe.wait_ge(on_done, g + 1)
                        three(("ty", g), g, part_c(on))
                pe.wait_ge(on_done, NG)
                three(("ty", NG - 1), NG - 1, part_c(on))
        end_block()
        st.close()

    with nc.Fori(0, HEADS - 1) as h:
        phase_hg(h)
        phase_gd(h)
    phase_hg(HEADS - 1)
    phase_gd(HEADS - 1)

    st = ExitStack()
    yraw = [sb(f"y_raw{i}", [P, KT, P], F32, st) for i in range(2)]
    xin = [sb(f"x_in{i}", [P, D], F32, st) for i in range(2)]
    hs = [sb(f"h_sum{i}", [P, D], F32, st) for i in range(2)]
    res = [sb(f"result{i}", [P, D], F32, st) for i in range(2)]
    fw = sb("final_w", [P, D], F32, st)
    sqo = sb("square_o", [P, D], F32, st)
    mso = sb("ms_o", [P, NC], F32, st)
    rso = sb("rs_o", [P, NC], F32, st)
    TILES = SEQ // P
    with nc.Block() as block:
        fw_in, y_in, x_in2 = sem("fw_in"), [sem(f"y_in{i}") for i in range(2)], [sem(f"x_in2_{i}") for i in range(2)]
        y_high, y_low, summed, o_ss, o_rs, o_res = (sem(n) for n in ("y_high", "y_low", "summed", "o_ss", "o_rs", "o_res"))
        o_done, stored = sem("o_done"), [sem(f"stored{i}") for i in range(2)]
        obank = [bank[0], bank[1], bank[2], bank[3]]

        @block.sync
        def _(sp):
            sp.dma_start(fw[:, :], final_norm_w.rearrange("(a c) -> a c", a=1).broadcast_to([P, D])).then_inc(fw_in, 16)
            for t in range(TILES + 1):
                if t < TILES:
                    if t >= 2:
                        sp.wait_ge(y_low, t - 1)
                        sp.wait_ge(summed, 2 * (t - 1))
                    sp.dma_start(yraw[t % 2][:, :, :], y_dram[:, :, (t + 1) * P:(t + 2) * P].rearrange("k p t -> p k t")
                                 ).then_inc(y_in[t % 2], 16)
                    sp.dma_start(xin[t % 2][:, :], x[0, t * P:(t + 1) * P, :]).then_inc(x_in2[t % 2], 16)
                if t:
                    sp.wait_ge(o_res, t)
                    sp.dma_start(out[0, (t - 1) * P:t * P, :], res[(t - 1) % 2][:, :]).then_inc(stored[(t - 1) % 2], 16)
            for i in range(2):
                sp.wait_ge(stored[i], 16 * TILES // 2)

        @block.scalar
        def _(act):
            def square_tile(t):
                act.wait_ge(summed, 2 * (t + 1))
                if t:
                    act.wait_ge(o_ss, t)
                act.activation(sqo[:, :], hs[t % 2][:, :], ACT.Square, scale=float(D) ** -0.5,
                               accum_out=mso[:, t:t + 1]).then_inc(o_ss, 1)

            for t in range(TILES):
                act.wait_ge(y_in[t % 2], 16 * (t // 2 + 1))
                if t >= 2:
                    act.wait_ge(o_done, 2 * (t - 1))
                act.copy(wh[t % 2][:, :, :], yraw[t % 2][:, :, :]).then_inc(y_high, 1)
                if t:
                    square_tile(t - 1)
            square_tile(TILES - 1)

        @block.gpsimd
        def _(pool):
            def rstd_tile(t):
                pool.wait_ge(o_ss, t + 1)
                rsqrt(pool, rso[:, t:t + 1], mso[:, t:t + 1], EPS, eps_added, t + 1).then_inc(o_rs, 1)

            for t in range(TILES):
                pool.wait_ge(y_high, t + 1)
                pool.tensor_tensor(wl[t % 2][:, :, :], yraw[t % 2][:, :, :],
                              wh[t % 2][:, :, :].bitcast(F32), ALU.subtract).then_inc(y_low, 1)
                if t:
                    rstd_tile(t - 1)
            rstd_tile(TILES - 1)

        @block.tensor
        def _(pe):
            for t in range(TILES):
                pe.wait_ge(y_low, t + 1)
                for half in range(2):
                    n = 2 * t + half
                    if n >= 4:
                        pe.wait_ge(summed, n - 3)
                    for k in range(KT):
                        for i, (y, w) in enumerate(((wh, woh), (wh, wol), (wl, woh))):
                            last = pe.matmul(obank[n % 4][:, :], y[t % 2][:, k, :], w[:, k, half * 512:(half + 1) * 512],
                                             start=(k == 0 and i == 0), stop=(k == KT - 1 and i == 2))
                    last.then_inc(o_done, 1)

        @block.vector
        def _(dve):
            def result_tile(t):
                dve.wait_ge(o_rs, t + 1)
                if t >= 2:
                    dve.wait_ge(stored[t % 2], 16 * (t // 2))
                dve.scalar_tensor_tensor(out=res[t % 2][:, :], in0=hs[t % 2][:, :], scalar=rso[:, t:t + 1],
                                         in1=fw[:, :], op0=ALU.mult, op1=ALU.mult).then_inc(o_res, 1)

            dve.wait_ge(fw_in, 16)
            for t in range(TILES):
                dve.wait_ge(x_in2[t % 2], 16 * (t // 2 + 1))
                for half in range(2):
                    n = 2 * t + half
                    cs = slice(half * 512, (half + 1) * 512)
                    dve.wait_ge(o_done, n + 1)
                    dve.tensor_tensor(hs[t % 2][:, cs], obank[n % 4][:, :], xin[t % 2][:, cs], ALU.add).then_inc(summed, 1)
                if t:
                    result_tile(t - 1)
            result_tile(TILES - 1)
    end_block()
    st.close()
    ctx.close()


_INS = ["x", "meta_tokens", "norm_w", "w_in", "conv_w", "hg_lb_logits", "hg_norm_w", "gdn_A_log",
        "gdn_dt_bias", "gdn_norm_w", "w_out", "final_norm_w"]


def kernel(**inputs):
    import numpy as _np
    import concourse.bacc as _bacc
    from concourse import mybir as _mybir
    from concourse.bass_utils import run_bass_kernel_spmd as _run

    nc = _bacc.Bacc("TRN2", target_bir_lowering=False, num_devices=1)
    arrays, args = {}, []
    for name in _INS:
        a = _np.ascontiguousarray(inputs[name])
        arrays[f"in_{name}"] = a
        args.append(nc.dram_tensor(f"in_{name}", a.shape, _mybir.dt.from_np(a.dtype), kind="ExternalInput").ap())
    args.append(nc.dram_tensor("out_y", (1, SEQ, D), F32, kind="ExternalOutput").ap())
    hybrid_layer(nc, *args)
    r = _run(nc, [arrays], core_ids=[0])
    return r.results[0]["out_y"]
```

```python
from contextlib import ExitStack

import concourse.bass as bass
from concourse import mybir

F32 = mybir.dt.float32
F32R = mybir.dt.float32r
U8 = mybir.dt.uint8
ALU = mybir.AluOpType
ACT = mybir.ActivationFunctionType

P = 128
D = 1024
KT = D // P
HEADS = 4
META = 16
SEQ = 1024
NC = 1 + SEQ // P
NT = NC * P
PAD = P - META
TOK = NT - PAD
NG = 3
GC = NC // NG
GW = GC * P
LEVELS = 7
WIDTH = HEADS * P
GD_COLS = 4 * WIDTH
AB_COLS = 8 * WIDTH
EPS = 1e-6
PIECES = ((0, 352), (352, 352), (704, 336))
PARTS = KT
RING = 6
CONVW = 4
YBUFS = 2


class Bank:

    def __init__(self, names, ring=RING):
        self.at = {n: (i % ring, i // ring) for i, n in enumerate(names)}


def hybrid_layer(nc, x, meta_tokens, norm_w, w_in, conv_w, lb_logits, hg_norm_w, A_log, dt_bias,
                 gdn_norm_w, w_out, final_norm_w, out):
    ctx = ExitStack()

    used = {}

    def sb(name, shape, dt=F32, stack=ctx):
        used[name] = used.get(name, 0) + 1
        name += f"_{used[name]}" if used[name] > 1 else ""
        return stack.enter_context(nc.sbuf_tensor(name, shape, dt))

    y_dram = nc.dram_tensor("y_scratch", [2 * HEADS, P, NT], F32, kind="Internal").ap()
    w_in_v = w_in.rearrange("l (k p) c -> p (l k) c", p=P)
    w_out_v = w_out.rearrange("l (k p) c -> p (l k) c", p=P)

    uTh = sb("uTh", [P, KT * TOK], F32R)
    uTl = sb("uTl", [P, KT * TOK], F32R)
    uh = uTh[:, :].rearrange("p (k t) -> p k t", k=KT)
    ul = uTl[:, :].rearrange("p (k t) -> p k t", k=KT)
    woh = uTh[:, 0:KT * D].rearrange("p (k c) -> p k c", k=KT)
    wol = uTl[:, 0:KT * D].rearrange("p (k c) -> p k c", k=KT)
    raw = [sb(f"w_raw{i}", [P, KT, P]) for i in range(2)]
    wh = [sb(f"w_high{i}", [P, KT, P], F32R) for i in range(2)]
    wl = [sb(f"w_low{i}", [P, KT, P], F32R) for i in range(2)]
    hq, hth, hv, hz = (sb(n, [P, NT]) for n in ("hg_q", "hg_th", "hg_v", "hg_z"))
    xq, xk, xv = (sb(n, [P, NT]) for n in ("gd_xq", "gd_xk", "gd_xv"))
    gz = sb("gd_z", [P, NT])
    DT = sb("decay", [P, HEADS, NT])
    cols = sb("gate_cols", [P, HEADS, 5, NC])
    ident = sb("ident", [P, P])
    tri = sb("tri", [P, P])
    mask_st = sb("mask_st", [P, LEVELS + 1, P], U8)
    mask_ts = sb("mask_ts", [P, LEVELS - 1, P], U8)
    prm = sb("prm_t", [P, 66])
    f_ab = sb("f_ab", [P, 2, HEADS])
    zero3 = sb("zero3", [P, CONVW - 1])
    neg_half = sb("neg_half", [P, 1])
    bank = [ctx.enter_context(nc.psum_tensor(f"mix{i}", [P, 512], F32)) for i in range(RING)]
    pbank = [ctx.enter_context(nc.psum_tensor(f"proj{i}", [P, 512], F32)) for i in range(2)]
    PRM_NORM, PRM_LB, PRM_HGN, PRM_GDN = 48, 56, 64, 65

    sems = {}

    def sem(name):
        if name not in sems:
            sems[name] = ctx.enter_context(nc.semaphore(name))
        return sems[name]

    mix_full = [sem(f"mix_full{i}") for i in range(RING)]
    mix_free = [sem(f"mix_free{i}") for i in range(RING)]
    raw_loaded = [sem(f"raw_loaded{i}") for i in range(2)]
    w_high, w_low = sem("w_high"), sem("w_low")
    piece_done = sem("piece_done")
    piece_out = sem("piece_out")

    def rsqrt(pool, dst, src, eps, added, n):
        pool.tensor_scalar(src, src, eps, None, ALU.add).then_inc(added, 1)
        pool.wait_ge(added, n)
        return pool.tensor_tensor(dst, src, neg_half[:, 0:1].broadcast_to([P, dst.shape[-1]]), ALU.pow)

    def end_block():
        nc.all_engine_barrier()
        lo = min(s.num for s in sems.values())
        hi = max(s.num for s in sems.values())
        nc.sync.sem_clear(range(lo, hi + 1))
        nc.all_engine_barrier()

    def full(eng, plan, name):
        b, n = plan.at[name]
        eng.wait_ge(mix_full[b], n + 1)
        return bank[b]

    def freed(eng, plan, name):
        b, n = plan.at[name]
        eng.wait_ge(mix_free[b], n + 1)

    def take(pe, plan, name):
        b, n = plan.at[name]
        if n:
            pe.wait_ge(mix_free[b], n)
        return bank[b], mix_full[b]

    def bank_free(plan, name):
        return mix_free[plan.at[name][0]]

    def load_weights(sp, n, src):
        if n >= 2:
            sp.wait_ge(w_low, n - 1)
        sp.dma_start(raw[n % 2][:, :, 0:src.shape[-1]], src).then_inc(raw_loaded[n % 2], 16)

    def project_part(pe, n):
        idx, part = divmod(n, PARTS)
        j, g = divmod(idx, len(PIECES))
        t0, tw = PIECES[g]
        acc = pbank[idx % 2]
        if part == 0:
            if j:
                pe.wait_ge(w_low, j)
            if idx >= 2:
                pe.wait_ge(piece_out, idx - 1)
        per = KT // PARTS
        for k in range(part * per, (part + 1) * per):
            for i, (w, u) in enumerate(((wh, uh), (wh, ul), (wl, uh))):
                last = pe.matmul(acc[:, 0:tw], w[j % 2][:, k, :], u[:, k, t0:t0 + tw],
                                 start=(k == 0 and i == 0), stop=(k == KT - 1 and i == 2))
        if part == PARTS - 1:
            last.then_inc(piece_done, 1)

    def split_high(act, n):
        act.wait_ge(raw_loaded[(n - 1) % 2], 16 * ((n + 1) // 2))
        if n >= 2:
            act.wait_ge(piece_done, 3 * (n - 1))
        act.copy(wh[n % 2][:, :, :], raw[(n - 1) % 2][:, :, :]).then_inc(w_high, 1)

    def split_low(pool, n):
        pool.wait_ge(w_high, n)
        pool.tensor_tensor(wl[n % 2][:, :, :], raw[(n - 1) % 2][:, :, :],
                              wh[n % 2][:, :, :].bitcast(F32), ALU.subtract).then_inc(w_low, 1)

    def take_piece(act, idx):
        j, g = divmod(idx, len(PIECES))
        t0, tw = PIECES[g]
        act.wait_ge(piece_done, idx + 1)
        fn, scale = ((ACT.Silu, 1.0), (ACT.Tanh, 0.5), (ACT.Copy, 1.0), (ACT.Silu, 1.0))[j]
        act.activation((hq, hth, hv, hz)[j][:, PAD + t0:PAD + t0 + tw], pbank[idx % 2][:, 0:tw], fn,
                       scale=scale).then_inc(piece_out, 1)
        if g == len(PIECES) - 1 and j < 3:
            split_high(act, j + 2)

    def pieces(parts):
        return [n // PARTS for n in parts if n % PARTS == PARTS - 1]

    def tile_cols(kind, j, h):
        return w_in_v[:, :, bass.ds(h * P + j * WIDTH + (GD_COLS if kind == "gd" else 0), P)]

    s5 = ExitStack()
    ab_t = sb("ab_t", [P, NT], F32, s5)
    s1 = ExitStack()
    xt = [sb(f"x_tile{i}", [P, D], F32, s1) for i in range(3)]
    ut = [sb(f"u_part{i}", [P, 512], F32, s1) for i in range(3)]
    square = sb("square", [P, D], F32, s1)
    ms = sb("mean_square", [P, NC], F32, s1)
    rstd = sb("rstd", [P, NC], F32, s1)
    rows = sb("prm_rows", [P, P], F32, s1)
    lbw = sb("lb_work", [P, 6, HEADS], F32, s1)
    names = ["rows"] + [("x", i, half) for i in range(NC) for half in range(2)]
    p1 = Bank(names)
    with nc.Block() as block:
        x_in, rows_in = [sem(f"x_in{i}") for i in range(3)], sem("rows_in")
        const0, consts = sem("const0"), sem("consts")
        sq_done, rstd_done, scaled = sem("sq_done"), sem("rstd_done"), sem("scaled")
        cleared, u_high, u_low = sem("cleared"), sem("u_high"), sem("u_low")
        lb_step, lb_exp, eps_added = sem("lb_step"), sem("lb_exp"), sem("eps_added")

        @block.sync
        def _(sp):
            sp.wait_ge(cleared, 1)
            sp.dma_start(xt[0][PAD:P, :], meta_tokens).then_inc(x_in[0], 16)
            for i in range(1, 3):
                sp.dma_start(xt[i][:, :], x[0, (i - 1) * P:i * P, :]).then_inc(x_in[i % 3], 16)
            sp.dma_start(rows[0:48, :], conv_w.rearrange("l j (b c) -> (l j b) c", c=P)).then_inc(rows_in, 16)
            sp.dma_start(rows[48:56, :], norm_w.rearrange("l (b c) -> (l b) c", c=P)).then_inc(rows_in, 16)
            sp.dma_start(rows[56:64, :], lb_logits.rearrange("l (b c) -> (l b) c", c=P)).then_inc(rows_in, 16)
            sp.dma_start(rows[64:65, :], hg_norm_w).then_inc(rows_in, 16)
            sp.dma_start(rows[65:66, :], gdn_norm_w).then_inc(rows_in, 16)
            sp.dma_start(raw[1][:, :, 0:2 * HEADS], w_in_v[:, :, AB_COLS:AB_COLS + 2 * HEADS]).then_inc(raw_loaded[1], 16)
            sp.dma_start(raw[0][:, :, :], tile_cols("hg", 0, 0)).then_inc(raw_loaded[0], 16)
            for i in range(3, NC):
                full(sp, p1, ("x", i - 3, 1))
                sp.dma_start(xt[i % 3][:, :], x[0, (i - 1) * P:i * P, :]).then_inc(x_in[i % 3], 16)

        @block.gpsimd
        def _(pool):
            pool.memset(neg_half[:, :], -0.5)
            pool.memset(ident[:, :], 0.0).then_inc(const0, 1)
            pool.memset(tri[:, :], 1.0).then_inc(const0, 1)
            pool.wait_ge(const0, 2)
            pool.affine_select(out=ident[:, :], in_=ident[:, :], compare_op=ALU.not_equal, fill=1.0,
                               base=0, pattern=[[-1, P]], channel_multiplier=1).then_inc(const0, 1)
            pool.affine_select(out=tri[:, :], in_=tri[:, :], compare_op=ALU.is_ge, fill=0.0,
                               base=0, pattern=[[1, P]], channel_multiplier=-1).then_inc(const0, 1)
            pool.wait_ge(const0, 4)
            pool.tensor_copy(mask_st[:, 0, :], ident[:, :]).then_inc(consts, 1)

            pool.wait_ge(w_high, 2)
            for i in range(2):
                pool.tensor_tensor(wl[i][:, :, :], raw[i][:, :, :],
                              wh[i][:, :, :].bitcast(F32), ALU.subtract).then_inc(w_low, 1)
            for i in range(NC):
                pool.wait_ge(sq_done, i + 1)
                rsqrt(pool, rstd[:, i:i + 1], ms[:, i:i + 1], EPS, eps_added, i + 1).then_inc(rstd_done, 1)

        def high_part(act, n):
            i, half = divmod(n, 2)
            w = META if i == 0 else P
            t0 = 0 if i == 0 else META + (i - 1) * P
            freed(act, p1, ("x", i, half))
            act.copy(uh[:, 4 * half:4 * half + 4, t0:t0 + w],
                     ut[n % 3][:, 0:4 * w].rearrange("p (k t) -> p k t", k=4)).then_inc(u_high, 1)

        @block.scalar
        def _(act):
            for i in (1, 0):
                act.wait_ge(raw_loaded[i], 16)
                act.copy(wh[i][:, :, :], raw[i][:, :, :]).then_inc(w_high, 1)
            def square_tile(i):
                act.wait_ge(x_in[i % 3], 16 * (i // 3 + 1))
                if i:
                    act.wait_ge(sq_done, i)
                act.activation(square[:, :], xt[i % 3][:, :], ACT.Square, scale=float(D) ** -0.5,
                               accum_out=ms[:, i:i + 1]).then_inc(sq_done, 1)

            square_tile(0)
            for i in range(NC):
                if i + 1 < NC:
                    square_tile(i + 1)
                act.wait_ge(rstd_done, i + 1)
                act.wait_ge(sq_done, i + 1)
                act.activation(xt[i % 3][:, :], xt[i % 3][:, :], ACT.Copy, scale=rstd[:, i:i + 1]).then_inc(scaled, 1)
                if i == 0:
                    act.wait_ge(lb_step, 2)
                    act.activation(lbw[:, 1:3, :], lbw[:, 3:5, :], ACT.Exp).then_inc(lb_exp, 1)
                if i >= 1:
                    for half in range(2):
                        high_part(act, 2 * (i - 1) + half)
            for half in range(2):
                high_part(act, 2 * (NC - 1) + half)
            for g, (t0, tw) in enumerate(PIECES):
                act.wait_ge(piece_done, g + 1)
                act.copy(ab_t[:, PAD + t0:PAD + t0 + tw], pbank[g % 2][:, 0:tw]).then_inc(piece_out, 1)

        def low_part(dve, n):
            i, half = divmod(n, 2)
            w = META if i == 0 else P
            t0 = 0 if i == 0 else META + (i - 1) * P
            dve.wait_ge(u_high, n + 1)
            dve.tensor_tensor(ul[:, 4 * half:4 * half + 4, t0:t0 + w],
                              ut[n % 3][:, 0:4 * w].rearrange("p (k t) -> p k t", k=4),
                              uh[:, 4 * half:4 * half + 4, t0:t0 + w].bitcast(F32),
                              ALU.subtract).then_inc(u_low, 1)

        def norm_part(dve, n):
            i, half = divmod(n, 2)
            w = META if i == 0 else P
            src = full(dve, p1, ("x", i, half))[:, :].rearrange("p (k t) -> p k t", k=4)[:, :, P - w:P]
            nw = prm[:, PRM_NORM + 4 * half:PRM_NORM + 4 * half + 4].unsqueeze(2).broadcast_to([P, 4, w])
            if n >= 3:
                dve.wait_ge(u_low, n - 2)
            dve.tensor_tensor(ut[n % 3][:, 0:4 * w].rearrange("p (k t) -> p k t", k=4), src, nw,
                              ALU.mult).then_inc(bank_free(p1, ("x", i, half)), 1)

        @block.vector
        def _(dve):
            dve.memset(xt[0][:, :], 0.0)
            dve.memset(rows[:, :], 0.0)
            dve.memset(raw[1][:, :, :], 0.0).then_inc(cleared, 1)
            for t in (hq, hv, hz, gz):
                dve.memset(t[:, 0:PAD], 0.0)
            dve.memset(hth[:, 0:PAD], 1.0)
            dve.memset(zero3[:, :], 0.0)
            dve.memset(ab_t[:, 0:PAD], 0.0)
            full(dve, p1, "rows")
            dve.tensor_copy(prm[:, :], bank[0][:, 0:66]).then_inc(mix_free[0], 1)
            freed(dve, p1, "rows")
            lg = prm[:, PRM_LB:PRM_LB + 8].rearrange("p (l h) -> p l h", l=2)
            dve.tensor_tensor(lbw[:, 0, :], lg[:, 0, :], lg[:, 1, :], ALU.max).then_inc(lb_step, 1)
            dve.wait_ge(lb_step, 1)
            dve.tensor_tensor(lbw[:, 3:5, :], lg, lbw[:, 0:1, :].broadcast_to([P, 2, HEADS]), ALU.subtract).then_inc(lb_step, 1)
            dve.wait_ge(lb_exp, 1)
            dve.tensor_tensor(lbw[:, 5, :], lbw[:, 1, :], lbw[:, 2, :], ALU.add).then_inc(lb_step, 1)
            dve.wait_ge(lb_step, 3)
            dve.reciprocal(lbw[:, 0, :], lbw[:, 5, :]).then_inc(lb_step, 1)
            dve.wait_ge(lb_step, 4)
            dve.tensor_tensor(lbw[:, 3, :], lbw[:, 1, :], lbw[:, 0, :], ALU.mult)
            dve.tensor_tensor(lbw[:, 4, :], lbw[:, 2, :], lbw[:, 0, :], ALU.mult).then_inc(lb_step, 1)
            dve.wait_ge(lb_step, 5)
            dve.tensor_scalar(f_ab[:, 1, :], lbw[:, 4, :], 0.5, None, ALU.mult)
            dve.scalar_tensor_tensor(out=f_ab[:, 0, :], in0=lbw[:, 4, :], scalar=0.5, in1=lbw[:, 3, :],
                                     op0=ALU.mult, op1=ALU.add)
            for n in range(2 * NC):
                norm_part(dve, n)
                if n:
                    low_part(dve, n - 1)
            low_part(dve, 2 * NC - 1)

        @block.tensor
        def _(pe):
            pe.wait_ge(rows_in, 80)
            pe.wait_ge(const0, 4)
            ap, done = take(pe, p1, "rows")
            pe.transpose(ap[:, 0:P], rows[:, :], ident[:, :]).then_inc(done, 1)
            for i in range(NC):
                pe.wait_ge(scaled, i + 1)
                for half in range(2):
                    ap, done = take(pe, p1, ("x", i, half))
                    for k in range(4):
                        c0 = (4 * half + k) * P
                        last = pe.transpose(ap[:, k * P:(k + 1) * P], xt[i % 3][:, c0:c0 + P], ident[:, :])
                    last.then_inc(done, 1)
            pe.wait_ge(w_low, 2)
            pe.wait_ge(u_low, 2 * NC)
            for g, (t0, tw) in enumerate(PIECES):
                if g >= 2:
                    pe.wait_ge(piece_out, g - 1)
                for k in range(KT):
                    for i, (w, u) in enumerate(((wh, uh), (wh, ul), (wl, uh))):
                        last = pe.matmul(pbank[g % 2][:, 0:tw], w[1][:, k, :], u[:, k, t0:t0 + tw],
                                         start=(k == 0 and i == 0), stop=(k == KT - 1 and i == 2))
                last.then_inc(piece_done, 1)
    end_block()
    s1.close()

    s2 = ExitStack()
    ab = sb("ab", [P, NC, 2 * HEADS], F32, s2)
    pr = sb("gate_prm", [P, 2, HEADS], F32, s2)
    ea = sb("exp_a", [P, HEADS], F32, s2)
    gw = sb("gate_work", [P, 6, HEADS, NC], F32, s2)
    g_in = sb("g_in", [P, HEADS, NC], F32, s2)
    gam = sb("gamma", [P, HEADS, NC], F32, s2)
    rep = sb("g_rep", [P, 2, GC, P], F32, s2)
    dtmp = sb("decay_tmp", [P, 2, GW], F32, s2)
    ones = sb("ones", [P, P], F32, s2)
    mwork = sb("mask_work", [P, 2 * LEVELS, P], F32, s2)
    pmask = sb("pad_mask", [P, 1], F32, s2)
    p2 = Bank([("ab", g) for g in range(NG)] + ["gam", "tot"] + [("dec", n) for n in range(HEADS * NG)])
    P2_PARTS = {("ab", 0): range(0, 20), ("gam", 0): range(20, 24)}
    P2_PARTS.update({("dec", n): range(24 + 6 * n, 30 + 6 * n) for n in range(HEADS * NG)})
    with nc.Block() as block:
        prm_in = sem("prm_in")
        ones_set, pm0, gate_step, mask_step, mask_set = sem("ones_set"), sem("pm0"), sem("gate_step"), sem("mask_step"), sem("mask_set")
        gate_exp, gate_rep, dec_exp = (sem(n) for n in
                                                         ("gate_exp", "gate_rep", "dec_exp"))

        @block.sync
        def _(sp):
            sp.dma_start(pr[:, 0, :], A_log[0:1, :].broadcast_to([P, HEADS])).then_inc(prm_in, 16)
            sp.dma_start(pr[:, 1, :], dt_bias[0:1, :].broadcast_to([P, HEADS])).then_inc(prm_in, 16)
            for n in range(1, 5):
                load_weights(sp, n - 1, tile_cols("hg", n, 0) if n < 4 else tile_cols("gd", 0, 0))

        @block.gpsimd
        def _(pool):
            pool.memset(ones[:, :], 1.0).then_inc(ones_set, 1)
            pool.memset(pmask[:, :], 1.0).then_inc(pm0, 1)
            pool.wait_ge(pm0, 1)
            pool.affine_select(out=pmask[:, :], in_=pmask[:, :], compare_op=ALU.is_ge, fill=0.0,
                               base=-PAD, pattern=[[1, 1]], channel_multiplier=1).then_inc(pm0, 1)
            split_low(pool, 1)

            def replicate(n):
                h, g = divmod(n, NG)
                if n >= 2:
                    full(pool, p2, ("dec", n - 2))
                pool.tensor_copy(rep[:, n % 2, :, :],
                                 g_in[:, h, g * GC:(g + 1) * GC].unsqueeze(2).broadcast_to([P, GC, P])).then_inc(gate_rep, 1)

            pool.wait_ge(mask_set, 2)
            for cut in range(2):
                for i in range(LEVELS):
                    b = 1 << i
                    groups = P // (2 * b)
                    sign = 1 - 2 * cut
                    v = mwork[:, i, :].rearrange("p (n two b) -> p n two b", two=2, b=b)[:, :, 1, :]
                    pool.affine_select(out=v, in_=v, compare_op=ALU.is_ge, fill=0.0, base=(b - 1) * cut,
                                       pattern=[[-2 * b * sign, groups], [0, b]], channel_multiplier=sign)
                    v = mwork[:, LEVELS + i, :].rearrange("p (n two b) -> p n two b", two=2, b=b)[:, :, 0, :]
                    last = pool.affine_select(out=v, in_=v, compare_op=ALU.is_ge, fill=0.0,
                                              base=(2 * b - 1) * cut - b * (1 - cut),
                                              pattern=[[-2 * b * sign, groups], [0, b]], channel_multiplier=sign)
                last.then_inc(mask_step, 1)
                pool.wait_ge(mask_step, 1 + cut)
            pool.wait_ge(gate_step, 9)
            replicate(0)
            replicate(1)
            for n in range(HEADS * NG):
                if n == 2:
                    split_low(pool, 2)
                if n == 6:
                    split_low(pool, 3)
                if n + 2 < HEADS * NG:
                    replicate(n + 2)
            split_low(pool, 4)

        @block.scalar
        def _(act):
            split_high(act, 1)
            for n in pieces(P2_PARTS[("ab", 0)]):
                take_piece(act, n)
            act.wait_ge(prm_in, 32)
            act.activation(ea[:, :], pr[:, 0, :], ACT.Exp).then_inc(gate_exp, 1)
            act.wait_ge(gate_step, 3)
            act.activation(gw[:, 3:5, :, :], gw[:, 1:3, :, :], ACT.Exp).then_inc(gate_exp, 1)
            act.wait_ge(gate_exp, 2)
            act.activation(gw[:, 5, :, :], gw[:, 3, :, :], ACT.Ln, bias=1.0).then_inc(gate_exp, 1)
            for n in pieces(P2_PARTS[("gam", 0)]):
                take_piece(act, n)
            act.wait_ge(gate_step, 12)
            act.activation(cols[:, :, 1, :], gw[:, 0, :, :], ACT.Exp)
            act.activation(cols[:, :, 3, :], gw[:, 1, :, :], ACT.Exp)
            act.activation(cols[:, :, 4, :], gw[:, 2, :, :], ACT.Exp).then_inc(gate_exp, 1)
            for n in range(HEADS * NG):
                h, g = divmod(n, NG)
                freed(act, p2, ("dec", n))
                act.activation(DT[:, h, g * GW:(g + 1) * GW], dtmp[:, n % 2, :], ACT.Exp).then_inc(dec_exp, 1)
                for m in pieces(P2_PARTS[("dec", n)]):
                    take_piece(act, m)

        def keep(dve, n):
            h, g = divmod(n, NG)
            dve.wait_ge(dec_exp, n + 1)
            d = DT[:, h, g * GW:(g + 1) * GW].rearrange("p (c t) -> p c t", c=GC)
            dve.tensor_tensor(d, d, tri[:, :].unsqueeze(1).broadcast_to([P, GC, P]), ALU.mult)

        @block.vector
        def _(dve):
            step = [0]

            def link(ins):
                step[0] += 1
                ins.then_inc(gate_step, 1)
                dve.wait_ge(gate_step, step[0])

            dve.memset(mwork[:, :, :], 0.0).then_inc(mask_set, 1)
            dve.wait_ge(mask_set, 1)
            for i in range(LEVELS):
                b = 1 << i
                dve.memset(mwork[:, i, :].rearrange("p (n two b) -> p n two b", two=2, b=b)[:, :, 1, :], 1.0)
                last = dve.memset(mwork[:, LEVELS + i, :].rearrange("p (n two b) -> p n two b", two=2, b=b)[:, :, 0, :], 1.0)
            last.then_inc(mask_set, 1)
            for g in range(NG):
                src = full(dve, p2, ("ab", g))[:, 0:GW].rearrange("p (c t) -> p c t", c=GC)[:, :, 0:2 * HEADS]
                dve.tensor_copy(ab[:, g * GC:(g + 1) * GC, :], src).then_inc(bank_free(p2, ("ab", g)), 1)
            for g in range(NG):
                freed(dve, p2, ("ab", g))
            dve.wait_ge(prm_in, 32)
            av = ab[:, :, 0:HEADS].rearrange("p c h -> p h c")
            bv = ab[:, :, HEADS:2 * HEADS].rearrange("p c h -> p h c")
            link(dve.tensor_tensor(gw[:, 0, :, :], av, pr[:, 1, :].unsqueeze(2).broadcast_to([P, HEADS, NC]), ALU.add))
            link(dve.scalar_tensor_tensor(out=gw[:, 1, :, :], in0=gw[:, 0, :, :], scalar=-1.0,
                                          in1=gw[:, 0, :, :], op0=ALU.mult, op1=ALU.min))
            link(dve.tensor_scalar(gw[:, 2, :, :], bv, -1.0, None, ALU.mult))
            dve.wait_ge(gate_exp, 3)
            link(dve.scalar_tensor_tensor(out=gw[:, 0, :, :], in0=gw[:, 0, :, :], scalar=0.0,
                                          in1=gw[:, 5, :, :], op0=ALU.max, op1=ALU.add))
            link(dve.scalar_tensor_tensor(out=g_in[:, :, :], in0=gw[:, 0, :, :], scalar=-1.0,
                                          in1=ea[:, :].unsqueeze(2).broadcast_to([P, HEADS, NC]),
                                          op0=ALU.mult, op1=ALU.mult))
            link(dve.tensor_scalar(gw[:, 4, :, :], gw[:, 4, :, :], 1.0, None, ALU.add))
            link(dve.reciprocal(cols[:, :, 0, :], gw[:, 4, :, :]))
            dve.wait_ge(pm0, 2)
            link(dve.tensor_scalar(cols[:, :, 0, 0:1], cols[:, :, 0, 0:1], pmask[:, 0:1], None, ALU.mult))
            link(dve.tensor_scalar(g_in[:, :, 0:1], g_in[:, :, 0:1], pmask[:, 0:1], None, ALU.mult))

            src = full(dve, p2, "gam")[:, 0:HEADS * NC].rearrange("p (h c) -> p h c", h=HEADS)
            link(dve.tensor_copy(gam[:, :, :], src))
            tot = full(dve, p2, "tot")[:, 0:HEADS * NC].rearrange("p (h c) -> p h c", h=HEADS)
            dve.tensor_copy(gw[:, 0, :, :], gam[:, :, :])
            dve.tensor_tensor(gw[:, 2, :, :], tot, gam[:, :, :], ALU.subtract)
            link(dve.tensor_copy(gw[:, 1, :, :], tot))
            link(dve.tensor_scalar(gw[:, 2, :, :], gw[:, 2, :, :], 0.0, None, ALU.min))
            dve.engine_nop().then_inc(bank_free(p2, "gam"), 1)
            dve.engine_nop().then_inc(bank_free(p2, "tot"), 1)
            dve.wait_ge(gate_exp, 4)
            dve.tensor_scalar(cols[:, :, 2, :], cols[:, :, 1, :], -1.0, None, ALU.mult)
            for n in range(HEADS * NG):
                h, g = divmod(n, NG)
                src = full(dve, p2, ("dec", n))
                if n >= 2:
                    dve.wait_ge(dec_exp, n - 1)
                for i in range(GC):
                    c = g * GC + i
                    last = dve.tensor_scalar(dtmp[:, n % 2, i * P:(i + 1) * P], src[:, i * P:(i + 1) * P],
                                             gam[:, h, c:c + 1], 0.0, ALU.subtract, ALU.min)
                last.then_inc(bank_free(p2, ("dec", n)), 1)
                if n:
                    keep(dve, n - 1)
            keep(dve, HEADS * NG - 1)
            dve.wait_ge(mask_step, 2)
            dve.tensor_copy(mask_st[:, 1:LEVELS + 1, :], mwork[:, 0:LEVELS, :])
            dve.tensor_copy(mask_ts[:, :, :], mwork[:, LEVELS:2 * LEVELS - 1, :])

        @block.tensor
        def _(pe):
            for g in range(NG):
                ap, done = take(pe, p2, ("ab", g))
                for i in range(GC):
                    c = g * GC + i
                    last = pe.transpose(ap[:, i * P:(i + 1) * P], ab_t[:, c * P:(c + 1) * P], ident[:, :])
                last.then_inc(done, 1)
            for n in P2_PARTS[("ab", 0)]:
                project_part(pe, n)
            pe.wait_ge(gate_step, 9)
            pe.wait_ge(ones_set, 1)
            g_all = g_in[:, :, :].rearrange("p h c -> p (h c)")
            ap, done = take(pe, p2, "gam")
            pe.matmul(ap[:, 0:HEADS * NC], tri[:, :], g_all, start=True, stop=True).then_inc(done, 1)
            ap, done = take(pe, p2, "tot")
            pe.matmul(ap[:, 0:HEADS * NC], ones[:, :], g_all, start=True, stop=True).then_inc(done, 1)
            for n in P2_PARTS[("gam", 0)]:
                project_part(pe, n)
            for n in range(HEADS * NG):
                pe.wait_ge(gate_rep, n + 1)
                ap, done = take(pe, p2, ("dec", n))
                for i in range(GC):
                    last = pe.matmul(ap[:, i * P:(i + 1) * P], rep[:, n % 2, i, :], tri[:, :], start=True, stop=True)
                last.then_inc(done, 1)
                for m in P2_PARTS[("dec", n)]:
                    project_part(pe, m)
    end_block()
    s2.close()
    s5.close()

    def phase_hg(h):
        more = not (isinstance(h, int) and h == HEADS - 1)
        st = ExitStack()
        pre = sb("f_prefix", [P, GW], F32, st)
        suf = sb("f_suffix", [P, GW], F32, st)
        kk = sb("hg_k", [P, GW], F32, st)
        X = [sb(f"level_x{i}", [P, GW], F32, st) for i in range(2)]
        A = [sb(f"hg_scores{i}", [P, GC, P], F32, st) for i in range(2)]
        vtok = sb("hg_vtok", [P, GW], F32, st)
        qf = sb("hg_qf", [P, GW], F32, st)
        kf = sb("hg_kf", [P, GW], F32, st)
        ktok = sb("hg_ktok", [P, GW], F32, st)
        on = sb("hg_on", [P, GW], F32, st)
        yb = [sb(f"hg_y{i}", [P, GW], F32, st) for i in range(2)]
        S = sb("hg_state", [P, P], F32, st)
        tot = [sb(f"hg_tot{i}", [P, GC], F32, st) for i in range(2)]
        ss = sb("hg_ss", [P, GC], F32, st)
        rs = sb("hg_rs", [P, GC], F32, st)
        sq = sb("hg_sq", [P, GW], F32, st)
        fc = sb("hg_fcur", [P, 3], F32, st)
        cw = sb("hg_taps", [P, CONVW, 3], F32, st)
        TW = PIECES[0][1]
        cin = [sb(f"conv_in{i}", [P, CONVW - 1 + TW], F32, st) for i in range(3)]
        cout = [sb(f"conv_out{i}", [P, TW], F32, st) for i in range(2)]
        steps = [("lead",)]
        names = []
        for g in range(NG):
            for m in range(LEVELS + 1):
                names.append(("gram", g, m))
                steps.append(("gram", g, m))
                if g and m in (2, 4, 6):
                    names.append(("kv", g - 1, m // 2 - 1))
                    steps.append(("rec", g - 1, m // 2 - 1))
            if g:
                names.append(("ty", g - 1))
                steps.append(("ty", g - 1))
            names += [("tv", g), ("tk", g)]
            steps.append(("t", g))
        for i in range(GC):
            names.append(("kv", NG - 1, i))
            steps.append(("rec", NG - 1, i))
        names.append(("ty", NG - 1))
        steps.append(("end",))
        parts, at = {}, 0
        for key in steps:
            n = {"lead": 4, "end": 10}.get(key[0], 4 if key[:2] == ("rec", NG - 1) else 2)
            parts[key] = range(at, at + n)
            at += n
        assert at == PARTS * 4 * len(PIECES)
        plan = Bank(names, RING - 1)
        for g in range(NG):
            plan.at[("o", g)] = (RING - 1, g)
        halves = lambda t, b: t[:, :].rearrange("p (n two b) -> p n two b", two=2, b=b)
        chunk = lambda i: slice(i * P, (i + 1) * P)
        with nc.Block() as block:
            init, par, fk = sem("hg_init"), sem("hg_par"), sem("hg_fk")
            suf_done, pre_done = sem("hg_suf"), sem("hg_pre")
            x_even, x_odd, kf_done, qf_done = sem("hg_x_even"), sem("hg_x_odd"), sem("hg_kf"), sem("hg_qf")
            tot_set, ssq, rstd_s = sem("hg_tot_set"), sem("hg_ssq"), sem("hg_rstd")
            y_out = [sem(f"hg_y_out{i}") for i in range(2)]
            halo, conv_step, conv_done, silu = sem("halo"), sem("conv_step"), sem("conv_done"), sem("conv_silu")

            def slot_free(eng, n):
                if n >= 2:
                    g2, i2 = divmod(n - 2, LEVELS)
                    full(eng, plan, ("gram", g2, i2 + 1))

            @block.sync
            def _(sp):
                for n in range(1, 5 if more else 4):
                    load_weights(sp, n - 1, tile_cols("gd", n, h) if n < 4 else tile_cols("hg", 0, h + 1))
                for g in range(NG):
                    freed(sp, plan, ("ty", g))
                    lo = P if g == 0 else g * GW
                    sp.dma_start(y_dram[bass.ds(h, 1), :, lo:(g + 1) * GW].rearrange("a p t -> (a p) t"),
                                 yb[g % 2][:, lo - g * GW:GW]).then_inc(y_out[g % 2], 16)
                sp.wait_ge(y_out[0], 32)
                sp.wait_ge(y_out[1], 16)

            @block.gpsimd
            def _(pool):
                for g in range(NG):
                    if g:
                        pool.wait_ge(kf_done, g)
                    pool.memset(suf[:, :], 1.0).then_inc(init, 1)
                    pool.wait_ge(fk, g + 1)
                    for i in range(LEVELS):
                        n = LEVELS * g + i
                        b = 1 << i
                        slot_free(pool, n)
                        xv_, kv_, sv_ = (halves(t, b) for t in (X[n % 2], kk, suf))
                        if i == 0:
                            pool.tensor_copy(xv_[:, :, 0, :], kv_[:, :, 0, :]).then_inc(x_even, 1)
                        else:
                            pool.wait_ge(suf_done, n)
                            pool.tensor_tensor(xv_[:, :, 0, :], kv_[:, :, 0, :], sv_[:, :, 0, :], ALU.mult
                                               ).then_inc(x_even, 1)
                        if i == 1:
                            split_low(pool, g + 1)
                    if g:
                        pool.wait_ge(ssq, g)
                        rsqrt(pool, rs[:, :], ss[:, :], EPS, eps_added, g).then_inc(rstd_s, 1)
                        full(pool, plan, ("tk", g - 1))
                    pool.wait_ge(suf_done, LEVELS * (g + 1))
                    pool.tensor_tensor(kf[:, :], kk[:, :], suf[:, :], ALU.mult).then_inc(kf_done, 1)
                if more:
                    split_low(pool, 4)
                pool.wait_ge(ssq, NG)
                rsqrt(pool, rs[:, :], ss[:, :], EPS, eps_added, NG).then_inc(rstd_s, 1)

            def take_gd(act, idx):
                j, g = divmod(idx, len(PIECES))
                t0, tw = PIECES[g]
                act.wait_ge(piece_done, idx + 1)
                src = pbank[idx % 2]
                if j < 3:
                    if idx >= 2:
                        act.wait_ge(conv_done, idx - 1)
                    if g == 0:
                        act.copy(cin[idx % 3][:, 0:CONVW - 1], zero3[:, :])
                    else:
                        act.wait_ge(halo, idx)
                    if g < len(PIECES) - 1:
                        act.copy(cin[(idx + 1) % 3][:, 0:CONVW - 1], src[:, tw - (CONVW - 1):tw])
                    act.copy(cin[idx % 3][:, CONVW - 1:CONVW - 1 + tw], src[:, 0:tw]).then_inc(halo, 1)
                    act.wait_ge(halo, idx + 1)
                    act.sem_inc(piece_out, 1)
                    if idx:
                        silu_piece(act, idx - 1)
                else:
                    act.activation(gz[:, PAD + t0:PAD + t0 + tw], src[:, 0:tw], ACT.Silu).then_inc(piece_out, 1)
                    if g == 0:
                        silu_piece(act, idx - 1)
                if g == len(PIECES) - 1 and j < (3 if more else 2):
                    split_high(act, j + 2)

            def silu_piece(act, idx):
                j, g = divmod(idx, len(PIECES))
                t0, tw = PIECES[g]
                act.wait_ge(conv_done, idx + 1)
                act.activation((xq, xk, xv)[j][:, PAD + t0:PAD + t0 + tw], cout[idx % 2][:, 0:tw],
                               ACT.Silu).then_inc(silu, 1)

            @block.scalar
            def _(act):
                def take(key):
                    for idx in pieces(parts[key]):
                        take_gd(act, idx)

                def squares(g):
                    o = full(act, plan, ("o", g))
                    for i in range(GC):
                        last = act.activation(sq[:, chunk(i)], o[:, chunk(i)], ACT.Square,
                                              scale=float(P) ** -0.5, accum_out=ss[:, i:i + 1])
                    last.then_inc(ssq, 1)

                def normalise(g):
                    act.wait_ge(rstd_s, g + 1)
                    o = bank[RING - 1]
                    for i in range(GC):
                        last = act.activation(on[:, chunk(i)], o[:, chunk(i)], ACT.Copy, scale=rs[:, i:i + 1])
                    last.then_inc(bank_free(plan, ("o", g)), 1)

                split_high(act, 1)
                take(("lead",))
                for g in range(NG):
                    for m in range(LEVELS + 1):
                        take(("gram", g, m))
                        if g and m in (2, 4, 6):
                            take(("rec", g - 1, m // 2 - 1))
                        if g and m == 6:
                            squares(g - 1)
                    if g:
                        normalise(g - 1)
                        take(("ty", g - 1))
                    act.copy(vtok[:, :], full(act, plan, ("tv", g))[:, 0:GW]).then_inc(bank_free(plan, ("tv", g)), 1)
                    act.copy(ktok[:, :], full(act, plan, ("tk", g))[:, 0:GW]).then_inc(bank_free(plan, ("tk", g)), 1)
                    take(("t", g))
                for i in range(GC):
                    take(("rec", NG - 1, i))
                squares(NG - 1)
                take(("end",))
                normalise(NG - 1)

            @block.vector
            def _(dve):
                dve.tensor_copy(fc[:, 0:2], f_ab[:, :, bass.ds(h, 1)].rearrange("p a b -> p (a b)")).then_inc(par, 1)
                dve.tensor_copy(cw[:, :, :], prm[:, 0:3 * CONVW * HEADS].rearrange("p (j y h) -> p j y h", j=CONVW, y=3)[
                    :, :, :, bass.ds(h, 1)].rearrange("p j y h -> p j (y h)")).then_inc(par, 1)
                dve.wait_ge(par, 2)
                dve.tensor_scalar(fc[:, 2:3], fc[:, 1:2], -1.0, None, ALU.mult).then_inc(par, 1)
                dve.wait_ge(par, 3)

                def start(g):
                    gs = slice(g * GW, (g + 1) * GW)
                    if g:
                        dve.wait_ge(kf_done, g)
                        dve.wait_ge(qf_done, g)
                        dve.wait_ge(tot_set, g)
                    dve.tensor_scalar(kk[:, :], hth[:, gs], fc[:, 2:3], fc[:, 1:2], ALU.mult, ALU.add).then_inc(fk, 1)
                    dve.tensor_scalar(pre[:, :], hth[:, gs], fc[:, 1:2], fc[:, 0:1], ALU.mult, ALU.add).then_inc(par, 1)
                    dve.wait_ge(par, 4 + g)

                def level(g, i):
                    b = 1 << i
                    n = LEVELS * g + i
                    slot_free(dve, n)
                    if i:
                        dve.wait_ge(pre_done, n)
                    qv_ = hq[:, g * GW:(g + 1) * GW].rearrange("p (n two b) -> p n two b", two=2, b=b)
                    xv_, pv_, sv_ = (halves(t, b) for t in (X[n % 2], pre, suf))
                    last_of = lambda half: pv_[:, :, half, b - 1:b].broadcast_to([P, GW // (2 * b), b])
                    dve.tensor_tensor(xv_[:, :, 1, :], qv_[:, :, 1, :], pv_[:, :, 1, :], ALU.mult).then_inc(x_odd, 1)
                    if i == 0:
                        dve.wait_ge(init, g + 1)
                    dve.wait_ge(x_even, n + 1)
                    dve.tensor_tensor(sv_[:, :, 0, :], sv_[:, :, 0, :], last_of(1), ALU.mult).then_inc(suf_done, 1)
                    dve.wait_ge(x_odd, n + 1)
                    dve.wait_ge(suf_done, n + 1)
                    dve.tensor_tensor(pv_[:, :, 1, :], pv_[:, :, 1, :], last_of(0), ALU.mult).then_inc(pre_done, 1)

                def merge(g, m):
                    if m:
                        freed(dve, plan, ("gram", g, m - 1))
                    src = full(dve, plan, ("gram", g, m))[:, 0:GW].rearrange("p (c t) -> p c t", c=GC)
                    dve.copy_predicated(A[g % 2][:, :, :], mask_st[:, m, :].unsqueeze(1).broadcast_to([P, GC, P]), src
                                        ).then_inc(bank_free(plan, ("gram", g, m)), 1)

                def update_state(g, i):
                    src = full(dve, plan, ("kv", g, i))
                    dve.scalar_tensor_tensor(out=S[:, :], in0=S[:, :], scalar=tot[g % 2][:, i:i + 1], in1=src[:, 0:P],
                                             op0=ALU.mult, op1=ALU.add).then_inc(bank_free(plan, ("kv", g, i)), 1)

                def gate(g):
                    src = full(dve, plan, ("ty", g))
                    if g >= 2:
                        dve.wait_ge(y_out[g % 2], 16)
                    dve.scalar_tensor_tensor(out=yb[g % 2][:, :], in0=src[:, 0:GW],
                                             scalar=prm[:, PRM_HGN:PRM_HGN + 1], in1=hz[:, g * GW:(g + 1) * GW],
                                             op0=ALU.mult, op1=ALU.mult).then_inc(bank_free(plan, ("ty", g)), 1)

                def convolve(idx):
                    j, g = divmod(idx, len(PIECES))
                    tw = PIECES[g][1]
                    dve.wait_ge(halo, idx + 1)
                    if idx >= 2:
                        dve.wait_ge(silu, idx - 1)
                    out_ = cout[idx % 2][:, 0:tw]
                    dve.tensor_scalar(out_, cin[idx % 3][:, 0:tw], cw[:, 0, j:j + 1], None, ALU.mult).then_inc(conv_step, 1)
                    for tap in range(1, CONVW):
                        dve.wait_ge(conv_step, (CONVW - 1) * idx + tap)
                        last = dve.scalar_tensor_tensor(out=out_, in0=cin[idx % 3][:, tap:tap + tw], scalar=cw[:, tap, j:j + 1],
                                                        in1=out_, op0=ALU.mult, op1=ALU.add)
                        last.then_inc(conv_step if tap < CONVW - 1 else conv_done, 1)

                def follow(key):
                    n = steps.index(key)
                    if n >= 2:
                        for idx in pieces(parts[steps[n - 2]]):
                            if idx < 3 * len(PIECES):
                                convolve(idx)

                start(0)
                for a in A:
                    dve.memset(a[:, :, :], 0.0)
                dve.memset(S[:, :], 0.0).then_inc(init, 1)
                for g in range(NG):
                    if g:
                        start(g)
                    for i in range(LEVELS):
                        level(g, i)
                        if g == 0 and i == 0:
                            for t in (xq, xk, xv):
                                dve.memset(t[:, 0:PAD], 0.0)
                        merge(g, i)
                        follow(("gram", g, i))
                        if g and i in (2, 4, 6):
                            update_state(g - 1, i // 2 - 1)
                            follow(("rec", g - 1, i // 2 - 1))
                    dve.wait_ge(pre_done, LEVELS * (g + 1))
                    dve.tensor_tensor(qf[:, :], hq[:, g * GW:(g + 1) * GW], pre[:, :], ALU.mult).then_inc(qf_done, 1)
                    dve.tensor_copy(tot[g % 2][:, :], pre[:, P - 1:GW:P]).then_inc(tot_set, 1)
                    merge(g, LEVELS)
                    follow(("gram", g, LEVELS))
                    if g:
                        gate(g - 1)
                        follow(("ty", g - 1))
                    dve.wait_ge(tot_set, g + 1)
                    follow(("t", g))
                for i in range(GC):
                    update_state(NG - 1, i)
                    follow(("rec", NG - 1, i))
                follow(("end",))
                for key in steps[-2:]:
                    for idx in pieces(parts[key]):
                        if idx < 3 * len(PIECES):
                            convolve(idx)
                gate(NG - 1)

            @block.tensor
            def _(pe):
                def project(key):
                    for n in parts[key]:
                        project_part(pe, n)

                def step_rec(g, i):
                    if i == 0:
                        freed(pe, plan, ("gram", g, LEVELS))
                        freed(pe, plan, ("tv", g))
                        freed(pe, plan, ("tk", g))
                        pe.wait_ge(qf_done, g + 1)
                        if g == 0:
                            pe.wait_ge(init, 2)
                        else:
                            freed(pe, plan, ("o", g - 1))
                    if g or i:
                        g1, i1 = divmod(GC * g + i - 1, GC)
                        freed(pe, plan, ("kv", g1, i1))
                    o, o_done = bank[RING - 1], mix_full[RING - 1]
                    pe.matmul(o[:, chunk(i)], A[g % 2][:, i, :], vtok[:, chunk(i)], start=True, stop=False)
                    last = pe.matmul(o[:, chunk(i)], qf[:, chunk(i)], S[:, :], start=False, stop=True)
                    if i == GC - 1:
                        last.then_inc(o_done, 1)
                    ap, done = take(pe, plan, ("kv", g, i))
                    pe.matmul(ap[:, 0:P], ktok[:, chunk(i)], vtok[:, chunk(i)], start=True, stop=True).then_inc(done, 1)
                    project(("rec", g, i))

                def turn(name, g, src):
                    ap, done = take(pe, plan, (name, g))
                    for i in range(GC):
                        last = pe.transpose(ap[:, chunk(i)], src(i), ident[:, :])
                    last.then_inc(done, 1)

                project(("lead",))
                for g in range(NG):
                    for m in range(LEVELS + 1):
                        ap, done = take(pe, plan, ("gram", g, m))
                        if m == 0:
                            pe.wait_ge(fk, g + 1)
                        else:
                            pe.wait_ge(x_even, LEVELS * g + m)
                            pe.wait_ge(x_odd, LEVELS * g + m)
                        for i in range(GC):
                            if m == 0:
                                left, right = kk[:, chunk(i)], hq[:, g * GW + i * P:g * GW + (i + 1) * P]
                            else:
                                left = right = X[(LEVELS * g + m - 1) % 2][:, chunk(i)]
                            last = pe.matmul(ap[:, chunk(i)], left, right, start=True, stop=True)
                        last.then_inc(done, 1)
                        project(("gram", g, m))
                        if g and m in (2, 4, 6):
                            step_rec(g - 1, m // 2 - 1)
                    if g:
                        freed(pe, plan, ("o", g - 1))
                        turn("ty", g - 1, lambda i: on[:, chunk(i)])
                        project(("ty", g - 1))
                    turn("tv", g, lambda i: hv[:, g * GW + i * P:g * GW + (i + 1) * P])
                    pe.wait_ge(kf_done, g + 1)
                    turn("tk", g, lambda i: kf[:, chunk(i)])
                    project(("t", g))
                for i in range(GC):
                    step_rec(NG - 1, i)
                project(("end",))
                freed(pe, plan, ("o", NG - 1))
                turn("ty", NG - 1, lambda i: on[:, chunk(i)])
        end_block()
        st.close()

    def phase_gd(h):
        more = not (isinstance(h, int) and h == HEADS - 1)
        st = ExitStack()
        N, Y, Lt = xq, xk, xv
        M = sb("gd_m", [P, NT], F32, st)
        QK = sb("gd_qk", [P, NT], F32, st)
        kT = sb("gd_kT", [P, NT], F32, st)
        qT = sb("gd_qT", [P, NT], F32, st)
        kd = sb("gd_kd", [P, NT], F32, st)
        vtok = sb("gd_vtok", [P, NT], F32, st)
        kn = sb("gd_kn", [P, GW], F32, st)
        qn = sb("gd_qn", [P, GW], F32, st)
        r = sb("gd_r", [P, P], F32, st)
        u = sb("gd_u", [P, P], F32, st)
        osb = [sb(f"gd_o{i}", [P, GW], F32, st) for i in range(2)]
        on = kn
        yb = [sb(f"gd_y{i}", [P, GW], F32, st) for i in range(2)]
        S = sb("gd_state", [P, P], F32, st)
        ss = sb("gd_ss", [P, 2, NC], F32, st)
        rr = sb("gd_rr", [P, 2, NC], F32, st)
        sq = [sb(f"gd_sq{i}", [P, GW], F32, st) for i in range(2)]
        cc = sb("gd_cc", [P, 5, NC], F32, st)
        names, parts, at = [], {}, 0

        def give(key, n):
            nonlocal at
            parts[key] = range(at, at + n)
            at += n

        A_ORDER = [("A1", 0), ("A1", 1), ("A2", 0), ("A3", 0), ("A1", 2), ("A2", 1), ("A3", 1), ("A2", 2), ("A3", 2)]
        for s, g in A_ORDER:
            names += [(n, g) for n in {"A1": ("tk", "tq", "tv"), "A2": ("tkn", "tqn"), "A3": ("kk", "qk")}[s]]
            give((s, g), 5 if (s, g) in (("A1", 0), ("A1", 1)) else 4)
        for i in range(LEVELS):
            names += [("Y", i, g) for g in range(NG)] + [("Z", i, g) for g in range(NG)]
            names += [("TM", i, g) for g in range(NG)] if i < LEVELS - 1 else []
            give(("B1", i), 1)
            give(("B2", i), 1)
        for c in range(NC):
            names += [("rec", c), ("U", c)]
            if c % GC == 1 and c > GC:
                names.append(("ty", c // GC - 1))
            give(("C1", c), 1)
            give(("C2", c), 1)
            give(("C3", c), 2)
        names.append(("ty", NG - 1))
        give(("end",), 8)
        assert at == PARTS * 4 * len(PIECES)
        plan = Bank(names)
        with nc.Block() as block:
            par, o_step = sem("gd_par"), sem("gd_o_step")
            ssq, rstd_s, kd_done, nm = sem("gd_ssq"), sem("gd_rstd"), sem("gd_kd_done"), sem("gd_nm")
            init, kq_done, r_done, state = sem("gd_init"), sem("gd_kq"), sem("gd_rdone"), sem("gd_state_done")
            on_done, y_out = sem("gd_on"), [sem(f"gd_y_out{i}") for i in range(2)]

            @block.sync
            def _(sp):
                if more:
                    for n in range(1, 5):
                        load_weights(sp, n - 1, tile_cols("hg", n, h + 1) if n < 4 else tile_cols("gd", 0, h + 1))
                else:
                    for n in range(KT):
                        if n >= 2:
                            sp.wait_ge(w_low, n - 1)
                        sp.dma_start(raw[n % 2][:, :, :].rearrange("p k c -> p (k c)"), w_out_v[:, n, :]
                                     ).then_inc(raw_loaded[n % 2], 16)
                for g in range(NG):
                    freed(sp, plan, ("ty", g))
                    lo = P if g == 0 else g * GW
                    sp.dma_start(y_dram[bass.ds(h + HEADS, 1), :, lo:(g + 1) * GW].rearrange("a p t -> (a p) t"),
                                 yb[g % 2][:, lo - g * GW:GW]).then_inc(y_out[g % 2], 16)
                sp.wait_ge(y_out[0], 32)
                sp.wait_ge(y_out[1], 16)

            def out_high(act, n):
                act.wait_ge(raw_loaded[n % 2], 16 * (n // 2 + 1))
                act.copy(woh[:, n, :], raw[n % 2][:, :, :].rearrange("p k c -> p (k c)")).then_inc(w_high, 1)

            def out_low(pool, n):
                pool.wait_ge(w_high, n + 1)
                pool.tensor_tensor(wol[:, n, :], raw[n % 2][:, :, :].rearrange("p k c -> p (k c)"),
                              woh[:, n, :].bitcast(F32), ALU.subtract).then_inc(w_low, 1)

            def take_hg(act, rng):
                if more:
                    for idx in pieces(rng):
                        take_piece(act, idx)

            def project(pe, rng):
                if more:
                    for n in rng:
                        project_part(pe, n)

            def scale_rows(pool, g):
                cs = slice(g * GC, (g + 1) * GC)
                pool.wait_ge(ssq, g + 1)
                rsqrt(pool, rr[:, 0, cs], ss[:, 0, cs], EPS, eps_added, 2 * g + 1)
                rsqrt(pool, rr[:, 1, cs], ss[:, 1, cs], EPS * P, eps_added, 2 * g + 2).then_inc(rstd_s, 1)
                freed(pool, plan, ("tk", g))
                k3 = lambda t: t.rearrange("p (c t) -> p c t", c=GC)
                pool.tensor_tensor(k3(kd[:, g * GW:(g + 1) * GW]), k3(kn[:, :]),
                                   cc[:, 4, cs].unsqueeze(2).broadcast_to([P, GC, P]), ALU.mult).then_inc(kd_done, 1)

            @block.gpsimd
            def _(pool):
                pool.wait_ge(par, 1)
                for g in range(NG):
                    scale_rows(pool, g)
                    if more and g == 0:
                        split_low(pool, 1)
                if more:
                    for n in range(2, 5):
                        split_low(pool, n)
                else:
                    for n in range(KT):
                        out_low(pool, n)
                for g in range(NG):
                    pool.wait_ge(ssq, NG + g + 1)
                    rsqrt(pool, rr[:, 0, 0:GC], ss[:, 0, 0:GC], EPS, eps_added, 2 * NG + g + 1).then_inc(rstd_s, 1)

            @block.scalar
            def _(act):
                def measure(g):
                    for n, (name, scale) in enumerate((("tk", 1.0), ("tq", float(P) ** 0.5))):
                        src = full(act, plan, (name, g))
                        if g:
                            act.wait_ge(ssq, g)
                        for i in range(GC):
                            last = act.activation(sq[n][:, i * P:(i + 1) * P], src[:, i * P:(i + 1) * P], ACT.Square,
                                                  scale=scale, accum_out=ss[:, n, g * GC + i:g * GC + i + 1])
                    last.then_inc(ssq, 1)
                    act.copy(vtok[:, g * GW:(g + 1) * GW], full(act, plan, ("tv", g))[:, 0:GW]
                             ).then_inc(bank_free(plan, ("tv", g)), 1)

                def turned(g):
                    for t, name in ((kT, "tkn"), (qT, "tqn")):
                        act.copy(t[:, g * GW:(g + 1) * GW], full(act, plan, (name, g))[:, 0:GW]
                                 ).then_inc(bank_free(plan, (name, g)), 1)

                if more:
                    split_high(act, 1)
                for s, g in A_ORDER:
                    if s == "A1":
                        measure(g)
                    elif s == "A2":
                        turned(g)
                    take_hg(act, parts[(s, g)])
                for i in range(LEVELS):
                    if not more:
                        out_high(act, i)
                    for g in range(NG):
                        gs = slice(g * GW, (g + 1) * GW)
                        act.copy(Y[:, gs], full(act, plan, ("Y", i, g))[:, 0:GW]).then_inc(bank_free(plan, ("Y", i, g)), 1)
                    take_hg(act, parts[("B1", i)])
                    if i < LEVELS - 1:
                        for g in range(NG):
                            gs = slice(g * GW, (g + 1) * GW)
                            act.copy(M[:, gs], full(act, plan, ("TM", i, g))[:, 0:GW]).then_inc(bank_free(plan, ("TM", i, g)), 1)
                    take_hg(act, parts[("B2", i)])
                if not more:
                    out_high(act, KT - 1)

                def squares(g):
                    freed(act, plan, ("rec", GC * g + GC - 1))
                    act.wait_ge(ssq, NG + g)
                    for i in range(GC):
                        last = act.activation(sq[0][:, i * P:(i + 1) * P], osb[g % 2][:, i * P:(i + 1) * P], ACT.Square,
                                              scale=float(P) ** -0.5, accum_out=ss[:, 0, i:i + 1])
                    last.then_inc(ssq, 1)

                def normed(g):
                    act.wait_ge(rstd_s, NG + g + 1)
                    for i in range(GC):
                        last = act.activation(on[:, i * P:(i + 1) * P], osb[g % 2][:, i * P:(i + 1) * P], ACT.Copy,
                                              scale=rr[:, 0, i:i + 1])
                    last.then_inc(on_done, 1)

                for c in range(NC):
                    take_hg(act, parts[("C1", c)])
                    act.copy(u[:, :], full(act, plan, ("U", c))[:, 0:P]).then_inc(bank_free(plan, ("U", c)), 1)
                    take_hg(act, parts[("C2", c)])
                    take_hg(act, parts[("C3", c)])
                    if c % GC == 0 and c:
                        squares(c // GC - 1)
                    if c % GC == 1 and c > GC:
                        normed(c // GC - 1)
                squares(NG - 1)
                take_hg(act, parts[("end",)])
                normed(NG - 1)

            @block.vector
            def _(dve):
                dve.tensor_copy(cc[:, :, :], cols[:, bass.ds(h, 1), :, :].rearrange("p h a c -> p (h a) c")).then_inc(par, 1)
                dve.memset(S[:, :], 0.0).then_inc(init, 1)
                dve.wait_ge(par, 1)
                step = [0]

                k3 = lambda t: t.rearrange("p (c t) -> p c t", c=GC)

                def norm(g):
                    dve.wait_ge(rstd_s, g + 1)
                    if g:
                        full(dve, plan, ("tqn", g - 1))
                        dve.wait_ge(kd_done, g)
                    for n, (t, name) in enumerate(((kn, "tk"), (qn, "tq"))):
                        dve.tensor_tensor(k3(t[:, :]), k3(full(dve, plan, (name, g))[:, 0:GW]),
                                          rr[:, n, g * GC:(g + 1) * GC].unsqueeze(2).broadcast_to([P, GC, P]),
                                          ALU.mult).then_inc(bank_free(plan, (name, g)), 1)

                def scores(g):
                    gs = slice(g * GW, (g + 1) * GW)
                    dec = DT[:, bass.ds(h, 1), gs].rearrange("p h t -> p (h t)")
                    dve.scalar_tensor_tensor(out=Lt[:, gs], in0=full(dve, plan, ("kk", g))[:, 0:GW], scalar=-1.0,
                                             in1=dec, op0=ALU.mult, op1=ALU.mult).then_inc(bank_free(plan, ("kk", g)), 1)
                    dve.tensor_tensor(QK[:, gs], full(dve, plan, ("qk", g))[:, 0:GW], dec,
                                      ALU.mult).then_inc(bank_free(plan, ("qk", g)), 1)

                norm(0)
                for g in range(NG):
                    if g + 1 < NG:
                        norm(g + 1)
                    scores(g)
                for g in range(NG):
                    gs = slice(g * GW, (g + 1) * GW)
                    for t in (N, M):
                        last = dve.tensor_tensor(k3(t[:, gs]), ident[:, :].unsqueeze(1).broadcast_to([P, GC, P]),
                                                 cc[:, 0, g * GC:(g + 1) * GC].unsqueeze(2).broadcast_to([P, GC, P]), ALU.mult)
                    last.then_inc(nm, 1)
                dve.wait_ge(nm, NG)
                for i in range(LEVELS):
                    for g in range(NG):
                        gs = slice(g * GW, (g + 1) * GW)
                        src = k3(full(dve, plan, ("Z", i, g))[:, 0:GW])
                        dst, msk = (N, mask_ts[:, min(i, LEVELS - 2), :]) if i < LEVELS - 1 else (M, mask_st[:, LEVELS, :])
                        dve.copy_predicated(k3(dst[:, gs]), msk.unsqueeze(1).broadcast_to([P, GC, P]), src
                                            ).then_inc(bank_free(plan, ("Z", i, g)), 1)

                def finish(g):
                    src = full(dve, plan, ("ty", g))
                    if g >= 2:
                        dve.wait_ge(y_out[g % 2], 16)
                    dve.scalar_tensor_tensor(out=yb[g % 2][:, :], in0=src[:, 0:GW],
                                             scalar=prm[:, PRM_GDN:PRM_GDN + 1], in1=gz[:, g * GW:(g + 1) * GW],
                                             op0=ALU.mult, op1=ALU.mult).then_inc(bank_free(plan, ("ty", g)), 1)

                for c in range(NC):
                    g, i = divmod(c, GC)
                    dve.wait_ge(kq_done, c + 1)
                    rec = bank[plan.at[("rec", c)][0]]
                    dve.scalar_tensor_tensor(out=r[:, :], in0=rec[:, 0:P], scalar=cc[:, 2, c:c + 1],
                                             in1=vtok[:, c * P:(c + 1) * P], op0=ALU.mult, op1=ALU.add).then_inc(r_done, 1)
                    full(dve, plan, ("rec", c))
                    dve.scalar_tensor_tensor(out=S[:, :], in0=S[:, :], scalar=cc[:, 3, c:c + 1],
                                             in1=rec[:, 2 * P:3 * P], op0=ALU.mult, op1=ALU.add).then_inc(state, 1)
                    dve.tensor_scalar(osb[g % 2][:, i * P:(i + 1) * P], rec[:, P:2 * P], cc[:, 1, c:c + 1], None,
                                      ALU.mult).then_inc(o_step, 1)
                    step[0] += 1
                    dve.wait_ge(o_step, step[0])
                    dve.tensor_tensor(osb[g % 2][:, i * P:(i + 1) * P], osb[g % 2][:, i * P:(i + 1) * P],
                                      rec[:, 3 * P:4 * P], ALU.add).then_inc(bank_free(plan, ("rec", c)), 1)
                    if c % GC == 2 and c > GC:
                        finish(c // GC - 1)
                finish(NG - 1)

            @block.tensor
            def _(pe):
                def three(name, g, left, right=None, wait=None):
                    ap, done = take(pe, plan, name)
                    if wait:
                        freed(pe, plan, wait)
                    for i in range(GC):
                        cs = slice(i * P, (i + 1) * P)
                        if right is None:
                            last = pe.transpose(ap[:, cs], left(i), ident[:, :])
                        else:
                            last = pe.matmul(ap[:, cs], left(i), right(i), start=True, stop=True)
                    last.then_inc(done, 1)

                full_c = lambda t, g: (lambda i: t[:, (g * GC + i) * P:(g * GC + i + 1) * P])
                part_c = lambda t: (lambda i: t[:, i * P:(i + 1) * P])
                for s, g in A_ORDER:
                    if s == "A1":
                        three(("tk", g), g, full_c(xk, g))
                        three(("tq", g), g, full_c(xq, g))
                        three(("tv", g), g, full_c(xv, g))
                    elif s == "A2":
                        three(("tkn", g), g, part_c(kn), wait=("tk", g))
                        three(("tqn", g), g, part_c(qn), wait=("tq", g))
                    else:
                        three(("kk", g), g, full_c(kT, g), full_c(kT, g), wait=("tkn", g))
                        three(("qk", g), g, full_c(kT, g), full_c(qT, g), wait=("tqn", g))
                    project(pe, parts[(s, g)])
                for i in range(LEVELS):
                    for g in range(NG):
                        if i == 0:
                            pe.wait_ge(nm, g + 1)
                        three(("Y", i, g), g, full_c(Lt, g), full_c(N, g), wait=("Z", i - 1, g) if i else ("kk", g))
                    project(pe, parts[("B1", i)])
                    for g in range(NG):
                        if i:
                            freed(pe, plan, ("TM", i - 1, g))
                        l, rt = (M, Y) if i < LEVELS - 1 else (Y, M)
                        three(("Z", i, g), g, full_c(l, g), full_c(rt, g), wait=("Y", i, g))
                    project(pe, parts[("B2", i)])
                    if i < LEVELS - 1:
                        for g in range(NG):
                            three(("TM", i, g), g, full_c(N, g), wait=("Z", i, g))
                for g in range(NG):
                    freed(pe, plan, ("Z", LEVELS - 1, g))
                pe.wait_ge(kd_done, NG)
                pe.wait_ge(init, 1)
                for c in range(NC):
                    cs = slice(c * P, (c + 1) * P)
                    rec, rec_done = take(pe, plan, ("rec", c))
                    if c:
                        pe.wait_ge(state, c)
                    pe.matmul(rec[:, 0:P], kT[:, cs], S[:, :], start=True, stop=True)
                    pe.matmul(rec[:, P:2 * P], qT[:, cs], S[:, :], start=True, stop=True).then_inc(kq_done, 1)
                    project(pe, parts[("C1", c)])
                    ap, done = take(pe, plan, ("U", c))
                    pe.wait_ge(r_done, c + 1)
                    pe.matmul(ap[:, 0:P], M[:, cs], r[:, :], start=True, stop=True).then_inc(done, 1)
                    project(pe, parts[("C2", c)])
                    freed(pe, plan, ("U", c))
                    pe.matmul(rec[:, 2 * P:3 * P], kd[:, cs], u[:, :], start=True, stop=True)
                    pe.matmul(rec[:, 3 * P:4 * P], QK[:, cs], u[:, :], start=True, stop=True).then_inc(rec_done, 1)
                    project(pe, parts[("C3", c)])
                    if c % GC == 1 and c > GC:
                        g = c // GC - 1
                        pe.wait_ge(on_done, g + 1)
                        three(("ty", g), g, part_c(on))
                project(pe, parts[("end",)])
                pe.wait_ge(on_done, NG)
                three(("ty", NG - 1), NG - 1, part_c(on))
        end_block()
        st.close()

    with nc.Fori(0, HEADS - 1) as h:
        phase_hg(h)
        phase_gd(h)
    phase_hg(HEADS - 1)
    phase_gd(HEADS - 1)

    st = ExitStack()
    yraw = [sb(f"y_raw{i}", [P, KT, P], F32, st) for i in range(2)]
    xin = [sb(f"x_in{i}", [P, D], F32, st) for i in range(2)]
    hs = [sb(f"h_sum{i}", [P, D], F32, st) for i in range(2)]
    res = [sb(f"result{i}", [P, D], F32, st) for i in range(2)]
    fw = sb("final_w", [P, D], F32, st)
    sqo = sb("square_o", [P, D], F32, st)
    mso = sb("ms_o", [P, NC], F32, st)
    rso = sb("rs_o", [P, NC], F32, st)
    TILES = SEQ // P
    with nc.Block() as block:
        fw_in, y_in, x_in2 = sem("fw_in"), [sem(f"y_in{i}") for i in range(2)], [sem(f"x_in2_{i}") for i in range(2)]
        y_high, y_low, summed, o_ss, o_rs, o_res = (sem(n) for n in ("y_high", "y_low", "summed", "o_ss", "o_rs", "o_res"))
        o_done, stored = sem("o_done"), [sem(f"stored{i}") for i in range(2)]
        obank = [bank[0], bank[1], bank[2], bank[3]]

        @block.sync
        def _(sp):
            sp.dma_start(fw[:, :], final_norm_w.rearrange("(a c) -> a c", a=1).broadcast_to([P, D])).then_inc(fw_in, 16)
            def load_tile(t):
                if t >= 2:
                    sp.wait_ge(y_low, t - 1)
                    sp.wait_ge(summed, 2 * (t - 1))
                sp.dma_start(yraw[t % 2][:, :, :], y_dram[:, :, (t + 1) * P:(t + 2) * P].rearrange("k p t -> p k t")
                             ).then_inc(y_in[t % 2], 16)
                sp.dma_start(xin[t % 2][:, :], x[0, t * P:(t + 1) * P, :]).then_inc(x_in2[t % 2], 16)

            def store_tile(t):
                sp.wait_ge(o_res, t + 1)
                sp.dma_start(out[0, t * P:(t + 1) * P, :], res[t % 2][:, :]).then_inc(stored[t % 2], 16)

            load_tile(0)
            for t in range(1, TILES):
                load_tile(t)
                if t >= 2:
                    store_tile(t - 2)
            store_tile(TILES - 2)
            store_tile(TILES - 1)
            for i in range(2):
                sp.wait_ge(stored[i], 16 * TILES // 2)

        @block.scalar
        def _(act):
            def square_tile(t):
                act.wait_ge(summed, 2 * (t + 1))
                if t:
                    act.wait_ge(o_ss, t)
                act.activation(sqo[:, :], hs[t % 2][:, :], ACT.Square, scale=float(D) ** -0.5,
                               accum_out=mso[:, t:t + 1]).then_inc(o_ss, 1)

            for t in range(TILES):
                act.wait_ge(y_in[t % 2], 16 * (t // 2 + 1))
                if t >= 2:
                    act.wait_ge(o_done, 2 * (t - 1))
                act.copy(wh[t % 2][:, :, :], yraw[t % 2][:, :, :]).then_inc(y_high, 1)
                if t:
                    square_tile(t - 1)
            square_tile(TILES - 1)

        @block.gpsimd
        def _(pool):
            def rstd_tile(t):
                pool.wait_ge(o_ss, t + 1)
                rsqrt(pool, rso[:, t:t + 1], mso[:, t:t + 1], EPS, eps_added, t + 1).then_inc(o_rs, 1)

            for t in range(TILES):
                pool.wait_ge(y_high, t + 1)
                pool.tensor_tensor(wl[t % 2][:, :, :], yraw[t % 2][:, :, :],
                              wh[t % 2][:, :, :].bitcast(F32), ALU.subtract).then_inc(y_low, 1)
                if t:
                    rstd_tile(t - 1)
            rstd_tile(TILES - 1)

        @block.tensor
        def _(pe):
            for t in range(TILES):
                pe.wait_ge(y_low, t + 1)
                for half in range(2):
                    n = 2 * t + half
                    if n >= 4:
                        pe.wait_ge(summed, n - 3)
                    for k in range(KT):
                        for i, (y, w) in enumerate(((wh, woh), (wh, wol), (wl, woh))):
                            last = pe.matmul(obank[n % 4][:, :], y[t % 2][:, k, :], w[:, k, half * 512:(half + 1) * 512],
                                             start=(k == 0 and i == 0), stop=(k == KT - 1 and i == 2))
                    last.then_inc(o_done, 1)

        @block.vector
        def _(dve):
            def result_tile(t):
                dve.wait_ge(o_rs, t + 1)
                if t >= 2:
                    dve.wait_ge(stored[t % 2], 16 * (t // 2))
                dve.scalar_tensor_tensor(out=res[t % 2][:, :], in0=hs[t % 2][:, :], scalar=rso[:, t:t + 1],
                                         in1=fw[:, :], op0=ALU.mult, op1=ALU.mult).then_inc(o_res, 1)

            dve.wait_ge(fw_in, 16)
            for t in range(TILES):
                dve.wait_ge(x_in2[t % 2], 16 * (t // 2 + 1))
                for half in range(2):
                    n = 2 * t + half
                    cs = slice(half * 512, (half + 1) * 512)
                    if t >= 2:
                        dve.wait_ge(o_res, t - 1)
                    dve.wait_ge(o_done, n + 1)
                    dve.tensor_tensor(hs[t % 2][:, cs], obank[n % 4][:, :], xin[t % 2][:, cs], ALU.add).then_inc(summed, 1)
                if t:
                    result_tile(t - 1)
            result_tile(TILES - 1)
    end_block()
    st.close()
    ctx.close()


_INS = ["x", "meta_tokens", "norm_w", "w_in", "conv_w", "hg_lb_logits", "hg_norm_w", "gdn_A_log",
        "gdn_dt_bias", "gdn_norm_w", "w_out", "final_norm_w"]


def kernel(**inputs):
    import numpy as _np
    import concourse.bacc as _bacc
    from concourse import mybir as _mybir
    from concourse.bass_utils import run_bass_kernel_spmd as _run

    nc = _bacc.Bacc("TRN2", target_bir_lowering=False, num_devices=1)
    arrays, args = {}, []
    for name in _INS:
        a = _np.ascontiguousarray(inputs[name])
        arrays[f"in_{name}"] = a
        args.append(nc.dram_tensor(f"in_{name}", a.shape, _mybir.dt.from_np(a.dtype), kind="ExternalInput").ap())
    args.append(nc.dram_tensor("out_y", (1, SEQ, D), F32, kind="ExternalOutput").ap())
    hybrid_layer(nc, *args)
    r = _run(nc, [arrays], core_ids=[0])
    return r.results[0]["out_y"]
```

```python
from contextlib import ExitStack

import concourse.bass as bass
from concourse import mybir

F32 = mybir.dt.float32
F32R = mybir.dt.float32r
U8 = mybir.dt.uint8
ALU = mybir.AluOpType
ACT = mybir.ActivationFunctionType

P = 128
D = 1024
KT = D // P
HEADS = 4
META = 16
SEQ = 1024
NC = 1 + SEQ // P
NT = NC * P
PAD = P - META
TOK = NT - PAD
NG = 3
GC = NC // NG
GW = GC * P
LEVELS = 7
WIDTH = HEADS * P
GD_COLS = 4 * WIDTH
AB_COLS = 8 * WIDTH
EPS = 1e-6
PIECES = ((0, 352), (352, 352), (704, 336))
PARTS = KT
RING = 6
CONVW = 4
OUT_K = KT - 1
TILES = SEQ // P
HOLD = 4


def live(g):
    return range(1 if g == 0 else 0, GC)


def first(g):
    return live(g)[0] * P


class Bank:

    def __init__(self, names, ring=RING):
        self.at = {n: (i % ring, i // ring) for i, n in enumerate(names)}


def hybrid_layer(nc, x, meta_tokens, norm_w, w_in, conv_w, lb_logits, hg_norm_w, A_log, dt_bias,
                 gdn_norm_w, w_out, final_norm_w, out):
    ctx = ExitStack()

    used = {}

    def sb(name, shape, dt=F32, stack=ctx):
        used[name] = used.get(name, 0) + 1
        name += f"_{used[name]}" if used[name] > 1 else ""
        return stack.enter_context(nc.sbuf_tensor(name, shape, dt))

    y_dram = nc.dram_tensor("y_scratch", [2 * HEADS, P, NT], F32, kind="Internal").ap()
    sum_dram = nc.dram_tensor("sum_scratch", [HOLD, P, D], F32, kind="Internal").ap()
    w_in_v = w_in.rearrange("l (k p) c -> p (l k) c", p=P)
    w_out_v = w_out.rearrange("l (k p) c -> p (l k) c", p=P)

    uTh = sb("uTh", [P, KT * TOK], F32R)
    uTl = sb("uTl", [P, KT * TOK], F32R)
    uh = uTh[:, :].rearrange("p (k t) -> p k t", k=KT)
    ul = uTl[:, :].rearrange("p (k t) -> p k t", k=KT)
    woh = uTh[:, 0:KT * D].rearrange("p (k c) -> p k c", k=KT)
    wol = uTl[:, 0:KT * D].rearrange("p (k c) -> p k c", k=KT)
    raw = [sb(f"w_raw{i}", [P, KT, P]) for i in range(2)]
    wh = [sb(f"w_high{i}", [P, KT, P], F32R) for i in range(2)]
    wl = [sb(f"w_low{i}", [P, KT, P], F32R) for i in range(2)]
    hq, hth, hv, hz = (sb(n, [P, NT]) for n in ("hg_q", "hg_th", "hg_v", "hg_z"))
    xq, xk, xv = (sb(n, [P, NT]) for n in ("gd_xq", "gd_xk", "gd_xv"))
    gz = sb("gd_z", [P, NT])
    held = (hq, hth, hv, hz)
    DT = sb("decay", [P, HEADS, NT])
    cols = sb("gate_cols", [P, HEADS, 7, NC])
    ident = sb("ident", [P, P])
    tri = sb("tri", [P, P])
    mask_st = sb("mask_st", [P, LEVELS + 1, P], U8)
    mask_ts = sb("mask_ts", [P, LEVELS - 1, P], U8)
    prm = sb("prm_t", [P, 66])
    f_ab = sb("f_ab", [P, 2, HEADS])
    zero3 = sb("zero3", [P, CONVW - 1])
    neg_half = sb("neg_half", [P, 1])
    y_last = {n: sb(f"y_last_{n}", [P, GW]) for n in ("hg", "gd")}
    bank = [ctx.enter_context(nc.psum_tensor(f"mix{i}", [P, 512], F32)) for i in range(RING)]
    pbank = [ctx.enter_context(nc.psum_tensor(f"proj{i}", [P, 512], F32)) for i in range(2)]
    PRM_NORM, PRM_LB, PRM_HGN, PRM_GDN = 48, 56, 64, 65

    sems = {}

    def sem(name):
        if name not in sems:
            sems[name] = ctx.enter_context(nc.semaphore(name))
        return sems[name]

    mix_full = [sem(f"mix_full{i}") for i in range(RING)]
    mix_free = [sem(f"mix_free{i}") for i in range(RING)]
    raw_loaded = [sem(f"raw_loaded{i}") for i in range(2)]
    w_high, w_low = sem("w_high"), sem("w_low")
    last_stored = sem("last_stored")
    piece_done = sem("piece_done")
    piece_out = sem("piece_out")

    def rsqrt(pool, dst, src, eps, added, n):
        pool.tensor_scalar(src, src, eps, None, ALU.add).then_inc(added, 1)
        pool.wait_ge(added, n)
        return pool.tensor_tensor(dst, src, neg_half[:, 0:1].broadcast_to([P, dst.shape[-1]]), ALU.pow)

    def end_block():
        nc.all_engine_barrier()
        lo = min(s.num for s in sems.values())
        hi = max(s.num for s in sems.values())
        nc.sync.sem_clear(range(lo, hi + 1))
        nc.all_engine_barrier()

    def y_rows(row, lo, hi):
        return y_dram[bass.ds(row, 1), :, lo:hi].rearrange("a p t -> (a p) t")

    def store_y(sp, plan, g, row, yb, y_out):
        freed(sp, plan, ("ty", g))
        sp.dma_start(y_rows(row, g * GW + first(g), (g + 1) * GW), yb[g][:, first(g):GW]).then_inc(y_out[g], 16)

    def store_last(sp, kind, row):
        sp.dma_start(y_rows(row, (NG - 1) * GW, NT), y_last[kind][:, :]).then_inc(last_stored, 16)

    def full(eng, plan, name):
        b, n = plan.at[name]
        eng.wait_ge(mix_full[b], n + 1)
        return bank[b]

    def freed(eng, plan, name):
        b, n = plan.at[name]
        eng.wait_ge(mix_free[b], n + 1)

    def take(pe, plan, name):
        b, n = plan.at[name]
        if n:
            pe.wait_ge(mix_free[b], n)
        return bank[b], mix_full[b]

    def bank_free(plan, name):
        return mix_free[plan.at[name][0]]

    def load_weights(sp, n, src):
        if n >= 2:
            sp.wait_ge(w_low, n - 1)
        sp.dma_start(raw[n % 2][:, :, 0:src.shape[-1]], src).then_inc(raw_loaded[n % 2], 16)

    def project_part(pe, n):
        idx, part = divmod(n, PARTS)
        j, g = divmod(idx, len(PIECES))
        t0, tw = PIECES[g]
        acc = pbank[idx % 2]
        if part == 0:
            if j:
                pe.wait_ge(w_low, j)
            if idx >= 2:
                pe.wait_ge(piece_out, idx - 1)
        per = KT // PARTS
        for k in range(part * per, (part + 1) * per):
            for i, (w, u) in enumerate(((wh, uh), (wh, ul), (wl, uh))):
                last = pe.matmul(acc[:, 0:tw], w[j % 2][:, k, :], u[:, k, t0:t0 + tw],
                                 start=(k == 0 and i == 0), stop=(k == KT - 1 and i == 2))
        if part == PARTS - 1:
            last.then_inc(piece_done, 1)

    def split_high(act, n):
        act.wait_ge(raw_loaded[(n - 1) % 2], 16 * ((n + 1) // 2))
        if n >= 2:
            act.wait_ge(piece_done, 3 * (n - 1))
        act.copy(wh[n % 2][:, :, :], raw[(n - 1) % 2][:, :, :]).then_inc(w_high, 1)

    LOW_PARTS = 4

    def split_low(pool, n, part=None):
        ks = slice(0, KT) if part is None else slice(part * KT // LOW_PARTS, (part + 1) * KT // LOW_PARTS)
        pool.wait_ge(w_high, n)
        last = pool.tensor_tensor(wl[n % 2][:, ks, :], raw[(n - 1) % 2][:, ks, :],
                                  wh[n % 2][:, ks, :].bitcast(F32), ALU.subtract)
        if part in (None, LOW_PARTS - 1):
            last.then_inc(w_low, 1)

    def take_piece(act, idx):
        j, g = divmod(idx, len(PIECES))
        t0, tw = PIECES[g]
        act.wait_ge(piece_done, idx + 1)
        fn, scale = ((ACT.Silu, 1.0), (ACT.Tanh, 0.5), (ACT.Copy, 1.0), (ACT.Silu, 1.0))[j]
        act.activation((hq, hth, hv, hz)[j][:, PAD + t0:PAD + t0 + tw], pbank[idx % 2][:, 0:tw], fn,
                       scale=scale).then_inc(piece_out, 1)
        if g == len(PIECES) - 1 and j < 3:
            split_high(act, j + 2)

    def pieces(parts):
        return [n // PARTS for n in parts if n % PARTS == PARTS - 1]

    def tile_cols(kind, j, h):
        return w_in_v[:, :, bass.ds(h * P + j * WIDTH + (GD_COLS if kind == "gd" else 0), P)]

    s5 = ExitStack()
    ab_t = sb("ab_t", [2 * HEADS, NT], F32, s5)
    s1 = ExitStack()
    XS = 4
    xt = [sb(f"x_tile{i}", [P, D], F32, s1) for i in range(XS)]
    ut = [sb(f"u_part{i}", [P, 512], F32, s1) for i in range(3)]
    square = sb("square", [P, D], F32, s1)
    ms = sb("mean_square", [P, NC], F32, s1)
    rstd = sb("rstd", [P, NC], F32, s1)
    rows = sb("prm_rows", [P, P], F32, s1)
    lbw = sb("lb_work", [P, 6, HEADS], F32, s1)
    gate_raw = sb("gate_raw", [P, KT, 2 * HEADS], F32, s1)
    gate_h = sb("gate_high", [P, KT, 2 * HEADS], F32R, s1)
    gate_l = sb("gate_low", [P, KT, 2 * HEADS], F32R, s1)
    names = ["rows"] + [("x", i, half) for i in range(NC) for half in range(2)]
    p1 = Bank(names, 4)
    gbank = bank[4:6]
    BESIDE = {4: [("gate", 0, range(0, 5))], 5: [("gate", 0, range(5, PARTS))], 6: [("head", 0, range(0, 5))],
              7: [("head", 0, range(5, PARTS))],
              NC - 1: [("gate", 1, range(PARTS)), ("head", 1, range(PARTS)), ("gate", 2, range(PARTS))]}
    EARLY = 2
    with nc.Block() as block:
        x_in, rows_in, gate_in = [sem(f"x_in{i}") for i in range(XS)], sem("rows_in"), sem("gate_in")
        gate_high, gate_low, gate_done, gate_out = (sem(n) for n in ("gate_high", "gate_low", "gate_done", "gate_out"))
        const0, consts = sem("const0"), sem("consts")
        sq_done, rstd_done, scaled = sem("sq_done"), sem("rstd_done"), sem("scaled")
        cleared, u_high, u_low = sem("cleared"), sem("u_high"), sem("u_low")
        lb_step, lb_exp, eps_added = sem("lb_step"), sem("lb_exp"), sem("eps_added")

        @block.sync
        def _(sp):
            sp.dma_start(xt[0][0:META, :], meta_tokens).then_inc(x_in[0], 16)
            sp.wait_ge(cleared, 1)
            sp.dma_start(rows[0:48, :], conv_w.rearrange("l j (b c) -> (l j b) c", c=P)).then_inc(rows_in, 16)
            sp.dma_start(rows[48:56, :], norm_w.rearrange("l (b c) -> (l b) c", c=P)).then_inc(rows_in, 16)
            sp.dma_start(rows[56:64, :], lb_logits.rearrange("l (b c) -> (l b) c", c=P)).then_inc(rows_in, 16)
            sp.dma_start(rows[64:65, :], hg_norm_w).then_inc(rows_in, 16)
            sp.dma_start(rows[65:66, :], gdn_norm_w).then_inc(rows_in, 16)
            for i in range(1, XS):
                sp.dma_start(xt[i][:, :], x[0, (i - 1) * P:i * P, :]).then_inc(x_in[i], 16)
            sp.dma_start(gate_raw[:, :, :], w_in_v[:, :, AB_COLS:AB_COLS + 2 * HEADS]).then_inc(gate_in, 16)
            sp.dma_start(raw[1][:, :, :], tile_cols("hg", 0, 0)).then_inc(raw_loaded[1], 16)
            for i in range(XS, NC):
                full(sp, p1, ("x", i - XS, 1))
                sp.dma_start(xt[i % XS][:, :], x[0, (i - 1) * P:i * P, :]).then_inc(x_in[i % XS], 16)
                if i == XS:
                    sp.dma_start(raw[0][:, :, :], tile_cols("hg", 1, 0)).then_inc(raw_loaded[0], 16)

        def rows_of(i):
            return META if i == 0 else P

        @block.gpsimd
        def _(pool):
            pool.memset(neg_half[:, :], -0.5)
            pool.memset(ident[:, :], 0.0).then_inc(const0, 1)
            pool.memset(tri[:, :], 1.0).then_inc(const0, 1)
            pool.wait_ge(const0, 2)
            pool.affine_select(out=ident[:, :], in_=ident[:, :], compare_op=ALU.not_equal, fill=1.0,
                               base=0, pattern=[[-1, P]], channel_multiplier=1).then_inc(const0, 1)
            pool.affine_select(out=tri[:, :], in_=tri[:, :], compare_op=ALU.is_ge, fill=0.0,
                               base=0, pattern=[[1, P]], channel_multiplier=-1).then_inc(const0, 1)
            pool.wait_ge(const0, 4)
            pool.tensor_copy(mask_st[:, 0, :], ident[:, :]).then_inc(consts, 1)

            for i in range(NC):
                w = rows_of(i)
                pool.wait_ge(sq_done, i + 1)
                pool.tensor_scalar(ms[0:w, i:i + 1], ms[0:w, i:i + 1], EPS, None, ALU.add).then_inc(eps_added, 1)
                pool.wait_ge(eps_added, i + 1)
                pool.tensor_tensor(rstd[0:w, i:i + 1], ms[0:w, i:i + 1], neg_half[0:w, 0:1], ALU.pow).then_inc(rstd_done, 1)
                if i in (3, 4, 6, 7):
                    n = i // 6
                    pool.wait_ge(w_high, n + 1)
                    for k in (2 * (i % 3), 2 * (i % 3) + 1):
                        ks = slice(k * KT // LOW_PARTS, (k + 1) * KT // LOW_PARTS)
                        last = pool.tensor_tensor(wl[n][:, ks, :], raw[1 - n][:, ks, :],
                                                  wh[n][:, ks, :].bitcast(F32), ALU.subtract)
                    if i % 3:
                        last.then_inc(w_low, 1)

        def high_part(act, n):
            i, half = divmod(n, 2)
            w = rows_of(i)
            t0 = 0 if i == 0 else META + (i - 1) * P
            freed(act, p1, ("x", i, half))
            act.copy(uh[:, 4 * half:4 * half + 4, t0:t0 + w],
                     ut[n % 3][:, 0:4 * w].rearrange("p (k t) -> p k t", k=4)).then_inc(u_high, 1)

        @block.scalar
        def _(act):
            def square_tile(i):
                w = rows_of(i)
                act.wait_ge(x_in[i % XS], 16 * (i // XS + 1))
                if i:
                    act.wait_ge(sq_done, i)
                act.activation(square[0:w, :], xt[i % XS][0:w, :], ACT.Square, scale=float(D) ** -0.5,
                               accum_out=ms[0:w, i:i + 1]).then_inc(sq_done, 1)

            def take_beside(i):
                for kind, g, part in BESIDE.get(i, []):
                    if PARTS - 1 not in part:
                        continue
                    if kind == "head":
                        take_piece(act, g)
                    else:
                        t0, tw = PIECES[g]
                        act.wait_ge(gate_done, g + 1)
                        act.copy(ab_t[:, PAD + t0:PAD + t0 + tw], gbank[g % 2][0:2 * HEADS, 0:tw]).then_inc(gate_out, 1)

            square_tile(0)
            for i in range(NC):
                if i + 1 < NC:
                    square_tile(i + 1)
                if i == 0:
                    act.wait_ge(lb_step, 2)
                    act.activation(lbw[:, 1:3, :], lbw[:, 3:5, :], ACT.Exp).then_inc(lb_exp, 1)
                if i == 1:
                    act.wait_ge(gate_in, 16)
                    act.copy(gate_h[:, :, :], gate_raw[:, :, :]).then_inc(gate_high, 1)
                if i in (3, 6):
                    act.wait_ge(raw_loaded[1 - i // 6], 16)
                    act.copy(wh[i // 6][:, :, :], raw[1 - i // 6][:, :, :]).then_inc(w_high, 1)
                if i >= 1:
                    for half in range(2):
                        high_part(act, 2 * (i - 1) + half)
                    take_beside(i - 2)
            for half in range(2):
                high_part(act, 2 * (NC - 1) + half)
            take_beside(NC - 2)
            take_beside(NC - 1)

        def low_part(dve, n):
            i, half = divmod(n, 2)
            w = rows_of(i)
            t0 = 0 if i == 0 else META + (i - 1) * P
            dve.wait_ge(u_high, n + 1)
            dve.tensor_tensor(ul[:, 4 * half:4 * half + 4, t0:t0 + w],
                              ut[n % 3][:, 0:4 * w].rearrange("p (k t) -> p k t", k=4),
                              uh[:, 4 * half:4 * half + 4, t0:t0 + w].bitcast(F32),
                              ALU.subtract).then_inc(u_low, 1)

        def norm_part(dve, n):
            i, half = divmod(n, 2)
            w = rows_of(i)
            src = full(dve, p1, ("x", i, half))[:, :].rearrange("p (k t) -> p k t", k=4)[:, :, 0:w]
            nw = prm[:, PRM_NORM + 4 * half:PRM_NORM + 4 * half + 4].unsqueeze(2).broadcast_to([P, 4, w])
            if n >= 3:
                dve.wait_ge(u_low, n - 2)
            dve.tensor_tensor(ut[n % 3][:, 0:4 * w].rearrange("p (k t) -> p k t", k=4), src, nw,
                              ALU.mult).then_inc(bank_free(p1, ("x", i, half)), 1)

        @block.vector
        def _(dve):
            dve.memset(rows[:, :], 0.0).then_inc(cleared, 1)
            for t in (hq, hv, hz, gz):
                dve.memset(t[:, 0:PAD], 0.0)
            dve.memset(hth[:, 0:PAD], 1.0)
            dve.memset(zero3[:, :], 0.0)
            dve.memset(ab_t[:, 0:PAD], 0.0)
            full(dve, p1, "rows")
            dve.tensor_copy(prm[:, :], bank[0][:, 0:66]).then_inc(mix_free[0], 1)
            freed(dve, p1, "rows")
            lg = prm[:, PRM_LB:PRM_LB + 8].rearrange("p (l h) -> p l h", l=2)
            dve.tensor_tensor(lbw[:, 0, :], lg[:, 0, :], lg[:, 1, :], ALU.max).then_inc(lb_step, 1)
            dve.wait_ge(lb_step, 1)
            dve.tensor_tensor(lbw[:, 3:5, :], lg, lbw[:, 0:1, :].broadcast_to([P, 2, HEADS]), ALU.subtract).then_inc(lb_step, 1)
            dve.wait_ge(lb_exp, 1)
            dve.tensor_tensor(lbw[:, 5, :], lbw[:, 1, :], lbw[:, 2, :], ALU.add).then_inc(lb_step, 1)
            dve.wait_ge(lb_step, 3)
            dve.reciprocal(lbw[:, 0, :], lbw[:, 5, :]).then_inc(lb_step, 1)
            dve.wait_ge(lb_step, 4)
            dve.tensor_tensor(lbw[:, 3, :], lbw[:, 1, :], lbw[:, 0, :], ALU.mult)
            dve.tensor_tensor(lbw[:, 4, :], lbw[:, 2, :], lbw[:, 0, :], ALU.mult).then_inc(lb_step, 1)
            dve.wait_ge(lb_step, 5)
            dve.tensor_scalar(f_ab[:, 1, :], lbw[:, 4, :], 0.5, None, ALU.mult)
            dve.scalar_tensor_tensor(out=f_ab[:, 0, :], in0=lbw[:, 4, :], scalar=0.5, in1=lbw[:, 3, :],
                                     op0=ALU.mult, op1=ALU.add)
            def scale_tile(i):
                w = rows_of(i)
                dve.wait_ge(sq_done, i + 1)
                dve.wait_ge(rstd_done, i + 1)
                dve.tensor_scalar(xt[i % XS][0:w, :], xt[i % XS][0:w, :], rstd[0:w, i:i + 1], None,
                                  ALU.mult).then_inc(scaled, 1)

            scale_tile(0)
            for n in range(2 * NC):
                if n % 2 == 0 and n // 2 + 1 < NC:
                    scale_tile(n // 2 + 1)
                norm_part(dve, n)
                if n:
                    low_part(dve, n - 1)
                if n == 3:
                    dve.wait_ge(gate_high, 1)
                    dve.tensor_tensor(gate_l[:, :, :], gate_raw[:, :, :], gate_h[:, :, :].bitcast(F32),
                                      ALU.subtract).then_inc(gate_low, 1)
            low_part(dve, 2 * NC - 1)

        @block.tensor
        def _(pe):
            pe.wait_ge(rows_in, 80)
            pe.wait_ge(const0, 4)
            ap, done = take(pe, p1, "rows")
            pe.transpose(ap[:, 0:P], rows[:, :], ident[:, :]).then_inc(done, 1)
            for i in range(NC):
                w = rows_of(i)
                pe.wait_ge(scaled, i + 1)
                for half in range(2):
                    ap, done = take(pe, p1, ("x", i, half))
                    for k in range(4):
                        c0 = (4 * half + k) * P
                        last = pe.transpose(ap[:, k * P:k * P + w], xt[i % XS][0:w, c0:c0 + P], ident[0:w, 0:w])
                    last.then_inc(done, 1)
                for kind, g, part in BESIDE.get(i, []):
                    t0, tw = PIECES[g]
                    pe.wait_ge(u_low, 2 * (1 + -(-(t0 + tw - META) // P)))
                    if kind == "head":
                        pe.wait_ge(w_low, 1)
                        for k in part:
                            project_part(pe, g * PARTS + k)
                        continue
                    pe.wait_ge(gate_low, 1)
                    if g >= 2:
                        pe.wait_ge(gate_out, g - 1)
                    for k in part:
                        for n, (wt, u) in enumerate(((gate_h, uh), (gate_h, ul), (gate_l, uh))):
                            last = pe.matmul(gbank[g % 2][0:2 * HEADS, 0:tw], wt[:, k, :], u[:, k, t0:t0 + tw],
                                             start=(k == 0 and n == 0), stop=(k == KT - 1 and n == 2))
                    if PARTS - 1 in part:
                        last.then_inc(gate_done, 1)
    end_block()
    s1.close()

    s2 = ExitStack()
    ab = sb("ab", [P, NC, 2 * HEADS], F32, s2)
    pr = sb("gate_prm", [P, 2, HEADS], F32, s2)
    ea = sb("exp_a", [P, HEADS], F32, s2)
    gw = sb("gate_work", [P, 6, HEADS, NC], F32, s2)
    g_in = sb("g_in", [P, HEADS, NC], F32, s2)
    gam = sb("gamma", [P, HEADS, NC], F32, s2)
    rep = sb("g_rep", [P, 2, GC, P], F32, s2)
    dtmp = sb("decay_tmp", [P, 2, GW], F32, s2)
    ones = sb("ones", [P, P], F32, s2)
    mwork = sb("mask_work", [P, 2 * LEVELS, P], F32, s2)
    pmask = sb("pad_mask", [P, 1], F32, s2)
    shifts = sb("shifts", [P, 2, P], F32, s2)
    sw = sb("shift_work", [P, 3, HEADS, NC], F32, s2)
    p2_names = [("ab", g) for g in range(NG)] + ["gam", "tot"] + [("dec", n) for n in range(HEADS * NG)]
    p2_names.insert(p2_names.index(("dec", 2)), "down")
    p2_names.insert(p2_names.index(("dec", 4)), "up")
    p2 = Bank(p2_names)
    P2_PARTS, at = {}, EARLY * PARTS
    for key in [("ab", 0), ("gam", 0)] + [("dec", n) for n in range(HEADS * NG)]:
        n = {"ab": 20, "gam": 4, "dec": 5 if key[1] < 8 else 4}[key[0]]
        P2_PARTS[key] = range(at, at + n)
        at += n
    assert at == PARTS * 4 * len(PIECES)
    with nc.Block() as block:
        prm_in, shift_set, shift_step = sem("prm_in"), sem("shift_set"), sem("shift_step")
        ones_set, pm0, gate_step, mask_step, mask_set = sem("ones_set"), sem("pm0"), sem("gate_step"), sem("mask_step"), sem("mask_set")
        gate_exp, gate_rep, dec_exp = (sem(n) for n in
                                                         ("gate_exp", "gate_rep", "dec_exp"))

        @block.sync
        def _(sp):
            sp.dma_start(pr[:, 0, :], A_log[0:1, :].broadcast_to([P, HEADS])).then_inc(prm_in, 16)
            sp.dma_start(pr[:, 1, :], dt_bias[0:1, :].broadcast_to([P, HEADS])).then_inc(prm_in, 16)
            sp.sem_inc(piece_done, EARLY)
            sp.sem_inc(piece_out, EARLY)
            sp.sem_inc(raw_loaded[0], 16)
            sp.sem_inc(w_high, 1)
            sp.sem_inc(w_low, 1)
            for n in range(2, 5):
                load_weights(sp, n - 1, tile_cols("hg", n, 0) if n < 4 else tile_cols("gd", 0, 0))

        @block.gpsimd
        def _(pool):
            pool.memset(ones[:, :], 1.0).then_inc(ones_set, 1)
            pool.memset(shifts[:, :, :], 0.0).then_inc(shift_set, 1)
            pool.wait_ge(shift_set, 1)
            for i, base in enumerate((1, -1)):
                pool.affine_select(out=shifts[:, i, :], in_=shifts[:, i, :], compare_op=ALU.not_equal, fill=1.0,
                                   base=base, pattern=[[-1, P]], channel_multiplier=1).then_inc(shift_set, 1)
            pool.memset(pmask[:, :], 1.0).then_inc(pm0, 1)
            pool.wait_ge(pm0, 1)
            pool.affine_select(out=pmask[:, :], in_=pmask[:, :], compare_op=ALU.is_ge, fill=0.0,
                               base=-PAD, pattern=[[1, 1]], channel_multiplier=1).then_inc(pm0, 1)

            def replicate(n):
                h, g = divmod(n, NG)
                if n >= 2:
                    full(pool, p2, ("dec", n - 2))
                pool.tensor_copy(rep[:, n % 2, :, :],
                                 g_in[:, h, g * GC:(g + 1) * GC].unsqueeze(2).broadcast_to([P, GC, P])).then_inc(gate_rep, 1)

            def level_masks(i):
                b = 1 << i
                groups = P // (2 * b)
                for cut in range(2):
                    sign = 1 - 2 * cut
                    v = mwork[:, i, :].rearrange("p (n two b) -> p n two b", two=2, b=b)[:, :, 1, :]
                    pool.affine_select(out=v, in_=v, compare_op=ALU.is_ge, fill=0.0, base=(b - 1) * cut,
                                       pattern=[[-2 * b * sign, groups], [0, b]], channel_multiplier=sign)
                    v = mwork[:, LEVELS + i, :].rearrange("p (n two b) -> p n two b", two=2, b=b)[:, :, 0, :]
                    pool.affine_select(out=v, in_=v, compare_op=ALU.is_ge, fill=0.0,
                                       base=(2 * b - 1) * cut - b * (1 - cut),
                                       pattern=[[-2 * b * sign, groups], [0, b]], channel_multiplier=sign
                                       ).then_inc(mask_step, 1)
                    pool.wait_ge(mask_step, 2 * i + 1 + cut)

            pool.wait_ge(mask_set, 2)
            level_masks(0)
            level_masks(1)
            pool.wait_ge(gate_step, 9)
            replicate(0)
            replicate(1)
            for n in range(HEADS * NG):
                if n in (1, 5):
                    split_low(pool, 2 + n // 4)
                if n + 2 < HEADS * NG:
                    replicate(n + 2)
                if n + 2 < LEVELS:
                    level_masks(n + 2)
            split_low(pool, 4)

        @block.scalar
        def _(act):
            act.wait_ge(prm_in, 32)
            act.activation(ea[:, :], pr[:, 0, :], ACT.Exp).then_inc(gate_exp, 1)
            act.wait_ge(gate_step, 3)
            act.activation(gw[:, 3:5, :, :], gw[:, 1:3, :, :], ACT.Exp).then_inc(gate_exp, 1)
            act.wait_ge(gate_exp, 2)
            act.activation(gw[:, 5, :, :], gw[:, 3, :, :], ACT.Ln, bias=1.0).then_inc(gate_exp, 1)
            for n in pieces(P2_PARTS[("ab", 0)]) + pieces(P2_PARTS[("gam", 0)]):
                take_piece(act, n)
            act.wait_ge(gate_step, 12)
            act.activation(sw[:, 1, :, :], g_in[:, :, :], ACT.Exp)
            act.activation(cols[:, :, 1, :], gw[:, 0, :, :], ACT.Exp)
            act.activation(cols[:, :, 3, :], gw[:, 1, :, :], ACT.Exp)
            act.activation(cols[:, :, 4, :], gw[:, 2, :, :], ACT.Exp).then_inc(gate_exp, 1)
            for n in range(HEADS * NG):
                h, g = divmod(n, NG)
                freed(act, p2, ("dec", n))
                act.activation(DT[:, h, g * GW:(g + 1) * GW], dtmp[:, n % 2, :], ACT.Exp).then_inc(dec_exp, 1)
                for m in pieces(P2_PARTS[("dec", n)]):
                    take_piece(act, m)

        def keep(dve, n):
            h, g = divmod(n, NG)
            dve.wait_ge(dec_exp, n + 1)
            d = DT[:, h, g * GW:(g + 1) * GW].rearrange("p (c t) -> p c t", c=GC)
            dve.tensor_tensor(d, d, tri[:, :].unsqueeze(1).broadcast_to([P, GC, P]), ALU.mult)

        @block.vector
        def _(dve):
            step = [0]

            def link(ins):
                step[0] += 1
                ins.then_inc(gate_step, 1)
                dve.wait_ge(gate_step, step[0])

            dve.memset(y_last["gd"][:, :], 0.0)
            dve.memset(mwork[:, :, :], 0.0).then_inc(mask_set, 1)
            dve.wait_ge(mask_set, 1)
            for i in range(LEVELS):
                b = 1 << i
                dve.memset(mwork[:, i, :].rearrange("p (n two b) -> p n two b", two=2, b=b)[:, :, 1, :], 1.0)
                last = dve.memset(mwork[:, LEVELS + i, :].rearrange("p (n two b) -> p n two b", two=2, b=b)[:, :, 0, :], 1.0)
            last.then_inc(mask_set, 1)
            for g in range(NG):
                src = full(dve, p2, ("ab", g))[:, 0:GW].rearrange("p (c t) -> p c t", c=GC)[:, :, 0:2 * HEADS]
                dve.tensor_copy(ab[:, g * GC:(g + 1) * GC, :], src).then_inc(bank_free(p2, ("ab", g)), 1)
            for g in range(NG):
                freed(dve, p2, ("ab", g))
            dve.wait_ge(prm_in, 32)
            av = ab[:, :, 0:HEADS].rearrange("p c h -> p h c")
            bv = ab[:, :, HEADS:2 * HEADS].rearrange("p c h -> p h c")
            link(dve.tensor_tensor(gw[:, 0, :, :], av, pr[:, 1, :].unsqueeze(2).broadcast_to([P, HEADS, NC]), ALU.add))
            link(dve.scalar_tensor_tensor(out=gw[:, 1, :, :], in0=gw[:, 0, :, :], scalar=-1.0,
                                          in1=gw[:, 0, :, :], op0=ALU.mult, op1=ALU.min))
            link(dve.tensor_scalar(gw[:, 2, :, :], bv, -1.0, None, ALU.mult))
            dve.wait_ge(gate_exp, 3)
            link(dve.scalar_tensor_tensor(out=gw[:, 0, :, :], in0=gw[:, 0, :, :], scalar=0.0,
                                          in1=gw[:, 5, :, :], op0=ALU.max, op1=ALU.add))
            link(dve.scalar_tensor_tensor(out=g_in[:, :, :], in0=gw[:, 0, :, :], scalar=-1.0,
                                          in1=ea[:, :].unsqueeze(2).broadcast_to([P, HEADS, NC]),
                                          op0=ALU.mult, op1=ALU.mult))
            link(dve.tensor_scalar(gw[:, 4, :, :], gw[:, 4, :, :], 1.0, None, ALU.add))
            link(dve.reciprocal(cols[:, :, 0, :], gw[:, 4, :, :]))
            dve.wait_ge(pm0, 2)
            link(dve.tensor_scalar(cols[:, :, 0, 0:1], cols[:, :, 0, 0:1], pmask[:, 0:1], None, ALU.mult))
            link(dve.tensor_scalar(g_in[:, :, 0:1], g_in[:, :, 0:1], pmask[:, 0:1], None, ALU.mult))

            src = full(dve, p2, "gam")[:, 0:HEADS * NC].rearrange("p (h c) -> p h c", h=HEADS)
            link(dve.tensor_copy(gam[:, :, :], src))
            tot = full(dve, p2, "tot")[:, 0:HEADS * NC].rearrange("p (h c) -> p h c", h=HEADS)
            dve.tensor_copy(gw[:, 0, :, :], gam[:, :, :])
            dve.tensor_tensor(gw[:, 2, :, :], tot, gam[:, :, :], ALU.subtract)
            link(dve.tensor_copy(gw[:, 1, :, :], tot))
            link(dve.tensor_scalar(gw[:, 2, :, :], gw[:, 2, :, :], 0.0, None, ALU.min))
            dve.engine_nop().then_inc(bank_free(p2, "gam"), 1)
            dve.engine_nop().then_inc(bank_free(p2, "tot"), 1)
            dve.wait_ge(gate_exp, 4)
            dve.tensor_scalar(cols[:, :, 2, :], cols[:, :, 1, :], -1.0, None, ALU.mult)
            dve.tensor_copy(sw[:, 0, :, :], cols[:, :, 0, :]).then_inc(shift_step, 1)
            per_head = lambda ap: ap[:, 0:HEADS * NC].rearrange("p (h c) -> p h c", h=HEADS)
            for n in range(HEADS * NG):
                h, g = divmod(n, NG)
                if n == 2:
                    dve.scalar_tensor_tensor(out=sw[:, 2, :, :], in0=per_head(full(dve, p2, "down")), scalar=-1.0,
                                             in1=sw[:, 0, :, :], op0=ALU.mult, op1=ALU.mult).then_inc(bank_free(p2, "down"), 1)
                    freed(dve, p2, "down")
                    dve.tensor_tensor(sw[:, 2, :, :], sw[:, 2, :, :], sw[:, 1, :, :], ALU.mult).then_inc(shift_step, 1)
                if n == 4:
                    dve.wait_ge(shift_step, 2)
                    dve.tensor_copy(cols[:, :, 5, :], sw[:, 2, :, :])
                    dve.tensor_copy(cols[:, :, 6, :], per_head(full(dve, p2, "up"))).then_inc(bank_free(p2, "up"), 1)
                src = full(dve, p2, ("dec", n))
                if n >= 2:
                    dve.wait_ge(dec_exp, n - 1)
                for i in range(GC):
                    c = g * GC + i
                    last = dve.tensor_scalar(dtmp[:, n % 2, i * P:(i + 1) * P], src[:, i * P:(i + 1) * P],
                                             gam[:, h, c:c + 1], 0.0, ALU.subtract, ALU.min)
                last.then_inc(bank_free(p2, ("dec", n)), 1)
                if n:
                    keep(dve, n - 1)
                if n == HEADS * NG - 3:
                    dve.wait_ge(mask_step, 2 * LEVELS)
                    dve.tensor_copy(mask_st[:, 1:LEVELS + 1, :], mwork[:, 0:LEVELS, :])
                    dve.tensor_copy(mask_ts[:, :, :], mwork[:, LEVELS:2 * LEVELS - 1, :])
            keep(dve, HEADS * NG - 1)

        @block.tensor
        def _(pe):
            for g in range(NG):
                ap, done = take(pe, p2, ("ab", g))
                for i in range(GC):
                    c = g * GC + i
                    last = pe.transpose(ap[:, i * P:i * P + 2 * HEADS], ab_t[:, c * P:(c + 1) * P],
                                        ident[0:2 * HEADS, 0:2 * HEADS])
                last.then_inc(done, 1)
            for n in P2_PARTS[("ab", 0)]:
                project_part(pe, n)
            pe.wait_ge(gate_step, 9)
            pe.wait_ge(ones_set, 1)
            g_all = g_in[:, :, :].rearrange("p h c -> p (h c)")
            ap, done = take(pe, p2, "gam")
            pe.matmul(ap[:, 0:HEADS * NC], tri[:, :], g_all, start=True, stop=True).then_inc(done, 1)
            ap, done = take(pe, p2, "tot")
            pe.matmul(ap[:, 0:HEADS * NC], ones[:, :], g_all, start=True, stop=True).then_inc(done, 1)
            for n in P2_PARTS[("gam", 0)]:
                project_part(pe, n)
            for n in range(HEADS * NG):
                pe.wait_ge(gate_rep, n + 1)
                ap, done = take(pe, p2, ("dec", n))
                for i in range(GC):
                    last = pe.matmul(ap[:, i * P:(i + 1) * P], rep[:, n % 2, i, :], tri[:, :], start=True, stop=True)
                last.then_inc(done, 1)
                for m in P2_PARTS[("dec", n)]:
                    project_part(pe, m)
                if n in (1, 3):
                    ap, done = take(pe, p2, "down" if n == 1 else "up")
                    pe.wait_ge(shift_set, 3)
                    pe.wait_ge(shift_step, 1 + n // 2)
                    pe.matmul(ap[:, 0:HEADS * NC], shifts[:, n // 2, :], sw[:, n - 1, :, :].rearrange("p h c -> p (h c)"),
                              start=True, stop=True).then_inc(done, 1)
    end_block()
    s2.close()
    s5.close()

    def phase_hg(h):
        more = not (isinstance(h, int) and h == HEADS - 1)
        st = ExitStack()
        pre = sb("f_prefix", [P, GW], F32, st)
        suf = sb("f_suffix", [P, GW], F32, st)
        kk = sb("hg_k", [P, GW], F32, st)
        X = [sb(f"level_x{i}", [P, GW], F32, st) for i in range(2)]
        A = [sb(f"hg_scores{i}", [P, GC, P], F32, st) for i in range(2)]
        vtok = sb("hg_vtok", [P, GW], F32, st)
        qf = [sb(f"hg_qf{i}", [P, GW], F32, st) for i in range(2)]
        kf = sb("hg_kf", [P, GW], F32, st)
        ktok = sb("hg_ktok", [P, GW], F32, st)
        on = sb("hg_on", [P, GW], F32, st)
        yb = [sb(f"hg_y{i}", [P, GW], F32, st) for i in range(2)]
        S = sb("hg_state", [P, P], F32, st)
        tot = [sb(f"hg_tot{i}", [P, GC], F32, st) for i in range(2)]
        ss = sb("hg_ss", [P, GC], F32, st)
        rs = sb("hg_rs", [P, GC], F32, st)
        sq = sb("hg_sq", [P, GW], F32, st)
        fc = sb("hg_fcur", [P, 3], F32, st)
        cw = sb("hg_taps", [P, CONVW, 3], F32, st)
        TW = PIECES[0][1]
        cin = [sb(f"conv_in{i}", [P, CONVW - 1 + TW], F32, st) for i in range(3)]
        cout = [sb(f"conv_out{i}", [P, TW], F32, st) for i in range(2)]
        steps = [("lead",)]
        names = []
        for g in range(NG):
            for m in range(LEVELS + 1):
                names.append(("gram", g, m))
                steps.append(("gram", g, m))
                if g and m in (2, 4, 6):
                    names.append(("kv", g - 1, m // 2 - 1))
                    steps.append(("rec", g - 1, m // 2 - 1))
            names += [("tv", g), ("tk", g)]
            steps.append(("t", g))
            if g:
                names.append(("ty", g - 1))
                steps.append(("ty", g - 1))
        for i in range(GC):
            names.append(("kv", NG - 1, i))
            steps.append(("rec", NG - 1, i))
        names.append(("ty", NG - 1))
        steps.append(("end",))
        parts, at = {}, 0
        for key in steps:
            n = {"lead": 4, "end": 10}.get(key[0], 4 if key[:2] == ("rec", NG - 1) else 2)
            parts[key] = range(at, at + n)
            at += n
        assert at == PARTS * 4 * len(PIECES)
        plan = Bank(names, RING - 1)
        for g in range(NG):
            plan.at[("o", g)] = (RING - 1, g)
        halves = lambda t, b: t.rearrange("p (n two b) -> p n two b", two=2, b=b)
        chunk = lambda i: slice(i * P, (i + 1) * P)
        with nc.Block() as block:
            suf_init = sem("hg_suf_init")
            init, par, fk = sem("hg_init"), sem("hg_par"), sem("hg_fk")
            suf_done, pre_done = sem("hg_suf"), sem("hg_pre")
            x_even, x_odd, kf_done, qf_done = sem("hg_x_even"), sem("hg_x_odd"), sem("hg_kf"), sem("hg_qf")
            tot_set, ssq, rstd_s = sem("hg_tot_set"), sem("hg_ssq"), sem("hg_rstd")
            y_out = [sem(f"hg_y_out{i}") for i in range(2)]
            tap0 = sem("tap0")
            halo, conv_step, conv_done, silu = sem("halo"), sem("conv_step"), sem("conv_done"), sem("conv_silu")

            def slot_free(eng, n):
                if n >= 2:
                    g2, i2 = divmod(n - 2, LEVELS)
                    full(eng, plan, ("gram", g2, i2 + 1))

            @block.sync
            def _(sp):
                for n in range(1, 5 if more else 4):
                    load_weights(sp, n - 1, tile_cols("gd", n, h) if n < 4 else tile_cols("hg", 0, h + 1))
                store_last(sp, "gd", h + HEADS - 1)
                for g in range(NG - 1):
                    store_y(sp, plan, g, h, yb, y_out)
                sp.wait_ge(last_stored, 16)
                for g in range(NG - 1):
                    sp.wait_ge(y_out[g], 16)

            @block.gpsimd
            def _(pool):
                for g in range(NG):
                    if g:
                        pool.wait_ge(kf_done, g)
                    pool.memset(suf[:, :], 1.0).then_inc(suf_init, 1)
                    pool.wait_ge(fk, g + 1)
                    pool.wait_ge(suf_init, g + 1)
                    for i in range(LEVELS):
                        n = LEVELS * g + i
                        b = 1 << i
                        slot_free(pool, n)
                        xv_, kv_, sv_ = (halves(t[:, first(g):GW], b) for t in (X[n % 2], kk, suf))
                        if i == 0:
                            pool.tensor_copy(xv_[:, :, 0, :], kv_[:, :, 0, :]).then_inc(x_even, 1)
                        else:
                            pool.wait_ge(suf_done, n)
                            pool.tensor_tensor(xv_[:, :, 0, :], kv_[:, :, 0, :], sv_[:, :, 0, :], ALU.mult
                                               ).then_inc(x_even, 1)
                        sv_, pv_ = halves(suf[:, :], b), halves(pre[:, :], b)
                        if i:
                            pool.wait_ge(pre_done, n)
                        else:
                            pool.wait_ge(par, 4 + g)
                        pool.wait_ge(x_even, n + 1)
                        pool.tensor_tensor(sv_[:, :, 0, :], sv_[:, :, 0, :],
                                           pv_[:, :, 1, b - 1:b].broadcast_to([P, GW // (2 * b), b]), ALU.mult
                                           ).then_inc(suf_done, 1)
                        if 1 <= i <= LOW_PARTS:
                            split_low(pool, g + 1, i - 1)
                    if g:
                        full(pool, plan, ("tk", g - 1))
                    pool.wait_ge(suf_done, LEVELS * (g + 1))
                    pool.tensor_tensor(kf[:, :], kk[:, :], suf[:, :], ALU.mult).then_inc(kf_done, 1)
                    if g:
                        pool.wait_ge(ssq, g)
                        i = live(g - 1)[0]
                        rsqrt(pool, rs[:, i:GC], ss[:, i:GC], EPS, eps_added, g).then_inc(rstd_s, 1)
                if more:
                    split_low(pool, 4)
                pool.wait_ge(ssq, NG)
                rsqrt(pool, rs[:, :], ss[:, :], EPS, eps_added, NG).then_inc(rstd_s, 1)

            def take_gd(act, idx):
                j, g = divmod(idx, len(PIECES))
                t0, tw = PIECES[g]
                act.wait_ge(piece_done, idx + 1)
                src = pbank[idx % 2]
                if j < 3:
                    if idx >= 2:
                        act.wait_ge(conv_done, idx - 1)
                    if g == 0:
                        act.copy(cin[idx % 3][:, 0:CONVW - 1], zero3[:, :])
                    else:
                        act.wait_ge(halo, idx)
                    if g < len(PIECES) - 1:
                        act.copy(cin[(idx + 1) % 3][:, 0:CONVW - 1], src[:, tw - (CONVW - 1):tw])
                    act.copy(cin[idx % 3][:, CONVW - 1:CONVW - 1 + tw], src[:, 0:tw]).then_inc(halo, 1)
                    act.wait_ge(halo, idx + 1)
                    act.sem_inc(piece_out, 1)
                    if idx >= 2:
                        act.wait_ge(silu, idx - 1)
                    act.activation(cout[idx % 2][:, 0:tw], cin[idx % 3][:, 0:tw], ACT.Copy,
                                   scale=cw[:, 0, j:j + 1]).then_inc(tap0, 1)
                    if idx:
                        silu_piece(act, idx - 1)
                else:
                    act.activation(gz[:, PAD + t0:PAD + t0 + tw], src[:, 0:tw], ACT.Silu).then_inc(piece_out, 1)
                    if g == 0:
                        silu_piece(act, idx - 1)
                if g == len(PIECES) - 1 and j < (3 if more else 2):
                    split_high(act, j + 2)

            def silu_piece(act, idx):
                j, g = divmod(idx, len(PIECES))
                t0, tw = PIECES[g]
                act.wait_ge(conv_done, idx + 1)
                act.activation((xq, xk, xv)[j][:, PAD + t0:PAD + t0 + tw], cout[idx % 2][:, 0:tw],
                               ACT.Silu).then_inc(silu, 1)

            @block.scalar
            def _(act):
                def take(key):
                    for idx in pieces(parts[key]):
                        take_gd(act, idx)

                def squares(g):
                    o = full(act, plan, ("o", g))
                    for i in live(g):
                        last = act.activation(sq[:, chunk(i)], o[:, chunk(i)], ACT.Square,
                                              scale=float(P) ** -0.5, accum_out=ss[:, i:i + 1])
                    last.then_inc(ssq, 1)

                def normalise(g):
                    act.wait_ge(rstd_s, g + 1)
                    o = bank[RING - 1]
                    for i in live(g):
                        last = act.activation(on[:, chunk(i)], o[:, chunk(i)], ACT.Copy, scale=rs[:, i:i + 1])
                    last.then_inc(bank_free(plan, ("o", g)), 1)

                split_high(act, 1)
                act.wait_ge(par, 2)
                take(("lead",))
                for g in range(NG):
                    for m in range(LEVELS + 1):
                        take(("gram", g, m))
                        if g and m in (2, 4, 6):
                            take(("rec", g - 1, m // 2 - 1))
                        if g and m == 6:
                            squares(g - 1)
                    act.copy(vtok[:, :], full(act, plan, ("tv", g))[:, 0:GW]).then_inc(bank_free(plan, ("tv", g)), 1)
                    act.copy(ktok[:, :], full(act, plan, ("tk", g))[:, 0:GW]).then_inc(bank_free(plan, ("tk", g)), 1)
                    if g:
                        normalise(g - 1)
                    take(("t", g))
                    if g:
                        take(("ty", g - 1))
                for i in range(GC):
                    take(("rec", NG - 1, i))
                squares(NG - 1)
                tail = pieces(parts[("end",)])
                for idx in tail[:-1]:
                    take_gd(act, idx)
                normalise(NG - 1)
                take_gd(act, tail[-1])

            @block.vector
            def _(dve):
                dve.tensor_copy(fc[:, 0:2], f_ab[:, :, bass.ds(h, 1)].rearrange("p a b -> p (a b)")).then_inc(par, 1)
                dve.tensor_copy(cw[:, :, :], prm[:, 0:3 * CONVW * HEADS].rearrange("p (j y h) -> p j y h", j=CONVW, y=3)[
                    :, :, :, bass.ds(h, 1)].rearrange("p j y h -> p j (y h)")).then_inc(par, 1)
                dve.wait_ge(par, 2)
                dve.tensor_scalar(fc[:, 2:3], fc[:, 1:2], -1.0, None, ALU.mult).then_inc(par, 1)
                dve.wait_ge(par, 3)

                def start(g):
                    gs = slice(g * GW, (g + 1) * GW)
                    if g:
                        dve.wait_ge(kf_done, g)
                        dve.wait_ge(qf_done, g)
                        dve.wait_ge(tot_set, g)
                    dve.tensor_scalar(kk[:, :], hth[:, gs], fc[:, 2:3], fc[:, 1:2], ALU.mult, ALU.add).then_inc(fk, 1)
                    dve.tensor_scalar(pre[:, :], hth[:, gs], fc[:, 1:2], fc[:, 0:1], ALU.mult, ALU.add).then_inc(par, 1)
                    dve.wait_ge(par, 4 + g)

                def level(g, i):
                    b = 1 << i
                    n = LEVELS * g + i
                    slot_free(dve, n)
                    if i:
                        dve.wait_ge(pre_done, n)
                    lo = first(g)
                    qv_ = halves(hq[:, g * GW + lo:(g + 1) * GW], b)
                    xv_, pv_ = (halves(t[:, lo:GW], b) for t in (X[n % 2], pre))
                    dve.tensor_tensor(xv_[:, :, 1, :], qv_[:, :, 1, :], pv_[:, :, 1, :], ALU.mult).then_inc(x_odd, 1)

                def extend(g, i):
                    b = 1 << i
                    n = LEVELS * g + i
                    pv_ = halves(pre[:, :], b)
                    dve.wait_ge(x_odd, n + 1)
                    dve.wait_ge(suf_done, n + 1)
                    dve.tensor_tensor(pv_[:, :, 1, :], pv_[:, :, 1, :],
                                      pv_[:, :, 0, b - 1:b].broadcast_to([P, GW // (2 * b), b]), ALU.mult).then_inc(pre_done, 1)

                def merge(g, m):
                    if g + m == 0:
                        dve.wait_ge(init, 1)
                    if m:
                        freed(dve, plan, ("gram", g, m - 1))
                    n = len(live(g))
                    src = full(dve, plan, ("gram", g, m))[:, first(g):GW].rearrange("p (c t) -> p c t", c=n)
                    dve.copy_predicated(A[g % 2][:, GC - n:GC, :], mask_st[:, m, :].unsqueeze(1).broadcast_to([P, n, P]), src
                                        ).then_inc(bank_free(plan, ("gram", g, m)), 1)

                def update_state(g, i):
                    src = full(dve, plan, ("kv", g, i))
                    dve.scalar_tensor_tensor(out=S[:, :], in0=S[:, :], scalar=tot[g % 2][:, i:i + 1], in1=src[:, 0:P],
                                             op0=ALU.mult, op1=ALU.add).then_inc(bank_free(plan, ("kv", g, i)), 1)

                def gate(g):
                    src = full(dve, plan, ("ty", g))
                    dst = y_last["hg"] if g == NG - 1 else yb[g]
                    lo = first(g)
                    dve.scalar_tensor_tensor(out=dst[:, lo:GW], in0=src[:, lo:GW],
                                             scalar=prm[:, PRM_HGN:PRM_HGN + 1], in1=hz[:, g * GW + lo:(g + 1) * GW],
                                             op0=ALU.mult, op1=ALU.mult).then_inc(bank_free(plan, ("ty", g)), 1)

                def tap_step(idx, tap):
                    j, g = divmod(idx, len(PIECES))
                    tw = PIECES[g][1]
                    out_ = cout[idx % 2][:, 0:tw]
                    if tap == 1:
                        dve.wait_ge(tap0, idx + 1)
                    else:
                        dve.wait_ge(conv_step, (CONVW - 2) * idx + tap - 1)
                    dve.scalar_tensor_tensor(out=out_, in0=cin[idx % 3][:, tap:tap + tw], scalar=cw[:, tap, j:j + 1],
                                             in1=out_, op0=ALU.mult, op1=ALU.add
                                             ).then_inc(conv_step if tap < CONVW - 1 else conv_done, 1)

                def follow(n):
                    for tap in range(CONVW - 1, 0, -1):
                        m = n - 1 - tap
                        if 0 <= m < len(steps):
                            for idx in pieces(parts[steps[m]]):
                                if idx < 3 * len(PIECES):
                                    tap_step(idx, tap)

                start(0)
                for a in A:
                    dve.memset(a[:, :, :], 0.0)
                dve.memset(S[:, :], 0.0).then_inc(init, 1)
                for g in range(NG):
                    if g:
                        start(g)
                    for i in range(LEVELS):
                        level(g, i)
                        if g == 0 and i == 0:
                            for t in (xq, xk, xv):
                                dve.memset(t[:, 0:PAD], 0.0)
                        merge(g, i)
                        extend(g, i)
                        if i == LEVELS - 1:
                            dve.wait_ge(pre_done, LEVELS * (g + 1))
                            dve.tensor_tensor(qf[g % 2][:, :], hq[:, g * GW:(g + 1) * GW], pre[:, :], ALU.mult).then_inc(qf_done, 1)
                            dve.tensor_copy(tot[g % 2][:, :], pre[:, P - 1:GW:P]).then_inc(tot_set, 1)
                        follow(steps.index(("gram", g, i)))
                        if g and i in (2, 4, 6):
                            update_state(g - 1, i // 2 - 1)
                            follow(steps.index(("rec", g - 1, i // 2 - 1)))
                    merge(g, LEVELS)
                    follow(steps.index(("gram", g, LEVELS)))
                    dve.wait_ge(tot_set, g + 1)
                    follow(steps.index(("t", g)))
                    if g:
                        gate(g - 1)
                        follow(steps.index(("ty", g - 1)))
                for i in range(GC):
                    update_state(NG - 1, i)
                    follow(steps.index(("rec", NG - 1, i)))
                follow(steps.index(("end",)))
                for n in range(len(steps), len(steps) + CONVW):
                    follow(n)
                gate(NG - 1)

            @block.tensor
            def _(pe):
                def project(key):
                    for n in parts[key]:
                        project_part(pe, n)

                def step_rec(g, i):
                    if i == 0:
                        freed(pe, plan, ("gram", g, LEVELS))
                        freed(pe, plan, ("tv", g))
                        freed(pe, plan, ("tk", g))
                        pe.wait_ge(qf_done, g + 1)
                        if g == 0:
                            pe.wait_ge(init, 1)
                        else:
                            freed(pe, plan, ("o", g - 1))
                    if g or i:
                        g1, i1 = divmod(GC * g + i - 1, GC)
                        freed(pe, plan, ("kv", g1, i1))
                    o, o_done = bank[RING - 1], mix_full[RING - 1]
                    if i in live(g):
                        pe.matmul(o[:, chunk(i)], A[g % 2][:, i, :], vtok[:, chunk(i)], start=True, stop=False)
                        last = pe.matmul(o[:, chunk(i)], qf[g % 2][:, chunk(i)], S[:, :], start=False, stop=True)
                    if i == GC - 1:
                        last.then_inc(o_done, 1)
                    ap, done = take(pe, plan, ("kv", g, i))
                    pe.matmul(ap[:, 0:P], ktok[:, chunk(i)], vtok[:, chunk(i)], start=True, stop=True).then_inc(done, 1)
                    project(("rec", g, i))

                def turn(name, g, src, which=range(GC)):
                    ap, done = take(pe, plan, (name, g))
                    for i in which:
                        last = pe.transpose(ap[:, chunk(i)], src(i), ident[:, :])
                    last.then_inc(done, 1)

                project(("lead",))
                for g in range(NG):
                    for m in range(LEVELS + 1):
                        ap, done = take(pe, plan, ("gram", g, m))
                        if m == 0:
                            pe.wait_ge(fk, g + 1)
                        else:
                            pe.wait_ge(x_even, LEVELS * g + m)
                            pe.wait_ge(x_odd, LEVELS * g + m)
                        for i in live(g):
                            if m == 0:
                                left, right = kk[:, chunk(i)], hq[:, g * GW + i * P:g * GW + (i + 1) * P]
                            else:
                                left = right = X[(LEVELS * g + m - 1) % 2][:, chunk(i)]
                            last = pe.matmul(ap[:, chunk(i)], left, right, start=True, stop=True)
                        last.then_inc(done, 1)
                        project(("gram", g, m))
                        if g and m in (2, 4, 6):
                            step_rec(g - 1, m // 2 - 1)
                    turn("tv", g, lambda i: hv[:, g * GW + i * P:g * GW + (i + 1) * P])
                    pe.wait_ge(kf_done, g + 1)
                    turn("tk", g, lambda i: kf[:, chunk(i)])
                    project(("t", g))
                    if g:
                        freed(pe, plan, ("o", g - 1))
                        turn("ty", g - 1, lambda i: on[:, chunk(i)], live(g - 1))
                        project(("ty", g - 1))
                for i in range(GC):
                    step_rec(NG - 1, i)
                for n in parts[("end",)][:-2]:
                    project_part(pe, n)
                freed(pe, plan, ("o", NG - 1))
                turn("ty", NG - 1, lambda i: on[:, chunk(i)])
                for n in parts[("end",)][-2:]:
                    project_part(pe, n)
        end_block()
        st.close()

    def phase_gd(h):
        more = not (isinstance(h, int) and h == HEADS - 1)
        st = ExitStack()
        Y, Lt = xk, xv
        M = sb("gd_m", [P, NT], F32, st)
        QK = sb("gd_qk", [P, NT], F32, st)
        kT = sb("gd_kT", [P, NT], F32, st)
        N = sb("gd_n", [P, NT], F32, st)
        kd = sb("gd_kd", [P, NT], F32, st)
        vtok = sb("gd_vtok", [P, NT], F32, st)
        kn = sb("gd_kn", [P, GW], F32, st)
        r = sb("gd_r", [P, P], F32, st)
        u = sb("gd_u", [P, P], F32, st)
        osb = [sb(f"gd_o{i}", [P, GW], F32, st) for i in range(2)]
        on = kn
        y_end = kd
        yb = [sb(f"gd_y{i}", [P, GW], F32, st) for i in range(2)]
        S = sb("gd_state", [P, P], F32, st)
        ss = sb("gd_ss", [P, 2, NC], F32, st)
        rr = sb("gd_rr", [P, 2, NC], F32, st)
        sq = [sb(f"gd_sq{i}", [P, GW], F32, st) for i in range(2)]
        cc = sb("gd_cc", [P, 7, NC], F32, st)
        SHORT = META.bit_length() - 1
        since = lambda i, g: 1 if g == 0 and i >= SHORT else 0
        names, parts, at = [], {}, 0

        def give(key, n):
            nonlocal at
            parts[key] = range(at, at + n)
            at += n

        A_ORDER = [("A1", 0), ("A1", 1), ("A2", 0), ("A3", 0), ("A1", 2), ("A2", 1), ("A3", 1), ("A2", 2), ("A3", 2)]
        for s, g in A_ORDER:
            names += [(n, g) for n in {"A1": ("tk", "tv"), "A2": ("tkn", "qs"), "A3": ("kk", "qk")}[s]]
            n = A_ORDER.index((s, g))
            give((s, g), (5, 5, 4, 5, 4, 4, 4, 3, 3)[n] if more else (0, 0, 0, 0, 1, 1, 1, 0, 0)[n])
        for i in range(1, LEVELS):
            names += [("Y", i, g) for g in range(NG)] + [("Z", i, g) for g in range(NG)]
            names += [("TM", i, g) for g in range(NG)] if i < LEVELS - 1 else []
            give(("B1", i), 0 if more or i == 1 else 1)
            give(("B2", i), 1)
        for c in range(NC):
            names += [("rec", c), ("U", c)]
            if c % GC == GC - 1 and c > GC:
                names.append(("ty", c // GC - 1))
            give(("C1", c), 2 if more else 3)
            give(("C2", c), 1 if more else 3)
            give(("C3", c), 2 if more else 4)
        names.append(("ty", NG - 1))
        give(("end",), (PARTS * 4 * len(PIECES) if more else 2 * TILES * OUT_K) - at)
        order = list(parts)
        plan = Bank(names)
        with nc.Block() as block:
            par, o_step = sem("gd_par"), sem("gd_o_step")
            q_squared, rq_done, diag_set, pair_set = (sem(n) for n in ("q_squared", "rq_done", "diag_set", "pair_set"))
            ssq, rstd_s, kd_done, nm = sem("gd_ssq"), sem("gd_rstd"), sem("gd_kd_done"), sem("gd_nm")
            init, kq_done, r_done, state = sem("gd_init"), sem("gd_kq"), sem("gd_rdone"), sem("gd_state_done")
            on_done, y_out = sem("gd_on"), [sem(f"gd_y_out{i}") for i in range(2)]
            wo_in, wo_high = [sem(f"wo_in{i}") for i in range(HOLD)], sem("wo_high")
            wo_low = [sem(f"wo_low{i}") for i in range(2)]
            x_held, sum_out = ([sem(f"{n}{i}") for i in range(HOLD)] for n in ("x_held", "sum_out"))

            def load_y(sp, t):
                if t >= 2:
                    sp.wait_ge(w_low, t - 1)
                sp.dma_start(raw[t % 2][:, 0:OUT_K, :], y_dram[0:OUT_K, :, (t + 1) * P:(t + 2) * P
                                                               ].rearrange("k p t -> p k t")).then_inc(raw_loaded[t % 2], 16)

            def y_split_high(act, t):
                act.wait_ge(raw_loaded[t % 2], 16 * (t // 2 + 1))
                if t >= 2:
                    act.wait_ge(piece_done, 2 * (t - 1))
                act.copy(wh[t % 2][:, 0:OUT_K, :], raw[t % 2][:, 0:OUT_K, :]).then_inc(w_high, 1)

            def y_split_low(pool, t):
                pool.wait_ge(w_high, t + 1)
                pool.tensor_tensor(wl[t % 2][:, 0:OUT_K, :], raw[t % 2][:, 0:OUT_K, :],
                                   wh[t % 2][:, 0:OUT_K, :].bitcast(F32), ALU.subtract).then_inc(w_low, 1)

            def wo_split_high(act, k):
                if not more and k < KT:
                    act.wait_ge(wo_in[k % HOLD], 16 * (k // HOLD + 1))
                    act.copy(woh[:, k, :], held[k % HOLD][:, 0:D]).then_inc(wo_high, 1)

            def wo_split_low(eng, k):
                if not more:
                    eng.wait_ge(wo_high, k + 1)
                    eng.tensor_tensor(wol[:, k, :], held[k % HOLD][:, 0:D], woh[:, k, :].bitcast(F32),
                                      ALU.subtract).then_inc(wo_low[k % 2], 1)

            def out_part(pe, n):
                idx, k = divmod(n, OUT_K)
                t, half = divmod(idx, 2)
                if k == 0:
                    if idx >= 2:
                        pe.wait_ge(piece_out, idx - 1)
                    pe.wait_ge(w_low, t + 1)
                if idx == 0:
                    pe.wait_ge(wo_low[k % 2], k // 2 + 1)
                cs = slice(half * 512, (half + 1) * 512)
                for i, (y, w) in enumerate(((wh, woh), (wh, wol), (wl, woh))):
                    last = pe.matmul(pbank[idx % 2][:, :], y[t % 2][:, k, :], w[:, k, cs],
                                     start=(k == 0 and i == 0), stop=(k == OUT_K - 1 and i == 2))
                if k == OUT_K - 1:
                    last.then_inc(piece_done, 1)

            def ends(rng):
                return [n // OUT_K for n in rng if n % OUT_K == OUT_K - 1] if not more else []

            def tiles_done(rng):
                return [idx // 2 for idx in ends(rng) if idx % 2]

            def take_out(dve, rng):
                for idx in ends(rng):
                    t, half = divmod(idx, 2)
                    dve.wait_ge(x_held[t % HOLD], 16 * (t // HOLD + 1))
                    dve.wait_ge(piece_done, idx + 1)
                    cs = slice(half * 512, (half + 1) * 512)
                    dve.tensor_tensor(held[t % HOLD][:, cs], pbank[idx % 2][:, :], held[t % HOLD][:, cs],
                                      ALU.add).then_inc(piece_out, 1)

            def take_hg(act, rng):
                if more:
                    for idx in pieces(rng):
                        take_piece(act, idx)
                else:
                    for t in tiles_done(rng):
                        if t + 2 < TILES:
                            y_split_high(act, t + 2)

            def take_low(pool, rng):
                if more:
                    for idx in pieces(rng):
                        if idx % len(PIECES) == len(PIECES) - 1 and idx < 3 * len(PIECES):
                            split_low(pool, idx // len(PIECES) + 2)
                else:
                    for t in tiles_done(rng):
                        if t + 2 < TILES:
                            y_split_low(pool, t + 2)

            def project(pe, rng):
                for n in rng:
                    (project_part if more else out_part)(pe, n)

            @block.sync
            def _(sp):
                if more:
                    for n in range(1, 5):
                        load_weights(sp, n - 1, tile_cols("hg", n, h + 1) if n < 4 else tile_cols("gd", 0, h + 1))
                    store_last(sp, "hg", h)
                    for g in range(NG - 1):
                        store_y(sp, plan, g, h + HEADS, yb, y_out)
                    sp.wait_ge(last_stored, 16)
                    for g in range(NG - 1):
                        sp.wait_ge(y_out[g], 16)
                    return
                store_last(sp, "hg", h)
                load_y(sp, 0)
                for k in range(KT):
                    if k >= HOLD:
                        sp.wait_ge(wo_low[k % 2], (k - HOLD) // 2 + 1)
                    sp.dma_start(held[k % HOLD][:, 0:D], w_out_v[:, k, :]).then_inc(wo_in[k % HOLD], 16)
                    if k == 0:
                        load_y(sp, 1)
                load_y(sp, 2)
                for t in range(HOLD):
                    sp.wait_ge(wo_low[t % 2], (t + HOLD) // 2 + 1)
                    sp.dma_start(held[t][:, 0:D], x[0, t * P:(t + 1) * P, :]).then_inc(x_held[t], 16)
                for t in tiles_done(range(at)):
                    if t + 3 == (NG - 1) * GC - 1:
                        sp.wait_ge(last_stored, 16)
                    if t + 3 < TILES:
                        load_y(sp, t + 3)
                    if t < TILES - HOLD:
                        sp.wait_ge(piece_out, 2 * t + 2)
                        sp.dma_start(sum_dram[t, :, :], held[t][:, 0:D]).then_inc(sum_out[t], 16)
                    if 1 <= t <= TILES - HOLD:
                        sp.wait_ge(sum_out[t - 1], 16)
                        sp.dma_start(held[t - 1][:, 0:D], x[0, (t - 1 + HOLD) * P:(t + HOLD) * P, :]
                                     ).then_inc(x_held[t - 1], 16)

            def scale_rows(pool, g):
                cs = slice(g * GC, (g + 1) * GC)
                pool.wait_ge(ssq, g + 1)
                rsqrt(pool, rr[:, 0, cs], ss[:, 0, cs], EPS, eps_added, g + 1).then_inc(rstd_s, 1)
                freed(pool, plan, ("tk", g))
                k3 = lambda t: t.rearrange("p (c t) -> p c t", c=GC)
                pool.tensor_tensor(k3(kd[:, g * GW:(g + 1) * GW]), k3(kn[:, :]),
                                   cc[:, 4, cs].unsqueeze(2).broadcast_to([P, GC, P]), ALU.mult).then_inc(kd_done, 1)

            @block.gpsimd
            def _(pool):
                pool.wait_ge(par, 1)
                for g in range(NG):
                    scale_rows(pool, g)
                    if more and g == 1:
                        split_low(pool, 1)
                    if not more and g == 0:
                        y_split_low(pool, 0)
                    if g == 1:
                        wo_split_low(pool, 1)
                for k in range(3, KT, 2):
                    wo_split_low(pool, k)
                if not more:
                    y_split_low(pool, 1)

                freed(pool, plan, ("qs", NG - 1))
                pool.tensor_tensor(rr[:, 1, :], ss[:, 1, :], neg_half[:, 0:1].broadcast_to([P, NC]), ALU.pow
                                   ).then_inc(rq_done, 1)

                def rstd_out(g):
                    pool.wait_ge(ssq, NG + g + 1)
                    rsqrt(pool, rr[:, 0, 0:GC], ss[:, 0, 0:GC], EPS, eps_added, NG + g + 1).then_inc(rstd_s, 1)

                for key in order:
                    if key[0] == "end":
                        rstd_out(NG - 1)
                    if key[0] == "C3" and key[1] % GC == 0 and key[1]:
                        rstd_out(key[1] // GC - 1)
                    take_low(pool, parts[key])

            @block.scalar
            def _(act):
                def measure(g):
                    src = full(act, plan, ("tk", g))
                    if g:
                        act.wait_ge(ssq, g)
                    for i in range(GC):
                        last = act.activation(sq[0][:, i * P:(i + 1) * P], src[:, i * P:(i + 1) * P], ACT.Square,
                                              accum_out=ss[:, 0, g * GC + i:g * GC + i + 1])
                    last.then_inc(ssq, 1)
                    if g:
                        full(act, plan, ("qs", g - 1))
                    act.activation(sq[1][:, :], xq[:, g * GW:(g + 1) * GW], ACT.Square,
                                   scale=float(P) ** 0.5).then_inc(q_squared, 1)
                    act.copy(vtok[:, g * GW:(g + 1) * GW], full(act, plan, ("tv", g))[:, 0:GW]
                             ).then_inc(bank_free(plan, ("tv", g)), 1)

                def turned(g):
                    act.copy(kT[:, g * GW:(g + 1) * GW], full(act, plan, ("tkn", g))[:, 0:GW]
                             ).then_inc(bank_free(plan, ("tkn", g)), 1)

                for s, g in A_ORDER:
                    if s == "A1":
                        measure(g)
                    elif s == "A2":
                        turned(g)
                    if more and (s, g) == ("A1", 1):
                        split_high(act, 1)
                    take_hg(act, parts[(s, g)])
                    n = A_ORDER.index((s, g))
                    if not more and n == 1:
                        y_split_high(act, 0)
                    if n >= 2:
                        wo_split_high(act, n - 2)
                for i in range(1, LEVELS):
                    for g in range(NG):
                        lo = since(i, g) * P
                        gs = slice(g * GW + lo, (g + 1) * GW)
                        act.copy(Y[:, gs], full(act, plan, ("Y", i, g))[:, lo:GW]).then_inc(bank_free(plan, ("Y", i, g)), 1)
                    if i == 1:
                        wo_split_high(act, KT - 1)
                    if not more and i == 2:
                        y_split_high(act, 1)
                    take_hg(act, parts[("B1", i)])
                    if i < LEVELS - 1:
                        for g in range(NG):
                            lo = since(i, g) * P
                            gs = slice(g * GW + lo, (g + 1) * GW)
                            act.copy(M[:, gs], full(act, plan, ("TM", i, g))[:, lo:GW]).then_inc(bank_free(plan, ("TM", i, g)), 1)
                    take_hg(act, parts[("B2", i)])
                def squares(g):
                    freed(act, plan, ("rec", GC * g + GC - 1))
                    act.wait_ge(ssq, NG + g)
                    for i in live(g):
                        last = act.activation(sq[0][:, i * P:(i + 1) * P], osb[g % 2][:, i * P:(i + 1) * P], ACT.Square,
                                              scale=float(P) ** -0.5, accum_out=ss[:, 0, i:i + 1])
                    last.then_inc(ssq, 1)

                def normed(g):
                    act.wait_ge(rstd_s, NG + g + 1)
                    if g:
                        full(act, plan, ("ty", g - 1))
                    for i in live(g):
                        last = act.activation(on[:, i * P:(i + 1) * P], osb[g % 2][:, i * P:(i + 1) * P], ACT.Copy,
                                              scale=rr[:, 0, i:i + 1])
                    last.then_inc(on_done, 1)

                for c in range(NC):
                    take_hg(act, parts[("C1", c)])
                    act.copy(u[:, :], full(act, plan, ("U", c))[:, 0:P]).then_inc(bank_free(plan, ("U", c)), 1)
                    take_hg(act, parts[("C2", c)])
                    if c % GC == 0 and c:
                        squares(c // GC - 1)
                    take_hg(act, parts[("C3", c)])
                    if c % GC == 1 and c > GC:
                        normed(c // GC - 1)
                squares(NG - 1)
                tail = pieces(parts[("end",)]) if more else []
                for idx in tail[:-1]:
                    take_piece(act, idx)
                normed(NG - 1)
                for idx in tail[-1:]:
                    take_piece(act, idx)
                if not more:
                    take_hg(act, parts[("end",)])

            @block.vector
            def _(dve):
                dve.tensor_copy(cc[:, :, :], cols[:, bass.ds(h, 1), :, :].rearrange("p h a c -> p (h a) c")).then_inc(par, 1)
                dve.memset(S[:, :], 0.0).then_inc(init, 1)
                dve.wait_ge(par, 1)
                step = [0]

                k3 = lambda t: t.rearrange("p (c t) -> p c t", c=GC)

                def norm(g):
                    dve.wait_ge(rstd_s, g + 1)
                    if g:
                        full(dve, plan, ("tkn", g - 1))
                        dve.wait_ge(kd_done, g)
                    dve.tensor_tensor(k3(kn[:, :]), k3(full(dve, plan, ("tk", g))[:, 0:GW]),
                                      rr[:, 0, g * GC:(g + 1) * GC].unsqueeze(2).broadcast_to([P, GC, P]),
                                      ALU.mult).then_inc(bank_free(plan, ("tk", g)), 1)

                def scores(g):
                    gs = slice(g * GW, (g + 1) * GW)
                    dec = DT[:, bass.ds(h, 1), gs].rearrange("p h t -> p (h t)")
                    dve.tensor_scalar(ss[:, 1, g * GC:(g + 1) * GC], full(dve, plan, ("qs", g))[:, 0:GC], EPS * P, None,
                                      ALU.add).then_inc(bank_free(plan, ("qs", g)), 1)
                    kk_ = full(dve, plan, ("kk", g))
                    if g:
                        dve.wait_ge(nm, g)
                    pair = osb[0]
                    for n, t in enumerate((Y[:, gs], pair[:, :])):
                        last = dve.tensor_tensor(k3(t), k3(kk_[:, 0:GW]),
                                                 cc[:, 5 + n, g * GC:(g + 1) * GC].unsqueeze(2).broadcast_to([P, GC, P]), ALU.mult)
                    last.then_inc(pair_set, 1)
                    dve.scalar_tensor_tensor(out=Lt[:, gs], in0=kk_[:, 0:GW], scalar=-1.0,
                                             in1=dec, op0=ALU.mult, op1=ALU.mult).then_inc(bank_free(plan, ("kk", g)), 1)
                    lo = first(g)
                    dve.tensor_tensor(QK[:, g * GW + lo:(g + 1) * GW], full(dve, plan, ("qk", g))[:, lo:GW], dec[:, lo:GW],
                                      ALU.mult).then_inc(bank_free(plan, ("qk", g)), 1)
                    dve.wait_ge(pair_set, g + 1)
                    dve.wait_ge(diag_set, 1)
                    for t, msk, src in ((N, mask_ts[:, 0, :], Y[:, gs]), (M, mask_st[:, 1, :], pair[:, :])):
                        last = dve.copy_predicated(k3(t[:, gs]), msk.unsqueeze(1).broadcast_to([P, GC, P]), k3(src))
                    last.then_inc(nm, 1)

                for g in range(NG):
                    gs = slice(g * GW, (g + 1) * GW)
                    for t in (N, M):
                        last = dve.tensor_tensor(k3(t[:, gs]), ident[:, :].unsqueeze(1).broadcast_to([P, GC, P]),
                                                 cc[:, 0, g * GC:(g + 1) * GC].unsqueeze(2).broadcast_to([P, GC, P]), ALU.mult)
                last.then_inc(diag_set, 1)
                norm(0)
                for g in range(NG):
                    if g + 1 < NG:
                        norm(g + 1)
                        wo_split_low(dve, 2 * g)
                    scores(g)
                wo_split_low(dve, 4)
                dve.wait_ge(nm, NG)
                for i in range(1, LEVELS):
                    for g in range(NG):
                        lo = since(i, g)
                        gs = slice(g * GW + lo * P, (g + 1) * GW)
                        part3 = lambda t: t.rearrange("p (c t) -> p c t", c=GC - lo)
                        src = part3(full(dve, plan, ("Z", i, g))[:, lo * P:GW])
                        dst, msk = (N, mask_ts[:, min(i, LEVELS - 2), :]) if i < LEVELS - 1 else (M, mask_st[:, LEVELS, :])
                        dve.copy_predicated(part3(dst[:, gs]), msk.unsqueeze(1).broadcast_to([P, GC - lo, P]), src
                                            ).then_inc(bank_free(plan, ("Z", i, g)), 1)
                    if i == 1:
                        wo_split_low(dve, 6)
                    take_out(dve, parts[("B1", i)])
                    take_out(dve, parts[("B2", i)])
                dve.wait_ge(rq_done, 1)
                dve.tensor_tensor(cc[:, 1, :], cc[:, 1, :], rr[:, 1, :], ALU.mult).then_inc(par, 1)
                dve.wait_ge(par, 2)

                def finish(g):
                    src = full(dve, plan, ("ty", g))
                    if more:
                        dst = y_last["gd"][:, :] if g == NG - 1 else yb[g][:, :]
                    else:
                        dst = y_end[:, g * GW:(g + 1) * GW]
                    lo = first(g)
                    dve.scalar_tensor_tensor(out=dst[:, lo:GW], in0=src[:, lo:GW],
                                             scalar=prm[:, PRM_GDN:PRM_GDN + 1], in1=gz[:, g * GW + lo:(g + 1) * GW],
                                             op0=ALU.mult, op1=ALU.mult).then_inc(bank_free(plan, ("ty", g)), 1)

                for c in range(NC):
                    g, i = divmod(c, GC)
                    dve.wait_ge(kq_done, c + 1)
                    rec = bank[plan.at[("rec", c)][0]]
                    dve.scalar_tensor_tensor(out=r[:, :], in0=rec[:, 0:P], scalar=cc[:, 2, c:c + 1],
                                             in1=vtok[:, c * P:(c + 1) * P], op0=ALU.mult, op1=ALU.add).then_inc(r_done, 1)
                    take_out(dve, parts[("C1", c)])
                    full(dve, plan, ("rec", c))
                    dve.scalar_tensor_tensor(out=S[:, :], in0=S[:, :], scalar=cc[:, 3, c:c + 1],
                                             in1=rec[:, 2 * P:3 * P], op0=ALU.mult, op1=ALU.add).then_inc(state, 1)
                    if c == 0:
                        dve.wait_ge(state, 1)
                        dve.engine_nop().then_inc(bank_free(plan, ("rec", c)), 1)
                        take_out(dve, parts[("C2", c)])
                        take_out(dve, parts[("C3", c)])
                        continue
                    dve.tensor_scalar(osb[g % 2][:, i * P:(i + 1) * P], rec[:, P:2 * P], cc[:, 1, c:c + 1], None,
                                      ALU.mult).then_inc(o_step, 1)
                    step[0] += 1
                    dve.wait_ge(o_step, step[0])
                    dve.scalar_tensor_tensor(out=osb[g % 2][:, i * P:(i + 1) * P], in0=rec[:, 3 * P:4 * P],
                                             scalar=rr[:, 1, c:c + 1], in1=osb[g % 2][:, i * P:(i + 1) * P],
                                             op0=ALU.mult, op1=ALU.add).then_inc(bank_free(plan, ("rec", c)), 1)
                    take_out(dve, parts[("C2", c)])
                    take_out(dve, parts[("C3", c)])
                    if c % GC == 0 and c > GC:
                        finish(c // GC - 2)
                finish(NG - 2)
                take_out(dve, parts[("end",)])
                finish(NG - 1)

            @block.tensor
            def _(pe):
                def three(name, g, left, right=None, wait=None, lo=0):
                    ap, done = take(pe, plan, name)
                    if wait:
                        freed(pe, plan, wait)
                    for i in range(lo, GC):
                        cs = slice(i * P, (i + 1) * P)
                        if right is None:
                            last = pe.transpose(ap[:, cs], left(i), ident[:, :])
                        else:
                            last = pe.matmul(ap[:, cs], left(i), right(i), start=True, stop=True)
                    last.then_inc(done, 1)

                full_c = lambda t, g: (lambda i: t[:, (g * GC + i) * P:(g * GC + i + 1) * P])
                part_c = lambda t: (lambda i: t[:, i * P:(i + 1) * P])
                for s, g in A_ORDER:
                    if s == "A1":
                        three(("tk", g), g, full_c(xk, g))
                        three(("tv", g), g, full_c(xv, g))
                    elif s == "A2":
                        three(("tkn", g), g, part_c(kn), wait=("tk", g))
                        ap, done = take(pe, plan, ("qs", g))
                        pe.wait_ge(q_squared, g + 1)
                        for i in range(GC):
                            last = pe.matmul(ap[:, i:i + 1], sq[1][:, i * P:(i + 1) * P], tri[:, P - 1:P],
                                             start=True, stop=True)
                        last.then_inc(done, 1)
                    else:
                        three(("kk", g), g, full_c(kT, g), full_c(kT, g), wait=("tkn", g))
                        three(("qk", g), g, full_c(kT, g), full_c(xq, g), lo=live(g)[0])
                    project(pe, parts[(s, g)])
                for i in range(1, LEVELS):
                    for g in range(NG):
                        if i == 1:
                            pe.wait_ge(nm, g + 1)
                        three(("Y", i, g), g, full_c(Lt, g), full_c(N, g), wait=("Z", i - 1, g) if i > 1 else ("kk", g), lo=since(i, g))
                    project(pe, parts[("B1", i)])
                    for g in range(NG):
                        if i > 1:
                            freed(pe, plan, ("TM", i - 1, g))
                        l, rt = (M, Y) if i < LEVELS - 1 else (Y, M)
                        three(("Z", i, g), g, full_c(l, g), full_c(rt, g), wait=("Y", i, g), lo=since(i, g))
                    project(pe, parts[("B2", i)])
                    if i < LEVELS - 1:
                        for g in range(NG):
                            three(("TM", i, g), g, full_c(N, g), wait=("Z", i, g), lo=since(i, g))
                for g in range(NG):
                    freed(pe, plan, ("Z", LEVELS - 1, g))
                pe.wait_ge(kd_done, NG)
                pe.wait_ge(init, 1)
                for c in range(NC):
                    cs = slice(c * P, (c + 1) * P)
                    rec, rec_done = take(pe, plan, ("rec", c))
                    if c:
                        pe.wait_ge(state, c)
                    last = pe.matmul(rec[:, 0:P], kT[:, cs], S[:, :], start=True, stop=True)
                    if c:
                        last = pe.matmul(rec[:, P:2 * P], xq[:, cs], S[:, :], start=True, stop=True)
                    last.then_inc(kq_done, 1)
                    project(pe, parts[("C1", c)])
                    ap, done = take(pe, plan, ("U", c))
                    pe.wait_ge(r_done, c + 1)
                    pe.matmul(ap[:, 0:P], M[:, cs], r[:, :], start=True, stop=True).then_inc(done, 1)
                    project(pe, parts[("C2", c)])
                    freed(pe, plan, ("U", c))
                    last = pe.matmul(rec[:, 2 * P:3 * P], kd[:, cs], u[:, :], start=True, stop=True)
                    if c:
                        last = pe.matmul(rec[:, 3 * P:4 * P], QK[:, cs], u[:, :], start=True, stop=True)
                    last.then_inc(rec_done, 1)
                    project(pe, parts[("C3", c)])
                    if c % GC == GC - 1 and c > GC:
                        g = c // GC - 1
                        pe.wait_ge(on_done, g + 1)
                        three(("ty", g), g, part_c(on), lo=live(g)[0])
                after = 2 if more else 0
                split = len(parts[("end",)]) - after
                project(pe, parts[("end",)][:split])
                pe.wait_ge(on_done, NG)
                three(("ty", NG - 1), NG - 1, part_c(on))
                project(pe, parts[("end",)][split:])
        end_block()
        if not more:
            return st, y_end, (kT, xq, QK, vtok), (Lt, M), N, Y
        st.close()

    with nc.Fori(0, HEADS - 1) as h:
        phase_hg(h)
        phase_gd(h)
    phase_hg(HEADS - 1)
    st, y_end, spare, more_spare, fw, sqo = phase_gd(HEADS - 1)

    mso = sb("ms_o", [P, TILES], F32, st)
    rso = sb("rs_o", [P, TILES], F32, st)
    yh, yl = (t[0][:, :, :].rearrange("p k c -> p (k c)") for t in (wh, wl))
    res = [*(t[:, :, :].rearrange("p k c -> p (k c)") for t in raw), *(t[:, 0:D] for t in more_spare)]
    ON_POOL = (1, 3)
    hs = [t[:, 0:D] for t in (*spare, *held)]
    LAG = 2
    ORDER = [*range(TILES - HOLD, TILES), *range(TILES - HOLD)]
    with nc.Block() as block:
        fw_in, sum_in = sem("fw_in"), [sem(f"sum_in{i}") for i in range(HOLD)]
        y_high, y_low, summed, o_ss, o_rs, o_scaled = (
            sem(n) for n in ("y_high", "y_low", "summed", "o_ss", "o_rs", "o_scaled"))
        o_res_dve, o_res_pool = sem("o_res_dve"), sem("o_res_pool")
        on_dve = [n for n in range(TILES) if n not in ON_POOL]
        o_done, stored = sem("o_done"), [sem(f"stored{i}") for i in range(len(res))]

        @block.sync
        def _(sp):
            sp.dma_start(fw[:, 0:D], final_norm_w.rearrange("(a c) -> a c", a=1).broadcast_to([P, D])).then_inc(fw_in, 16)
            for t in range(TILES - HOLD):
                sp.dma_start(hs[t], sum_dram[t, :, :]).then_inc(sum_in[t], 16)
            for n, t in enumerate(ORDER):
                if n in ON_POOL:
                    sp.wait_ge(o_res_pool, ON_POOL.index(n) + 1)
                else:
                    sp.wait_ge(o_res_dve, on_dve.index(n) + 1)
                sp.dma_start(out[0, t * P:(t + 1) * P, :], res[n % len(res)]).then_inc(stored[n % len(res)], 16)
            for i in range(len(res)):
                sp.wait_ge(stored[i], 16 * TILES // len(res))

        def y_part(i):
            t0 = ORDER[i * HOLD] * P
            return slice(t0, t0 + HOLD * P), slice(P + t0, P + t0 + HOLD * P)

        @block.scalar
        def _(act):
            for i in range(2):
                dst, src = y_part(i)
                act.copy(yh[:, dst], y_end[:, src]).then_inc(y_high, 1)
            for n, t in enumerate(ORDER):
                act.wait_ge(summed, 2 * (n + 1))
                if n:
                    act.wait_ge(o_ss, n)
                act.activation(sqo[:, 0:D], hs[t], ACT.Square, scale=float(D) ** -0.5,
                               accum_out=mso[:, t:t + 1]).then_inc(o_ss, 1)
                m = n - 1
                if m in ON_POOL:
                    act.wait_ge(o_rs, m + 1)
                    if m >= len(res):
                        act.wait_ge(stored[m % len(res)], 16 * (m // len(res)))
                    act.activation(res[m % len(res)], hs[ORDER[m]], ACT.Copy, scale=rso[:, ORDER[m]:ORDER[m] + 1]
                                   ).then_inc(o_scaled, 1)

        @block.gpsimd
        def _(pool):
            def weigh(n):
                pool.wait_ge(o_scaled, ON_POOL.index(n) + 1)
                pool.wait_ge(fw_in, 16)
                pool.tensor_tensor(res[n % len(res)], res[n % len(res)], fw[:, 0:D], ALU.mult).then_inc(o_res_pool, 1)

            for n, t in enumerate(ORDER):
                pool.wait_ge(o_ss, n + 1)
                rsqrt(pool, rso[:, t:t + 1], mso[:, t:t + 1], EPS, eps_added, n + 1).then_inc(o_rs, 1)
                if n - 1 in ON_POOL:
                    weigh(n - 1)

        @block.tensor
        def _(pe):
            for n, t in enumerate(ORDER):
                if n % HOLD == 0:
                    pe.wait_ge(y_low, n // HOLD + 1)
                for half in range(2):
                    m = 2 * n + half
                    if m >= 4:
                        pe.wait_ge(summed, m - 3)
                    for i, (y, w) in enumerate(((yh, woh), (yh, wol), (yl, woh))):
                        last = pe.matmul(bank[m % 4][:, :], y[:, t * P:(t + 1) * P],
                                         w[:, KT - 1, half * 512:(half + 1) * 512], start=(i == 0), stop=(i == 2))
                    last.then_inc(o_done, 1)

        @block.vector
        def _(dve):
            def low_half(i):
                dst, src = y_part(i)
                dve.wait_ge(y_high, i + 1)
                dve.tensor_tensor(yl[:, dst], y_end[:, src], yh[:, dst].bitcast(F32), ALU.subtract).then_inc(y_low, 1)

            low_half(0)

            def result_tile(n):
                if n in ON_POOL:
                    return
                t = ORDER[n]
                dve.wait_ge(o_rs, n + 1)
                if n >= len(res):
                    dve.wait_ge(stored[n % len(res)], 16 * (n // len(res)))
                dve.scalar_tensor_tensor(out=res[n % len(res)], in0=hs[t], scalar=rso[:, t:t + 1],
                                         in1=fw[:, 0:D], op0=ALU.mult, op1=ALU.mult).then_inc(o_res_dve, 1)

            for n, t in enumerate(ORDER):
                if t < TILES - HOLD:
                    dve.wait_ge(sum_in[t], 16)
                for half in range(2):
                    m = 2 * n + half
                    cs = slice(half * 512, (half + 1) * 512)
                    dve.wait_ge(o_done, m + 1)
                    dve.tensor_tensor(hs[t][:, cs], bank[m % 4][:, :], hs[t][:, cs], ALU.add).then_inc(summed, 1)
                if n == 0:
                    low_half(1)
                    dve.wait_ge(fw_in, 16)
                if n >= LAG:
                    result_tile(n - LAG)
            for n in range(TILES - LAG, TILES):
                result_tile(n)
    end_block()
    st.close()
    ctx.close()


_INS = ["x", "meta_tokens", "norm_w", "w_in", "conv_w", "hg_lb_logits", "hg_norm_w", "gdn_A_log",
        "gdn_dt_bias", "gdn_norm_w", "w_out", "final_norm_w"]


def kernel(**inputs):
    import numpy as _np
    import concourse.bacc as _bacc
    from concourse import mybir as _mybir
    from concourse.bass_utils import run_bass_kernel_spmd as _run

    nc = _bacc.Bacc("TRN2", target_bir_lowering=False, num_devices=1)
    arrays, args = {}, []
    for name in _INS:
        a = _np.ascontiguousarray(inputs[name])
        arrays[f"in_{name}"] = a
        args.append(nc.dram_tensor(f"in_{name}", a.shape, _mybir.dt.from_np(a.dtype), kind="ExternalInput").ap())
    args.append(nc.dram_tensor("out_y", (1, SEQ, D), F32, kind="ExternalOutput").ap())
    hybrid_layer(nc, *args)
    r = _run(nc, [arrays], core_ids=[0])
    return r.results[0]["out_y"]
```
